# Optimizing a Trainium2 kernel written in Bass

```python
import math
import jax, jax.numpy as jnp
from jax import lax
import numpy as np

D_MODEL = 1024
BATCH = 1
SEQ = 256
DEPTH = 2

CHUNK = 64
Q_BLOCK = 128
CONV_DIM = D_MODEL // 2
CONV_WIDTH = 3
HG_HEADS = 4
HG_DK = 128
HG_DV = (D_MODEL // 2) // HG_HEADS
HG_FDIM = HG_HEADS * HG_DK
HG_WIDTH = HG_HEADS * HG_DV
SB_HEADS = 16
SB_HEAD_DIM = D_MODEL // SB_HEADS
SB_WIDTH = SB_HEADS * SB_HEAD_DIM
D_FF = 4 * D_MODEL
N_EVEN = (DEPTH + 1) // 2
N_ODD = DEPTH // 2
AB_IN = 3 * CONV_DIM + 2 * HG_FDIM + 2 * HG_WIDTH
AB_MIX = CONV_DIM + HG_WIDTH
AB_SPLITS = [CONV_DIM, 2 * CONV_DIM, 3 * CONV_DIM,
             3 * CONV_DIM + HG_FDIM, 3 * CONV_DIM + 2 * HG_FDIM,
             3 * CONV_DIM + 2 * HG_FDIM + HG_WIDTH]
EPS = 1e-6


def rms_norm(x, g):
    xf = x.astype(jnp.float32)
    y = xf * lax.rsqrt(jnp.mean(xf * xf, axis=-1, keepdims=True) + EPS)
    return (y * g.astype(jnp.float32)).astype(x.dtype)

def causal_depthwise_conv(u, w):
    width, ch = w.shape
    return lax.conv_general_dilated(
        u, w[:, None, :], window_strides=(1,), padding=[(width - 1, 0)],
        dimension_numbers=('NWC', 'WIO', 'NWC'), feature_group_count=ch)

def hgrn2_chunkwise(q, k, v, log_f):
    B, S, H, Dk = q.shape
    Dv = v.shape[-1]
    n = S // CHUNK

    def to_chunks(t):
        return t.reshape(B, n, CHUNK, H, t.shape[-1]).transpose(1, 0, 3, 2, 4)

    qc, kc, vc, gc = to_chunks(q), to_chunks(k), to_chunks(v), to_chunks(log_f)
    bc = jnp.cumsum(gc, axis=3)
    causal = jnp.tril(jnp.ones((CHUNK, CHUNK), dtype=bool))

    def step(state, inp):
        q_, k_, v_, b_ = inp
        inter = jnp.einsum('bhtk,bhkv->bhtv', q_ * jnp.exp(b_), state)
        diff = jnp.where(causal[None, None, :, :, None],
                         b_[:, :, :, None, :] - b_[:, :, None, :, :], -jnp.inf)
        decay = jnp.exp(diff)
        scores = jnp.einsum('bhtk,bhsk,bhtsk->bhts', q_, k_, decay)
        intra = jnp.einsum('bhts,bhsv->bhtv', scores, v_)
        b_last = b_[:, :, -1:, :]
        new_state = (jnp.exp(b_last[:, :, 0, :])[..., None] * state
                     + jnp.einsum('bhsk,bhsv->bhkv', k_ * jnp.exp(b_last - b_), v_))
        return new_state, inter + intra

    init = jnp.zeros((B, H, Dk, Dv), jnp.float32)
    _, out = lax.scan(step, init, (qc, kc, vc, bc))
    return out.transpose(1, 0, 3, 2, 4).reshape(B, S, H, Dv)

def stick_breaking_attention(q, k, v):
    S = q.shape[2]
    scale = SB_HEAD_DIM ** -0.5
    outs = []
    for blk in range(S // Q_BLOCK):
        q0 = blk * Q_BLOCK
        end = q0 + Q_BLOCK
        qb = q[:, :, q0:end]
        kb = k[:, :, :end]
        vb = v[:, :, :end]
        z = jnp.einsum('bhqd,bhkd->bhqk', qb, kb) * scale
        qpos = q0 + jnp.arange(Q_BLOCK)
        kpos = jnp.arange(end)
        mask = (kpos[None, :] < qpos[:, None])[None, None]
        log_beta = jax.nn.log_sigmoid(z)
        log_one_minus = jnp.where(mask, log_beta - z, 0.0)
        later = lax.cumsum(log_one_minus, axis=3, reverse=True) - log_one_minus
        w = jnp.where(mask, jnp.exp(log_beta + later), 0.0)
        outs.append(jnp.einsum('bhqk,bhkd->bhqd', w, vb))
    return jnp.concatenate(outs, axis=2)

def mixer_conv_hgrn(h, w_in, conv_w, hg_norm, lower_bound, w_out):
    B, S, _ = h.shape
    u = h @ w_in
    a_b, a_c, a_h, hq, hf, hi, hg = jnp.split(u, AB_SPLITS, axis=-1)
    y_a = a_b * causal_depthwise_conv(a_c * a_h, conv_w)
    f = lower_bound + (1.0 - lower_bound) * jax.nn.sigmoid(hf.astype(jnp.float32))
    log_f = jnp.log(f)
    k_in = 1.0 - f
    heads_k = lambda t: t.reshape(B, S, HG_HEADS, HG_DK)
    o = hgrn2_chunkwise(heads_k(hq.astype(jnp.float32)), heads_k(k_in), 
                        hi.astype(jnp.float32).reshape(B, S, HG_HEADS, HG_DV), heads_k(log_f))
    o = rms_norm(o, hg_norm.reshape(HG_HEADS, HG_DV))
    y_b = (o.reshape(B, S, HG_WIDTH) * jax.nn.silu(hg.astype(jnp.float32))).astype(h.dtype)
    return jnp.concatenate([y_a, y_b], axis=-1) @ w_out

def mixer_stick_breaking(h, w_qkv, q_norm, k_norm, w_out):
    B, S, _ = h.shape
    qkv = (h @ w_qkv).reshape(B, S, 3, SB_HEADS, SB_HEAD_DIM)
    q = rms_norm(qkv[:, :, 0], q_norm)
    k = rms_norm(qkv[:, :, 1], k_norm)
    v = qkv[:, :, 2]
    to_bhsd = lambda t: t.astype(jnp.float32).transpose(0, 2, 1, 3)
    o = stick_breaking_attention(to_bhsd(q), to_bhsd(k), to_bhsd(v))
    o = o.transpose(0, 2, 1, 3).reshape(B, S, SB_WIDTH).astype(h.dtype)
    return o @ w_out

def first_inputs(seed: int = 0) -> dict:
    key = jax.random.key(seed)
    ks = jax.random.split(key, 20)
    nrm = lambda k, shape, s: jax.random.normal(k, shape, jnp.float32) * s
    gain = lambda k, shape: 1.0 + 0.02 * jax.random.normal(k, shape, jnp.float32)
    return {
        "x": nrm(ks[0], (BATCH, SEQ, D_MODEL), 1.0),
        "c": nrm(ks[1], (BATCH, D_MODEL), 1.0),
        "ada_w": nrm(ks[2], (DEPTH, D_MODEL, 6 * D_MODEL), 0.5 * D_MODEL ** -0.5),
        "ada_b": nrm(ks[3], (DEPTH, 6 * D_MODEL), 0.02),
        "norm_mix": gain(ks[4], (DEPTH, D_MODEL)),
        "norm_mlp": gain(ks[5], (DEPTH, D_MODEL)),
        "w_in_ab": nrm(ks[6], (N_EVEN, D_MODEL, AB_IN), D_MODEL ** -0.5),
        "conv_w": nrm(ks[7], (N_EVEN, CONV_WIDTH, CONV_DIM), CONV_WIDTH ** -0.5),
        "hg_norm": gain(ks[8], (N_EVEN, HG_WIDTH)),
        "lb_logits": nrm(ks[9], (DEPTH + 1, HG_FDIM), 0.1),
        "w_out_ab": nrm(ks[10], (N_EVEN, AB_MIX, D_MODEL), AB_MIX ** -0.5),
        "w_qkv": nrm(ks[11], (N_ODD, D_MODEL, 3 * SB_WIDTH), D_MODEL ** -0.5),
        "q_norm": gain(ks[12], (N_ODD, SB_HEAD_DIM)),
        "k_norm": gain(ks[13], (N_ODD, SB_HEAD_DIM)),
        "w_out_c": nrm(ks[14], (N_ODD, SB_WIDTH, D_MODEL), SB_WIDTH ** -0.5),
        "mlp_w1": nrm(ks[15], (DEPTH, D_MODEL, D_FF), D_MODEL ** -0.5),
        "mlp_w2": nrm(ks[16], (DEPTH, D_FF, D_MODEL), D_FF ** -0.5),
    }

def first_block(x, c, ada_w, ada_b, norm_mix, norm_mlp, w_in_ab, conv_w, hg_norm,
              lb_logits, w_out_ab, w_qkv, q_norm, k_norm, w_out_c, mlp_w1, mlp_w2):
    c_act = jax.nn.silu(c)
    lower_bounds = jnp.cumsum(jax.nn.softmax(lb_logits.astype(jnp.float32), axis=0), axis=0)
    for layer in range(DEPTH):
        mod = c_act @ ada_w[layer] + ada_b[layer]
        shift1, scale1, gate1, shift2, scale2, gate2 = jnp.split(mod[:, None, :], 6, axis=-1)
        h = rms_norm(x, norm_mix[layer]) * (1.0 + scale1) + shift1
        j = layer // 2
        if layer % 2 == 0:
            y = mixer_conv_hgrn(h, w_in_ab[j], conv_w[j], hg_norm[j],
                                lower_bounds[layer], w_out_ab[j])
        else:
            y = mixer_stick_breaking(h, w_qkv[j], q_norm[j], k_norm[j], w_out_c[j])
        x = x + gate1 * y
        h = rms_norm(x, norm_mlp[layer]) * (1.0 + scale2) + shift2
        x = x + gate2 * (jnp.square(jax.nn.relu(h @ mlp_w1[layer])) @ mlp_w2[layer])
    return x


SSM_GROUP = 16
N_GROUPS = D_MODEL // SSM_GROUP
SSM_STATE = 64
N_HEADS = 16
HEAD_DIM = D_MODEL // N_HEADS
ATTN_DIM = N_HEADS * HEAD_DIM
D_FF_2 = 4 * D_MODEL
N_A_LAYERS = DEPTH // 2
N_B_LAYERS = DEPTH - N_A_LAYERS
RMS_EPS = 1e-6
DT_MIN = 1e-3
DT_MAX = 1e-1


def rmsnorm(x, g):
    xf = x.astype(jnp.float32)
    y = xf * lax.rsqrt(jnp.mean(xf * xf, axis=-1, keepdims=True) + RMS_EPS)
    return (y * g.astype(jnp.float32)).astype(x.dtype)

def sqrelu_mlp(h, w1, w2):
    a = jnp.square(jax.nn.relu(h @ w1))
    return a @ w2

def _ssm_binop(e1, e2):
    a1, b1 = e1
    a2, b2 = e2
    return a2 * a1, a2 * b1 + b2

def s5_mixer(u, log_dt, a_re, a_im, b_re, b_im, c_re, c_im, d_skip, w_glu):
    f32 = jnp.float32
    bsz, length, _ = u.shape
    uf = u.astype(f32).reshape(bsz, length, N_GROUPS, SSM_GROUP)
    lam = lax.complex(a_re.astype(f32), a_im.astype(f32))
    dt = jnp.exp(log_dt.astype(f32))[:, None]
    lam_bar = jnp.exp(lam * dt)
    b = lax.complex(b_re.astype(f32), b_im.astype(f32))
    b_bar = ((lam_bar - 1.0) / lam)[..., None] * b
    bu = jnp.einsum('blgc,gpc->blgp', uf.astype(jnp.complex64), b_bar)
    a_elems = jnp.broadcast_to(lam_bar, bu.shape)
    _, states = lax.associative_scan(_ssm_binop, (a_elems, bu), axis=1)
    c = lax.complex(c_re.astype(f32), c_im.astype(f32))
    y = jnp.real(jnp.einsum('blgp,gcp->blgc', states, c))
    y = y + d_skip.astype(f32).reshape(N_GROUPS, SSM_GROUP) * uf
    z = jax.nn.gelu(y.reshape(bsz, length, D_MODEL)).astype(u.dtype)
    zw = z @ w_glu
    val, gate = zw[..., :D_MODEL], zw[..., D_MODEL:]
    return val * jax.nn.sigmoid(gate)

def shared_kv(h, kv_norm, w_kvf, b_f):
    bsz, length, _ = h.shape
    kvf = rmsnorm(h, kv_norm) @ w_kvf
    k = kvf[..., :ATTN_DIM].reshape(bsz, length, N_HEADS, HEAD_DIM).transpose(0, 2, 1, 3)
    v = kvf[..., ATTN_DIM:2 * ATTN_DIM].reshape(bsz, length, N_HEADS, HEAD_DIM).transpose(0, 2, 1, 3)
    f_logit = kvf[..., 2 * ATTN_DIM:].astype(jnp.float32) + b_f.astype(jnp.float32)
    log_f = jax.nn.log_sigmoid(f_logit)
    cum_log_f = jnp.cumsum(log_f, axis=1).transpose(0, 2, 1)
    return k, v, cum_log_f

def fox_attention(hn, wq, wo, k, v, cum_log_f):
    bsz, length, _ = hn.shape
    nb = length // Q_BLOCK
    q = (hn @ wq) * (HEAD_DIM ** -0.5)
    q_blocks = q.reshape(bsz, nb, Q_BLOCK, N_HEADS, HEAD_DIM).transpose(1, 0, 3, 2, 4)
    f_blocks = cum_log_f.reshape(bsz, N_HEADS, nb, Q_BLOCK).transpose(2, 0, 1, 3)
    pos_q = jnp.arange(length, dtype=jnp.int32).reshape(nb, Q_BLOCK)
    pos_k = jnp.arange(length, dtype=jnp.int32)

    def one_block(args):
        qb, fq, pq = args
        s = jnp.einsum('bhqd,bhkd->bhqk', qb, k).astype(jnp.float32)
        s = s + fq[..., None] - cum_log_f[:, :, None, :]
        mask = pq[:, None] >= pos_k[None, :]
        s = jnp.where(mask[None, None], s, -jnp.inf)
        p = jax.nn.softmax(s, axis=-1)
        return jnp.einsum('bhqk,bhkd->bhqd', p.astype(v.dtype), v)

    o = lax.map(one_block, (q_blocks, f_blocks, pos_q))
    o = o.transpose(1, 0, 3, 2, 4).reshape(bsz, length, ATTN_DIM)
    return o @ wo

def second_inputs(seed: int = 0) -> dict:
    key = jax.random.key(seed)
    ks = jax.random.split(key, 20)
    f32 = jnp.float32

    def nrm(k, shape, scale):
        return scale * jax.random.normal(k, shape, f32)

    x = nrm(ks[0], (BATCH, SEQ, D_MODEL), 1.0)
    mix_norm = 1.0 + nrm(ks[1], (DEPTH, D_MODEL), 0.05)
    mlp_norm = 1.0 + nrm(ks[2], (DEPTH, D_MODEL), 0.05)
    mlp_w1 = nrm(ks[3], (DEPTH, D_MODEL, D_FF_2), D_MODEL ** -0.5)
    mlp_w2 = nrm(ks[4], (DEPTH, D_FF_2, D_MODEL), 0.5 * D_FF_2 ** -0.5)
    ssm_log_dt = jax.random.uniform(ks[5], (N_A_LAYERS, N_GROUPS), f32,
                                    math.log(DT_MIN), math.log(DT_MAX))
    ssm_a_re = -0.5 + nrm(ks[6], (N_A_LAYERS, N_GROUPS, SSM_STATE), 0.01)
    ssm_a_im = math.pi * jnp.arange(SSM_STATE, dtype=f32) + nrm(ks[7], (N_A_LAYERS, N_GROUPS, SSM_STATE), 0.01)
    ssm_b_re = nrm(ks[8], (N_A_LAYERS, N_GROUPS, SSM_STATE, SSM_GROUP), (2 * SSM_GROUP) ** -0.5)
    ssm_b_im = nrm(ks[9], (N_A_LAYERS, N_GROUPS, SSM_STATE, SSM_GROUP), (2 * SSM_GROUP) ** -0.5)
    ssm_c_re = nrm(ks[10], (N_A_LAYERS, N_GROUPS, SSM_GROUP, SSM_STATE), (2 * SSM_STATE) ** -0.5)
    ssm_c_im = nrm(ks[11], (N_A_LAYERS, N_GROUPS, SSM_GROUP, SSM_STATE), (2 * SSM_STATE) ** -0.5)
    ssm_d = nrm(ks[12], (N_A_LAYERS, D_MODEL), 1.0)
    ssm_w_glu = nrm(ks[13], (N_A_LAYERS, D_MODEL, 2 * D_MODEL), D_MODEL ** -0.5)
    kv_norm = 1.0 + nrm(ks[14], (D_MODEL,), 0.05)
    w_kvf = nrm(ks[15], (D_MODEL, 2 * ATTN_DIM + N_HEADS), D_MODEL ** -0.5)
    b_f = jax.random.uniform(ks[16], (N_HEADS,), f32, 0.5, 3.0)
    attn_wq = nrm(ks[17], (N_B_LAYERS, D_MODEL, ATTN_DIM), D_MODEL ** -0.5)
    attn_wo = nrm(ks[18], (N_B_LAYERS, ATTN_DIM, D_MODEL), ATTN_DIM ** -0.5)
    final_norm = 1.0 + nrm(ks[19], (D_MODEL,), 0.05)
    return {"x": x, "mix_norm": mix_norm, "mlp_norm": mlp_norm, "mlp_w1": mlp_w1, "mlp_w2": mlp_w2,
            "ssm_log_dt": ssm_log_dt, "ssm_a_re": ssm_a_re, "ssm_a_im": ssm_a_im,
            "ssm_b_re": ssm_b_re, "ssm_b_im": ssm_b_im, "ssm_c_re": ssm_c_re, "ssm_c_im": ssm_c_im,
            "ssm_d": ssm_d, "ssm_w_glu": ssm_w_glu, "kv_norm": kv_norm, "w_kvf": w_kvf, "b_f": b_f,
            "attn_wq": attn_wq, "attn_wo": attn_wo, "final_norm": final_norm}

def second_block(x, mix_norm, mlp_norm, mlp_w1, mlp_w2, ssm_log_dt, ssm_a_re, ssm_a_im,
              ssm_b_re, ssm_b_im, ssm_c_re, ssm_c_im, ssm_d, ssm_w_glu, kv_norm, w_kvf, b_f,
              attn_wq, attn_wo, final_norm):
    h = x
    k = v = cum_log_f = None
    for i in range(DEPTH):
        hn = rmsnorm(h, mix_norm[i])
        if i < N_A_LAYERS:
            h = h + s5_mixer(hn, ssm_log_dt[i], ssm_a_re[i], ssm_a_im[i], ssm_b_re[i], ssm_b_im[i],
                             ssm_c_re[i], ssm_c_im[i], ssm_d[i], ssm_w_glu[i])
        else:
            j = i - N_A_LAYERS
            h = h + fox_attention(hn, attn_wq[j], attn_wo[j], k, v, cum_log_f)
        h = h + sqrelu_mlp(rmsnorm(h, mlp_norm[i]), mlp_w1[i], mlp_w2[i])
        if i == N_A_LAYERS - 1:
            k, v, cum_log_f = shared_kv(h, kv_norm, w_kvf, b_f)
    return rmsnorm(h, final_norm)


def setup_inputs(seed=0):
    out = dict(first_inputs(seed))
    for name, value in second_inputs(seed + 1).items():
        if name != "x":
            out[name + "_2"] = value
    return out


def reference(
    x, c, ada_w, ada_b, norm_mix, norm_mlp, w_in_ab, conv_w, hg_norm, lb_logits, w_out_ab,
    w_qkv, q_norm, k_norm, w_out_c, mlp_w1, mlp_w2, mix_norm_2, mlp_norm_2, mlp_w1_2, mlp_w2_2,
    ssm_log_dt_2, ssm_a_re_2, ssm_a_im_2, ssm_b_re_2, ssm_b_im_2, ssm_c_re_2, ssm_c_im_2,
    ssm_d_2, ssm_w_glu_2, kv_norm_2, w_kvf_2, b_f_2, attn_wq_2, attn_wo_2, final_norm_2,
):
    x = first_block(
        x, c, ada_w, ada_b, norm_mix, norm_mlp, w_in_ab, conv_w, hg_norm, lb_logits, w_out_ab,
        w_qkv, q_norm, k_norm, w_out_c, mlp_w1, mlp_w2,
    )
    return second_block(
        x, mix_norm_2, mlp_norm_2, mlp_w1_2, mlp_w2_2, ssm_log_dt_2, ssm_a_re_2, ssm_a_im_2,
        ssm_b_re_2, ssm_b_im_2, ssm_c_re_2, ssm_c_im_2, ssm_d_2, ssm_w_glu_2, kv_norm_2,
        w_kvf_2, b_f_2, attn_wq_2, attn_wo_2, final_norm_2,
    )


_drawn_inputs = setup_inputs


def setup_inputs(seed=0):
    import zlib

    import numpy as np

    out = dict(_drawn_inputs(seed))
    spreads = {}
    factors = {'norm_mix': 4.422,
     'norm_mlp': 20.273,
     'hg_norm': 64.0,
     'lb_logits': 6.332,
     'q_norm': 200.0,
     'k_norm': 200.0,
     'mix_norm_2': 60.011,
     'ssm_log_dt_2': 27.096,
     'ssm_a_re_2': 64.0,
     'ssm_a_im_2': 24.896,
     'ssm_b_re_2': 36.504,
     'ssm_b_im_2': 34.632,
     'ssm_c_re_2': 35.336,
     'ssm_c_im_2': 35.848,
     'kv_norm_2': 57.532,
     'mlp_norm_2': 31.239,
     'w_qkv': 5.119,
     'w_out_c': 5.06,
     'b_f_2': 7.678}
    for name, (base, spread) in spreads.items():
        noise = np.random.default_rng([zlib.crc32(name.encode()), seed]).standard_normal(out[name].shape)
        drawn = base * np.exp(spread * noise) if base else spread * noise
        out[name] = __import__('jax').numpy.asarray(drawn.astype(out[name].dtype))
    for name, factor in factors.items():
        out[name] = (out[name] * factor).astype(out[name].dtype)
    return out
```

```python
from contextlib import ExitStack

import numpy as np
import concourse.bass as bass
from concourse import mybir

F32 = mybir.dt.float32
F32R = mybir.dt.float32r
I32 = mybir.dt.int32
ALU = mybir.AluOpType
ACT = mybir.ActivationFunctionType
AX = mybir.AxisListType

P = 128
D = 1024
S = 256
KT = D // P
FF = 4 * D
CW = 2 * P
NB = S // P
EPS = 1e-6
UNITS = 6 * D // P
MLP_CHUNKS = FF // CW
HG_HEADS = 4
HEADS = 16
HD = D // HEADS
ARENA = 24576
GROUPS = 64
GC = 16
NSTATE = 64
TAPS = 8
NJ = S // TAPS
TWO_PI = 2.0 * np.pi
PI_A = 6.28125
PI_B = 0.001935303211212158
PI_C = TWO_PI - PI_A - PI_B
ROUND = 12582912.0


PARAM_COLS = [("c", KT), ("ada_b", 2 * UNITS), ("norm_mix", 2 * KT), ("norm_mlp", 2 * KT), ("lb", 12),
              ("hg_norm", 4), ("conv_w", 12), ("q_norm", 1), ("k_norm", 1), ("mix_norm_2", 2 * KT),
              ("mlp_norm_2", 2 * KT), ("kv_norm_2", KT), ("final_norm_2", KT), ("ssm_d", KT), ("b_f", 1)]
TOTAL = 14 + 4 + 32 + 12 + 4 + 32 + 8 + 32 + 8 + 4 + 4 + 32


class Mark:

    def __init__(self, lane, count, loop):
        self.lane, self.count, self.loop = lane, count, loop

    def value(self):
        if self.loop is None:
            return self.count
        i, per = self.loop
        return i * per + self.count


class Lane:

    def __init__(self, eng, sem):
        self.eng, self.sem, self.n, self.loop = eng, sem, 0, None

    def mark(self, ins):
        ins.then_inc(self.sem, 1)
        self.n += 1
        return Mark(self, self.n, self.loop)

    def wait(self, *marks):
        for m in marks:
            if m is not None:
                self.eng.wait_ge(m.lane.sem, m.value())

    def after(self):
        self.eng.wait_ge(self.sem, Mark(self, self.n, self.loop).value())

    def last(self):
        return Mark(self, self.n, self.loop)

    def then(self):
        self.after()
        return self.eng


def build(nc, p, out, stop=None):
    ctx = ExitStack()
    with ctx:
        def sb(name, shape, dt=F32):
            return ctx.enter_context(nc.sbuf_tensor(name, shape, dt))

        def sem(name):
            return ctx.enter_context(nc.semaphore(name))

        x = sb("x_res", [P, KT, S])
        xa = sb("x_scaled", [P, KT, S])
        hh = sb("act_hi", [P, KT, S], F32R)
        hl = sb("act_lo", [P, KT, S], F32R)
        stage = [sb(f"w_stage{s}", [P, 2048]) for s in range(2)]
        whi = [sb(f"w_hi{s}", [P, 2048], F32R) for s in range(2)]
        wlo = [sb(f"w_lo{s}", [P, 2048], F32R) for s in range(2)]
        ada = sb("ada_stage", [P, 4, KT * P])
        adacc = sb("ada_acc", [P, 4, P])
        mod = sb("mod", [P, 2 * UNITS])
        ident = sb("ident", [P, P])
        ones = sb("ones", [P, P])
        ones_h = sb("ones_h", [P, P])
        blk = sb("ones_blk", [P, P])
        eps = sb("eps", [P, 1])
        zero = sb("zero", [P, 1])
        one = sb("one", [P, 1])
        halfpi = sb("halfpi", [P, 1])
        jt = sb("rotate", [P, P])
        zr = sb("zero_r", [P, S], F32R)
        rstd = sb("rstd", [P, S])
        gain = sb("gain", [P, KT])
        small = sb("small", [P, 64])
        arena = sb("arena", [P, ARENA])
        PS = ctx.enter_context(nc.psum_tensor("PS", [P, 4096], F32))

        def bank(b, n=512, w=1):
            return PS[:, b * 512:b * 512 + n]

        V = Lane(nc.vector, sem("vector_done"))
        A = Lane(nc.scalar, sem("scalar_done"))
        T = Lane(nc.tensor, sem("tensor_done"))
        G = Lane(nc.gpsimd, sem("gpsimd_done"))
        lanes = [V, A, T, G]
        w_here = [sem(f"w_here{s}") for s in range(2)]
        w_hi_done = sem("w_hi_done")
        w_lo_done = sem("w_lo_done")
        w_used = sem("w_used")
        out_free = sem("out_free")
        ada_here = [sem(f"ada_here{s}") for s in range(4)]
        ada_mult = sem("ada_mult")
        ada_sum = sem("ada_sum")
        ada_col = sem("ada_col")
        s_par = sem("params_here")
        s_par2 = sem("params2_here")
        s_x = sem("x_here")
        s_dma = sem("moves")
        s_out = sem("out_written")

        class Loop:

            def __init__(self, count, **per):
                self.count, self.per = count, [per.get(k, 0) for k in "VATG"]

            def __enter__(self):
                self.cm = nc.Fori(0, self.count)
                i = self.cm.__enter__()
                self.n0 = [l.n for l in lanes]
                for l, q in zip(lanes, self.per):
                    l.loop = (i, q)
                return i

            def __exit__(self, *e):
                if e[0] is None:
                    got = [l.n - n for l, n in zip(lanes, self.n0)]
                    assert got == self.per, (got, self.per)
                for l, n, q in zip(lanes, self.n0, self.per):
                    l.loop = None
                    l.n = n + q * self.count
                return self.cm.__exit__(*e)

        par = {}
        off = 0
        PARS = [(n, w) for n, w in PARAM_COLS]
        ptile = sb("params", [P, sum(w for _, w in PARS)])
        for n, w in PARS:
            par[n] = ptile[:, off:off + w]
            off += w
        nc.sync.dma_start(par["c"], p["params"][:, 0:KT]).then_inc(s_par, 16)
        nc.scalar.dma_start(ptile[:, KT:], p["params"][:, KT:]).then_inc(s_par2, 16)
        nc.scalar.dma_start(x[:], p["x"]).then_inc(s_x, 16)
        G.mark(nc.gpsimd.memset(ident[:], 0.0))
        G.mark(G.then().memset(ones[:], 1.0 / D))
        G.mark(G.then().memset(ones_h[:], 1.0 / P))
        G.mark(G.then().memset(blk[:], 0.0))
        G.after()
        G.mark(G.then().memset(blk[0:64, 0:64], 1.0 / HD))
        G.mark(G.then().memset(blk[64:128, 64:128], 1.0 / HD))
        G.mark(G.then().affine_select(out=ident[:], in_=ident[:], compare_op=ALU.not_equal, fill=1.0,
                                       base=0, pattern=[[-1, P]], channel_multiplier=1))
        G.mark(G.then().memset(jt[:], 0.0))
        G.mark(G.then().affine_select(out=jt[:], in_=jt[:], compare_op=ALU.not_equal, fill=-1.0, base=-64,
                                      pattern=[[-1, P]], channel_multiplier=1))
        G.mark(G.then().affine_select(out=jt[:], in_=jt[:], compare_op=ALU.not_equal, fill=1.0, base=64,
                                      pattern=[[-1, P]], channel_multiplier=1))
        G.mark(G.then().memset(eps[:], EPS))
        G.mark(G.then().memset(zero[:], 0.0))
        G.mark(G.then().memset(one[:], 1.0))
        G.mark(G.then().memset(halfpi[:], float(np.pi / 2)))
        consts = G.mark(G.then().memset(zr[:].bitcast(F32), 0.0))
        masks = [arena[:, ARENA - 1024 + n * P:ARENA - 1024 + (n + 1) * P] for n in range(8)]
        G.mark(G.then().memset(arena[:, ARENA - 1024:ARENA], 0.0))
        for lev in range(7):
            c = 2 ** lev
            view = masks[lev].rearrange("p (n a c) -> p n a c", a=2, c=c)
            G.mark(G.then().memset(view[:, :, 1, :], 1.0))
        for lev in range(7):
            c = 2 ** lev
            n = P // (2 * c)
            view = masks[lev].rearrange("p (n r) -> p n r", n=n)
            G.mark(G.then().affine_select(out=view, in_=view, compare_op=ALU.is_ge, fill=0.0, base=0,
                                          pattern=[[-2 * c, n], [0, 2 * c]], channel_multiplier=1))
            G.mark(G.then().affine_select(out=view, in_=view, compare_op=ALU.is_ge, fill=0.0, base=c - 1,
                                          pattern=[[2 * c, n], [0, 2 * c]], channel_multiplier=-1))
        G.mark(G.then().tensor_copy(masks[7], ident[:]))
        nc.tensor.sem_inc(w_used, 2)
        nc.vector.sem_inc(out_free, 2)
        nc.vector.sem_inc(ada_sum, 4)
        nc.tensor.sem_inc(ada_col, 4)

        cact = small[:, 0:KT]
        nc.scalar.wait_ge(s_par, 16)
        silu_c = A.mark(nc.scalar.activation(small[:, 8:16], par["c"], ACT.Sigmoid))
        V.wait(silu_c)
        c_ready = V.mark(nc.vector.tensor_tensor(cact, small[:, 8:16], par["c"], ALU.mult))
        G.wait(c_ready)

        ada_slot = [0, 0, 0, 0]
        state = {"a": 0, "q": 0}
        segments = []

        def unit_index(slots, u, i):
            if i is None:
                return state["a"] + u
            if isinstance(i, tuple):
                return i[0] * 4 + (state["a"] + 2 * i[1] + u)
            return i * len(slots) + (state["a"] + u)

        def ada_units(n, slots, i=None):
            for u, s in enumerate(slots):
                r = i[0] if isinstance(i, tuple) else i
                land = ada_slot[s] + 1 if i is None else r + (ada_slot[s] + 1)
                t = ada[:, s, :].rearrange("p (k n) -> p k n", k=KT)
                nc.gpsimd.wait_ge(ada_here[s], land * 16)
                nc.gpsimd.tensor_tensor(t, t, cact.unsqueeze(2).to_broadcast([P, KT, P]),
                                        ALU.mult).then_inc(ada_mult, 1)

        def ada_sums(slots, i=None):
            for u, s in enumerate(slots):
                a = unit_index(slots, u, i)
                t = ada[:, s, :].rearrange("p (k n) -> p n k", k=KT)
                nc.vector.wait_ge(ada_mult, a + 1)
                nc.vector.wait_ge(ada_col, a + 1)
                nc.vector.tensor_reduce(adacc[:, s, :], t, AX.X, ALU.add).then_inc(ada_sum, 1)

        def ada_cols(slots, i=None):
            for u, s in enumerate(slots):
                a = unit_index(slots, u, i)
                nc.tensor.wait_ge(ada_sum, a + 5)
                nc.tensor.matmul(PS[:, bass.ds(a + 6 * 512, 1)] if i is not None
                                 else PS[:, 3072 + a:3073 + a],
                                 adacc[:, s, :], ones_f[:, 0:1], start=True, stop=True,
                                 skip_group_check=True).then_inc(ada_col, 1)

        def ada_advance(slots, turns=1):
            for s in slots:
                ada_slot[s] += turns
            state["a"] += len(slots) * turns

        ones_f = sb("ones_f", [P, 1])
        ones_ready = V.mark(nc.vector.memset(ones_f[:], 1.0))
        T.wait(ones_ready)

        def mod_add(a0, a1):
            nc.vector.wait_ge(ada_col, a1 + 4)
            return V.mark(nc.vector.tensor_tensor(mod[:, a0:a1], PS[:, 3072 + a0:3072 + a1],
                                                  par["ada_b"][:, a0:a1], ALU.add))

        def prep(q, s):
            nc.scalar.wait_ge(w_here[s], q * 8 + (16 - 8 * s))
            nc.scalar.wait_ge(w_used, q + 1)
            for h in range(2):
                c = slice(h * 1024, (h + 1) * 1024)
                nc.scalar.activation(whi[s][:, c], stage[s][:, c], ACT.Copy).then_inc(w_hi_done, 1)
                nc.vector.wait_ge(w_hi_done, q * 2 + (h + 1))
                nc.vector.tensor_tensor(wlo[s][:, c], stage[s][:, c], whi[s][:, c].bitcast(F32),
                                        ALU.subtract).then_inc(w_lo_done, 1)

        def half_ready(q, h):
            nc.tensor.wait_ge(w_lo_done, q * 2 + (h + 1))

        def up_products(q, s, o_of, token_major):
            wh = whi[s][:].rearrange("p (k n) -> p k n", k=KT)
            wl = wlo[s][:].rearrange("p (k n) -> p k n", k=KT)
            half_ready(q, 0)
            for t in range(2):
                o, c = o_of(t), slice(t * P, (t + 1) * P)
                for k in range(KT):
                    if t == 0 and k == KT // 2:
                        half_ready(q, 1)
                    for n, (w, a) in enumerate(((wh, hh), (wh, hl), (wl, hh))):
                        first, last = k == 0 and n == 0, k == KT - 1 and n == 2
                        if token_major:
                            m = nc.tensor.matmul(o, a[:, k, c], w[:, k, :], start=first, stop=last)
                        else:
                            m = nc.tensor.matmul(o, w[:, k, c], a[:, k, :], start=first, stop=last)
            m.then_inc(w_used, 1)

        def gemm_chunk(q, s, token_major):
            nc.tensor.wait_ge(out_free, q_out(q) + 1)
            up_products(q, s, lambda t: PS[:, s * 512 + t * S:s * 512 + (t + 1) * S], token_major)

        outs = {"n": 0}

        def q_out(q):
            return q - outs["n"]

        def gemm(n, evac, token_major=False, units=(), per=None, last=False):
            per = dict(per or {})
            segments.append((n // 2, 2, tuple(units)))
            q0 = state["q"]
            with Loop(n // 2, **per) as i:
                for s in range(2):
                    q = i * 2 + (q0 + s)
                    half = units[s * len(units) // 2:(s + 1) * len(units) // 2]
                    prep(q + 1, 1 - s)
                    gemm_chunk(q, s, token_major)
                    if s == 0 and units:
                        ada_units(len(units), units, i)
                        ada_sums(units, i)
                    if s == 1 and units:
                        ada_cols(units, i)
                    evac(i, s, q)
            if units:
                ada_advance(units, n // 2)
            state["q"] += n

        def product_ready(lane, q):
            lane.eng.wait_ge(w_used, q + 3)

        def norm(gain_of, shift_cols, same_x=False, split=True):
            sq = arena[:, 0:KT * S].rearrange("p (k t) -> p k t", k=KT)
            sums = PS[:, 7 * 512:7 * 512 + S]
            A.wait(V.last())
            A.wait(T.last())
            V.wait(A.last())
            if not same_x:
                for k in range(KT):
                    m = A.mark(nc.scalar.activation(sq[:, k, :], x[:, k, :], ACT.Square))
                    T.wait(m)
                    mm = nc.tensor.matmul(sums, ones[:], sq[:, k, :], start=k == 0, stop=k == KT - 1)
                summed = T.mark(mm)
            for k in range(KT):
                scaled = A.mark(nc.scalar.activation(xa[:, k, :], x[:, k, :], ACT.Copy,
                                                     scale=gain_of[:, k:k + 1]))
            if not same_x:
                A.wait(summed)
                root = A.mark(nc.scalar.activation(rstd[:, 0:S], sums, ACT.Sqrt, bias=eps[:]))
                V.wait(root)
                V.mark(nc.vector.reciprocal(rstd[:, 0:S], rstd[:, 0:S]))
                V.after()
            V.wait(scaled)
            prods = []
            for k in range(KT):
                prods.append(V.mark(nc.vector.tensor_tensor(xa[:, k, :], xa[:, k, :], rstd[:, 0:S], ALU.mult)))
            if not split:
                return
            for k in range(KT):
                sh = shift_cols[:, k:k + 1] if shift_cols is not None else zero[:]
                A.wait(prods[k])
                hi = A.mark(nc.scalar.activation(hh[:, k, :], xa[:, k, :], ACT.Identity, bias=sh))
                V.wait(hi)
                lo = V.mark(nc.vector.scalar_tensor_tensor(hl[:, k, :], xa[:, k, :], sh,
                                                           hh[:, k, :].bitcast(F32), ALU.add, ALU.subtract))
            T.wait(lo)

        def gain_mod(g, scale_cols):
            V.after()
            V.mark(nc.vector.scalar_tensor_tensor(gain[:], scale_cols, 1.0, g, ALU.add, ALU.mult))

        def split_act(src, k, waits):
            A.wait(waits)
            hi = A.mark(nc.scalar.activation(hh[:, k, :], src, ACT.Copy))
            V.wait(hi)
            return V.mark(nc.vector.tensor_tensor(hl[:, k, :], src, hh[:, k, :].bitcast(F32), ALU.subtract))

        def residual_evac(gate_cols):
            def evac(i, s, q):
                product_ready(V, q)
                for t in range(2):
                    tile = i * 4 + (2 * s + t)
                    xt = x[:, bass.ds(tile, 1), :].rearrange("p a t -> p (a t)")
                    src = PS[:, s * 512 + t * S:s * 512 + (t + 1) * S]
                    g = gate_cols[:, bass.ds(tile, 1)] if gate_cols is not None else one[:]
                    m = nc.vector.scalar_tensor_tensor(xt, src, g, xt, ALU.mult, ALU.add)
                    V.mark(m)
                V.after()
                nc.vector.sem_inc(out_free, 1)
            return evac

        f_parts = sb("forget_parts", [112, S], F32R)
        f_sel = sb("forget_select", [112, 32], F32R)
        act_a = sb("mlp_relu", [P, 2 * S])
        act_y = act_a
        ah = sb("mlp_hi", [P, 2 * S], F32R)
        al = sb("mlp_lo", [P, 2 * S], F32R)

        def mlp(gate_of, units=()):
            q0 = state["q"]
            segments.append((1, 1, ()))
            segments.append((MLP_CHUNKS // 2 - 1, 4, tuple(units)))
            segments.append((1, 2, tuple(units[:2])))
            segments.append((1, 1, tuple(units[2:])))
            T.wait(V.last())
            for b in range(4):
                for t in range(2):
                    nc.tensor.matmul(PS[:, b * 512 + t * S:b * 512 + (t + 1) * S], zr[:, 0:P], zr[:],
                                     start=t == 0, stop=False, skip_group_check=True)

            def up(q, s):
                up_products(q, s, lambda t: PS[:, 2048 + t * S:2048 + (t + 1) * S], False)

            def hidden(q, waits):
                product_ready(A, q)
                A.wait(waits)
                V.wait(A.mark(nc.scalar.activation(act_a[:], bank(4), ACT.Relu)))
                V.mark(nc.vector.tensor_tensor(act_a[:], act_a[:], act_a[:], ALU.mult))

            def split_hidden(squared, q_before):
                A.wait(squared)
                product_ready(A, q_before)
                V.wait(A.mark(nc.scalar.activation(ah[:], act_a[:], ACT.Copy)))
                return V.mark(nc.vector.tensor_tensor(al[:], act_a[:], ah[:].bitcast(F32), ALU.subtract))

            def down(q, s, lo):
                wh = whi[s][:].rearrange("p (k n) -> p k n", k=2)
                wl = wlo[s][:].rearrange("p (k n) -> p k n", k=2)
                T.wait(lo)
                for kk in range(2):
                    half_ready(q, kk)
                    a_h, a_l = ah[:, kk * S:(kk + 1) * S], al[:, kk * S:(kk + 1) * S]
                    for n in range(KT):
                        c = slice(n * P, (n + 1) * P)
                        for w, a in ((wh, a_h), (wh, a_l), (wl, a_h)):
                            m = nc.tensor.matmul(PS[:, n * S:(n + 1) * S], w[:, kk, c], a, start=False,
                                                 stop=False, skip_group_check=True)
                m.then_inc(w_used, 1)

            def turn(q, i, last_al, slots):
                relu = A.last()
                lo = split_hidden(V.last(), q - 1)
                T.wait(relu)
                up(q, 1)
                prep(q + 1, 0)
                down(q + 1, 0, lo)
                if slots:
                    ada_units(len(slots), slots, i)
                hidden(q, lo)
                prep(q + 2, 1)
                if slots:
                    ada_sums(slots, i)
                    ada_cols(slots, i)

            prep(q0 + 1, 1)
            up(q0, 0)
            hidden(q0, None)
            both = (units[:2], units[2:])
            with Loop(MLP_CHUNKS // 2 - 1, V=4, A=4) as i:
                for n in range(2):
                    turn(i * 4 + (q0 + 1 + 2 * n), (i, n) if units else i, None, both[n])
            if units:
                ada_advance(units, MLP_CHUNKS // 2 - 1)
            q = q0 + 2 * MLP_CHUNKS - 3
            turn(q, None, None, both[0])
            if units:
                ada_advance(both[0])
            q += 2
            lo = split_hidden(V.last(), q - 1)
            if units:
                ada_units(2, both[1])
                ada_sums(both[1])
            if q + 1 < TOTAL:
                prep(q + 1, 0)
            down(q, 1, lo)
            if units:
                ada_cols(both[1])
                ada_advance(both[1])
            state["q"] += 2 * MLP_CHUNKS
            outs["n"] += 2 * MLP_CHUNKS
            product_ready(V, q)
            g = gate_of()
            V.after()
            for n in range(KT):
                V.mark(nc.vector.scalar_tensor_tensor(x[:, n, :], PS[:, n * S:(n + 1) * S],
                                                      g[:, n:n + 1] if g is not None else one[:],
                                                      x[:, n, :], ALU.mult, ALU.add))
            V.after()

        def copy_evac(dst, scale=1.0):
            def evac(i, s, q):
                product_ready(A, q)
                o = dst[:, bass.ds(i * 4 + 2 * s, 2), :]
                A.mark(nc.scalar.activation(o, bank(s).rearrange("p (a t) -> p a t", a=2), ACT.Copy,
                                            scale=scale))
                A.after()
                nc.scalar.sem_inc(out_free, 1)
            return evac

        def copy_evac_tm(dst):
            def evac(i, s, q):
                product_ready(A, q)
                o = dst[:, :, bass.ds(i * 2 * CW + s * CW, CW)]
                A.mark(nc.scalar.activation(o, bank(s).rearrange("p (a t) -> p a t", a=2), ACT.Copy))
                A.after()
                nc.scalar.sem_inc(out_free, 1)
            return evac

        def carve(*sizes):
            o, got = 0, []
            for n in sizes:
                got.append(arena[:, o:o + n])
                o += n
            assert o <= ARENA, o
            return got

        def hgrn(u, vt):
            ab, ac, acth, hq, hf, hg = (u[:, 4 * n:4 * n + 4, :] for n in range(6))
            o = 24 * S + NB * 512
            pre, suf, ql, kl, kk, sc0, sc1, y, t1 = [arena[:, o + n * 1024:o + (n + 1) * 1024] for n in range(9)]
            heads = lambda t: t.rearrange("p (h t) -> p h t", h=HG_HEADS)
            A.wait(V.last())
            V.wait(A.last())
            sig = A.mark(nc.scalar.activation(hf, hf, ACT.Sigmoid))
            sig_g = A.mark(nc.scalar.activation(heads(y), hg, ACT.Sigmoid))
            lg = par["lb"]
            lb, oml, tmp, ex = small[:, 16:20], small[:, 20:24], small[:, 24:28], small[:, 28:40]
            V.mark(nc.vector.tensor_tensor(tmp, lg[:, 0:4], lg[:, 4:8], ALU.max))
            V.mark(V.then().tensor_tensor(tmp, tmp, lg[:, 8:12], ALU.max))
            for r in range(3):
                V.mark(V.then().tensor_tensor(ex[:, 4 * r:4 * r + 4], lg[:, 4 * r:4 * r + 4], tmp, ALU.subtract))
            A.wait(V.last())
            V.wait(A.mark(nc.scalar.activation(ex, ex, ACT.Exp)))
            V.mark(nc.vector.tensor_tensor(tmp, ex[:, 0:4], ex[:, 4:8], ALU.add))
            V.mark(V.then().tensor_tensor(tmp, tmp, ex[:, 8:12], ALU.add))
            V.mark(V.then().reciprocal(tmp, tmp))
            V.mark(V.then().tensor_tensor(lb, ex[:, 0:4], tmp, ALU.mult))
            V.mark(V.then().tensor_scalar(oml, lb, -1.0, 1.0, ALU.mult, ALU.add))
            V.wait(sig)
            V.after()
            for h in range(HG_HEADS):
                V.mark(nc.vector.tensor_scalar(heads(pre)[:, h, :], hf[:, h, :], oml[:, h:h + 1],
                                               lb[:, h:h + 1], ALU.mult, ALU.add))
            V.mark(V.then().tensor_scalar(kk, pre, -1.0, 1.0, ALU.mult, ALU.add))
            V.mark(nc.vector.memset(suf, 1.0))
            V.mark(nc.vector.memset(ql, 0.0))
            V.mark(nc.vector.memset(kl, 0.0))
            V.mark(nc.vector.memset(sc0, 0.0))
            V.mark(nc.vector.memset(sc1[:, 0:512], 0.0))
            sc0h = sc0.rearrange("p (h t) -> p h t", h=HG_HEADS)
            sc1h = sc1[:, 0:512].rearrange("p (h t) -> p h t", h=HG_HEADS)

            def block_scores(key, query, mask, waits):
                T.wait(waits)
                for b in range(NB):
                    for h in range(HG_HEADS):
                        cols = slice(h * S + b * P, h * S + (b + 1) * P)
                        m = nc.tensor.matmul(PS[:, (2 + b) * 512 + h * P:(2 + b) * 512 + (h + 1) * P],
                                             key[:, cols], query[:, cols], start=True, stop=True)
                V.wait(T.mark(m))
                for b, dst in ((0, sc0h[:, :, 0:P]), (1, sc1h)):
                    V.mark(V.then().copy_predicated(
                        dst, mask.bitcast(I32).unsqueeze(1).to_broadcast([P, HG_HEADS, P]),
                        bank(2 + b).rearrange("p (h t) -> p h t", h=HG_HEADS)))

            hqf = u[:, 12:16, :].rearrange("p h t -> p (h t)")
            block_scores(kk, hqf, masks[7], V.last())
            c = 1
            for lev in range(8):
                seg = lambda t: t.rearrange("p (n a c) -> p n a c", a=2, c=c)
                n = HG_HEADS * S // (2 * c)
                V.after()
                left_total = seg(pre)[:, :, 0, c - 1:c].to_broadcast([P, n, c])
                right_total = seg(pre)[:, :, 1, c - 1:c].to_broadcast([P, n, c])
                V.mark(nc.vector.tensor_tensor(seg(ql)[:, :, 1, :], seg(hqf)[:, :, 1, :],
                                               seg(pre)[:, :, 1, :], ALU.mult))
                V.mark(nc.vector.tensor_tensor(seg(kl)[:, :, 0, :], seg(kk)[:, :, 0, :],
                                               seg(suf)[:, :, 0, :], ALU.mult))
                scaled = V.last()
                if lev < 7:
                    V.mark(V.then().tensor_tensor(seg(suf)[:, :, 0, :], seg(suf)[:, :, 0, :], right_total,
                                                  ALU.mult))
                    V.mark(V.then().tensor_tensor(seg(pre)[:, :, 1, :], seg(pre)[:, :, 1, :], left_total,
                                                  ALU.mult))
                    block_scores(kl, ql, masks[lev], scaled)
                else:
                    T.wait(scaled)
                    for h in range(HG_HEADS):
                        m = nc.tensor.matmul(PS[:, 1024 + h * P:1024 + (h + 1) * P], kl[:, h * S:h * S + P],
                                             ql[:, h * S + P:(h + 1) * S], start=True, stop=True)
                    V.wait(T.mark(m))
                    V.mark(V.then().tensor_copy(sc0h[:, :, P:S], bank(2).rearrange("p (h t) -> p h t", h=HG_HEADS)))
                c *= 2
            T.wait(V.last())
            for h in range(HG_HEADS):
                o_h = PS[:, 2048 + h * S:2048 + (h + 1) * S]
                nc.tensor.matmul(o_h, vt[:, 0, h * P:(h + 1) * P], sc0h[:, h, :], start=True, stop=False,
                                 skip_group_check=True)
                m = nc.tensor.matmul(o_h[:, P:S], vt[:, 1, h * P:(h + 1) * P], sc1h[:, h, :], start=False,
                                     stop=True, skip_group_check=True)
            o_done = T.mark(m)
            A.wait(o_done)
            sq = A.mark(nc.scalar.activation(ql, PS[:, 2048:3072], ACT.Square))
            T.wait(sq)
            for b in range(2):
                m = nc.tensor.matmul(bank(2 + b), ones_h[:], ql[:, b * 512:(b + 1) * 512], start=True, stop=True)
            A.wait(T.mark(m))
            V.wait(A.mark(nc.scalar.activation(kl, PS[:, 1024:2048], ACT.Sqrt, bias=eps[:])))
            V.wait(sig_g)
            V.mark(V.then().reciprocal(kl, kl))
            V.mark(nc.vector.tensor_tensor(heads(y), heads(y), hg, ALU.mult))
            for h in range(HG_HEADS):
                V.after()
                V.mark(nc.vector.scalar_tensor_tensor(heads(t1)[:, h, :], PS[:, 2048 + h * S:2048 + (h + 1) * S],
                                                      par["hg_norm"][:, h:h + 1], heads(kl)[:, h, :],
                                                      ALU.mult, ALU.mult))
            V.mark(V.then().tensor_tensor(y, y, t1, ALU.mult))
            for h in range(HG_HEADS):
                split_act(heads(y)[:, h, :], 4 + h, V.last())
            cw = par["conv_w"]
            p_, cv = ql, kl
            V.mark(nc.vector.tensor_tensor(heads(p_), ac, acth, ALU.mult))
            for m_ in range(4):
                V.mark(V.then().tensor_scalar(heads(cv)[:, m_, :], heads(p_)[:, m_, :], cw[:, 8 + m_:9 + m_],
                                              None, ALU.mult))
            for tap, sh in ((1, 1), (0, 2)):
                for m_ in range(4):
                    d = heads(cv)[:, m_, sh:S]
                    V.after()
                    V.mark(nc.vector.scalar_tensor_tensor(d, heads(p_)[:, m_, 0:S - sh],
                                                          cw[:, 4 * tap + m_:4 * tap + m_ + 1], d,
                                                          ALU.mult, ALU.add))
            V.mark(V.then().tensor_tensor(heads(cv), heads(cv), ab, ALU.mult))
            for m_ in range(4):
                lo = split_act(heads(cv)[:, m_, :], m_, V.last())
            T.wait(lo)

        def attend_out(h, w_s0, w_s1, vt, waits):
            po, pr = HD * (h % 2), h // 2
            o = PS[po:po + HD, (6 + pr % 2) * 512:(6 + pr % 2) * 512 + S]
            T.wait(waits)
            nc.tensor.matmul(o, vt[:, 0, h * HD:(h + 1) * HD], w_s0, start=True, stop=False,
                             skip_group_check=True)
            return T.mark(nc.tensor.matmul(o[:, P:S], vt[:, 1, h * HD:(h + 1) * HD], w_s1, start=False,
                                           stop=True, skip_group_check=True))

        def split_pair(pr, waits):
            return split_act(PS[:, (6 + pr % 2) * 512:(6 + pr % 2) * 512 + S], pr, waits)

        def scores(h, qk, b_of, waits, stop=True):
            po, pr = HD * (h % 2), h // 2
            T.wait(*waits)
            z = bank(b_of)
            nc.tensor.matmul(z[:, 0:P], qk[po:po + HD, pr, 0:P], qk[po:po + HD, 8 + pr, 0:P], start=True,
                             stop=stop, skip_group_check=True)
            return nc.tensor.matmul(z[:, P:P + S], qk[po:po + HD, pr, P:S], qk[po:po + HD, 8 + pr, :],
                                    start=True, stop=stop, skip_group_check=True)

        def stick_breaking(qk, vt, work):
            A.wait(V.last())
            V.wait(A.last())
            T.wait(A.last())
            sq2 = [work[:, 0:512], work[:, 512:1024]]
            rs2 = [work[:, 1024:1536], work[:, 1536:2048]]
            used = [None, None]
            freed = [None, None]
            for n in range(8):
                src = qk[:, 2 * n:2 * n + 2, :].rearrange("p m t -> p (m t)")
                A.wait(used[n % 2])
                T.wait(A.mark(nc.scalar.activation(sq2[n % 2], src, ACT.Square)))
                m = T.mark(nc.tensor.matmul(bank(2 + n % 2), blk[:], sq2[n % 2], start=True, stop=True))
                used[n % 2] = m
                A.wait(m, freed[n % 2])
                V.wait(A.mark(nc.scalar.activation(rs2[n % 2], bank(2 + n % 2), ACT.Sqrt, bias=eps[:])))
                V.mark(nc.vector.reciprocal(rs2[n % 2], rs2[n % 2]))
                g = par["q_norm"] if n < 4 else par["k_norm"]
                freed[n % 2] = V.mark(V.then().scalar_tensor_tensor(src, src, g, rs2[n % 2], ALU.mult, ALU.mult))
            A.wait(V.last())
            W = P + S
            bt = [work[:, n * W:(n + 1) * W] for n in (0, 1)]
            om = [work[:, n * W:(n + 1) * W] for n in (2, 3)]
            o = 4 * W
            pr_ = [work[:, o + n * (W + 2):o + (n + 1) * (W + 2)] for n in (0, 1)]
            o += 2 * (W + 2)
            wt = [work[:, o + n * W:o + (n + 1) * W] for n in (0, 1)]
            o += 2 * W
            late, keep = work[:, o:o + S], work[:, o + S:o + S + W]
            V.mark(V.then().memset(late[:, 0:P], 0.0))
            V.mark(nc.vector.memset(late[:, P:S], 1.0))
            V.mark(nc.vector.memset(keep, 1.0))
            G.wait(V.last())
            G.mark(G.then().affine_select(out=late[:, P:S], in_=late[:, P:S], compare_op=ALU.is_ge, fill=0.0,
                                           base=0, pattern=[[1, P]], channel_multiplier=-1))
            for c in (0, S):
                G.mark(G.then().affine_select(out=keep[:, c:c + P], in_=keep[:, c:c + P], compare_op=ALU.is_ge,
                                               fill=0.0, base=-1, pattern=[[1, P]], channel_multiplier=-1))
            for n in (0, 1):
                V.mark(nc.vector.memset(pr_[n][:, P:P + 1], 1.0))
                V.mark(nc.vector.memset(pr_[n][:, W + 1:W + 2], 1.0))
            V.wait(G.last())
            T.wait(V.last())
            z_read, w_done, w_read, wt_done, pv, o_read = {}, {}, {}, {}, {}, {}

            def weights(h):
                n = h % 2
                zz = T.mark(scores(h, qk, n, (z_read.get(h - 2),)))
                A.wait(zz, w_read.get(h - 2))
                A.mark(nc.scalar.activation(bt[n], bank(n)[:, 0:W], ACT.Sigmoid, scale=HD ** -0.5))
                z_read[h] = A.mark(nc.scalar.activation(om[n], bank(n)[:, 0:W], ACT.Sigmoid,
                                                        scale=-HD ** -0.5))
                V.wait(z_read[h])
                q = pr_[n]
                V.mark(nc.vector.tensor_tensor_scan(q[:, 0:P][:, ::-1], om[n][:, 0:P][:, ::-1],
                                                    late[:, P:S][:, ::-1], 1.0, ALU.mult, ALU.max))
                V.mark(nc.vector.tensor_tensor_scan(q[:, P + 1:W + 1][:, ::-1], om[n][:, P:W][:, ::-1],
                                                    late[:, ::-1], 1.0, ALU.mult, ALU.max))
                V.mark(V.then().tensor_tensor(bt[n][:, 0:P], bt[n][:, 0:P], q[:, 1:P + 1], ALU.mult))
                w_done[h] = V.mark(nc.vector.tensor_tensor(bt[n][:, P:W], bt[n][:, P:W],
                                                           q[:, P + 2:W + 2], ALU.mult))

            def turned(h):
                n = h % 2
                T.wait(w_done[h], wt_done.get(h - 2))
                wb = bank(2 + n)
                for c in (0, P, S):
                    m = nc.tensor.transpose(wb[:, c:c + P], bt[n][:, c:c + P], ident[:])
                w_read[h] = T.mark(m)
                V.wait(w_read[h], pv.get(h - 2))
                wt_done[h] = V.mark(nc.vector.tensor_tensor(wt[n], wb[:, 0:W], keep, ALU.mult))

            def values(h):
                n, pr = h % 2, h // 2
                if n == 0:
                    T.wait(o_read.get(pr - 2))
                pv[h] = attend_out(h, wt[n][:, 0:S], wt[n][:, S:W], vt, wt_done[h])
                if n:
                    o_read[pr] = split_pair(pr, pv[h])

            for step in range(HEADS + 2):
                if step < HEADS:
                    weights(step)
                if 1 <= step <= HEADS:
                    turned(step - 1)
                if step >= 2:
                    values(step - 2)
            T.wait(o_read[HEADS // 2 - 1])

        def glu_evac(sg):
            def evac(i, s, q):
                product_ready(A, q)
                A.wait(V.last())
                V.wait(A.mark(nc.scalar.activation(sg[s], PS[:, s * 512 + S:s * 512 + 2 * S], ACT.Sigmoid)))
                V.mark(nc.vector.tensor_tensor(sg[s], PS[:, s * 512:s * 512 + S], sg[s], ALU.mult))
                xt = x[:, bass.ds(i * 2 + s, 1), :].rearrange("p a t -> p (a t)")
                V.mark(V.then().tensor_tensor(xt, xt, sg[s], ALU.add))
                V.after()
                nc.vector.sem_inc(out_free, 1)
            return evac

        def ssm():
            wide = lambda t: t.unsqueeze(2).to_broadcast([P, GROUPS, GC])
            gc = lambda t: t.rearrange("p (g c) -> p g c", g=GROUPS)
            big1, big2 = arena[:, 0:8192], arena[:, 8192:16384]
            rest = arena[:, 16384:24576]
            bs, bsw, cs, csw, t1, t2 = [rest[:, n * 1024:(n + 1) * 1024] for n in range(6)]
            kcol = rest[:, 6144:7168]
            tiny = ada[:, 0, :], ada[:, 1, :], ada[:, 2, :], ada[:, 3, :]
            A.wait(V.last(), T.last())
            V.wait(A.last())
            ssm_in = p["ssm_in"]
            w0 = GROUPS * 3
            nc.scalar.dma_start(tiny[0][:, 0:w0], ssm_in[:, 0:w0]).then_inc(s_dma, 16)
            nc.scalar.dma_start(rest[:, 0:4096], ssm_in[:, w0:w0 + 4096]).then_inc(s_dma, 16)
            ldt, are, aim = [tiny[0][:, n * 64:(n + 1) * 64] for n in range(3)]
            tn = lambda n: tiny[1][:, n * 64:(n + 1) * 64]
            t2n = lambda n: tiny[0][:, 192 + n * 64:256 + n * 64]
            dt, er, th, rn, co, si, den, wr, wi, nr = [tn(n) for n in range(10)]
            tt, tu = t2n(0), t2n(1)
            powr = [tiny[2][:, n * 64:(n + 1) * 64] for n in range(13)]
            powi = [tiny[3][:, n * 64:(n + 1) * 64] for n in range(13)]
            sgn = small[:, 40:41]
            nsgn = small[:, 41:42]
            V.mark(nc.vector.memset(small[0:64, 40:41], -1.0))
            V.mark(nc.vector.memset(small[64:128, 40:41], 1.0))
            V.mark(nc.vector.memset(small[0:64, 41:42], 1.0))
            V.mark(nc.vector.memset(small[64:128, 41:42], -1.0))
            nc.scalar.wait_ge(s_dma, 32)
            nc.vector.wait_ge(s_dma, 32)
            V.wait(A.mark(nc.scalar.activation(dt, ldt, ACT.Exp)))
            V.mark(nc.vector.tensor_tensor(er, are, dt, ALU.mult))
            V.mark(nc.vector.tensor_tensor(th, aim, dt, ALU.mult))
            A.wait(V.last())
            mag = A.mark(nc.scalar.activation(er, er, ACT.Exp))
            V.mark(V.then().tensor_scalar(rn, th, 1.0 / TWO_PI, ROUND, ALU.mult, ALU.add))
            V.mark(V.then().tensor_scalar(rn, rn, -ROUND, None, ALU.add))
            for part in (PI_A, PI_B, PI_C):
                V.mark(V.then().scalar_tensor_tensor(th, rn, -part, th, ALU.mult, ALU.add))
            V.mark(V.then().tensor_scalar(th, th, -3.1415925, 3.1415925, ALU.max, ALU.min))
            A.wait(V.last())
            A.mark(nc.scalar.activation(si, th, ACT.Sin))
            A.mark(nc.scalar.activation(co, th, ACT.Abs))
            A.mark(A.then().activation(co, co, ACT.Sin, scale=-1.0, bias=halfpi[:]))
            V.wait(A.last())
            lr, li = powr[1], powi[1]
            V.mark(nc.vector.tensor_tensor(lr, er, co, ALU.mult))
            V.mark(nc.vector.tensor_tensor(li, er, si, ALU.mult))
            V.mark(nc.vector.memset(powr[0], 1.0))
            V.mark(nc.vector.memset(powi[0], 0.0))

            def cmul(o_r, o_i, a_r, a_i, b_r, b_i):
                V.mark(V.then().tensor_tensor(tt, a_i, b_i, ALU.mult))
                V.mark(nc.vector.tensor_tensor(tu, a_i, b_r, ALU.mult))
                V.mark(V.then().tensor_tensor(o_r, a_r, b_r, ALU.mult))
                V.mark(nc.vector.tensor_tensor(o_i, a_r, b_i, ALU.mult))
                V.mark(V.then().tensor_tensor(o_r, o_r, tt, ALU.subtract))
                V.mark(nc.vector.tensor_tensor(o_i, o_i, tu, ALU.add))

            for k in range(2, 9):
                cmul(powr[k], powi[k], powr[k // 2], powi[k // 2], powr[k - k // 2], powi[k - k // 2])
            for k in range(9, 13):
                cmul(powr[k], powi[k], powr[k - 1], powi[k - 1], powr[k - 1], powi[k - 1])
            V.mark(V.then().tensor_scalar(nr, lr, -1.0, None, ALU.add))
            V.mark(nc.vector.tensor_tensor(den, are, are, ALU.mult))
            V.mark(nc.vector.tensor_tensor(tt, aim, aim, ALU.mult))
            V.mark(V.then().tensor_tensor(den, den, tt, ALU.add))
            V.mark(V.then().reciprocal(den, den))
            V.mark(nc.vector.tensor_tensor(wr, nr, are, ALU.mult))
            V.mark(nc.vector.tensor_tensor(tt, li, aim, ALU.mult))
            V.mark(nc.vector.tensor_tensor(wi, li, are, ALU.mult))
            V.mark(nc.vector.tensor_tensor(tu, nr, aim, ALU.mult))
            V.mark(V.then().tensor_tensor(wr, wr, tt, ALU.add))
            V.mark(nc.vector.tensor_tensor(wi, wi, tu, ALU.subtract))
            V.mark(V.then().tensor_tensor(wr, wr, den, ALU.mult))
            V.mark(nc.vector.tensor_tensor(wi, wi, den, ALU.mult))
            V.mark(V.then().tensor_scalar(bsw, bsw, sgn, None, ALU.mult))
            V.mark(nc.vector.tensor_scalar(cs, cs, nsgn, None, ALU.mult))
            V.mark(V.then().tensor_tensor(gc(t1), gc(bs), wide(wr), ALU.mult))
            V.mark(nc.vector.tensor_tensor(gc(kcol), gc(bsw), wide(wi), ALU.mult))
            V.mark(V.then().tensor_tensor(t1, t1, kcol, ALU.add))
            V.mark(nc.vector.tensor_tensor(gc(t2), gc(bsw), wide(wr), ALU.mult))
            V.mark(V.then().tensor_tensor(gc(kcol), gc(bs), wide(wi), ALU.mult))
            V.mark(V.then().tensor_tensor(t2, t2, kcol, ALU.subtract))
            g4 = big1.rearrange("p (g i c) -> p g i c", g=GROUPS, i=TAPS)
            for i in range(TAPS):
                V.mark(V.then().tensor_tensor(gc(kcol), gc(t2), wide(powi[7 - i]), ALU.mult))
                V.mark(nc.vector.tensor_tensor(g4[:, :, i, :], gc(t1), wide(powr[7 - i]), ALU.mult))
                V.mark(V.then().tensor_tensor(g4[:, :, i, :], g4[:, :, i, :], gc(kcol), ALU.add))
            T.wait(V.last())
            for n in range(GROUPS // 4):
                b = n % 2
                for g in range(4):
                    m = nc.tensor.transpose(PS[:, b * 512 + g * P:b * 512 + (g + 1) * P],
                                            big1[:, (4 * n + g) * P:(4 * n + g + 1) * P], ident[:])
                A.wait(T.mark(m))
                cp = A.mark(nc.scalar.activation(big2[:, n * 512:(n + 1) * 512], bank(b), ACT.Copy))
                if n == 0:
                    first_cp = cp
                if n >= 1:
                    T.wait(prev)
                prev = cp
            for g in range(GROUPS):
                m = nc.tensor.matmul(PS[:, 1024 + g * GC:1024 + (g + 1) * GC], big1[:, g * P:(g + 1) * P],
                                     cs[:, g * GC:(g + 1) * GC], start=True, stop=True)
            A.wait(T.mark(m), V.last())
            taps_done = A.mark(nc.scalar.activation(kcol, PS[:, 1024:2048], ACT.Copy))
            V.wait(taps_done)
            V.mark(V.then().memset(big1, 0.0))
            toep = big1.rearrange("p (g i c) -> p g i c", g=GROUPS, i=TAPS)
            moved = [bs, bsw, t1, t2]
            A.wait(V.last())
            for rnd in range(2):
                A.after()
                for n in range(4):
                    rows = (4 * rnd + n + 1) * GC
                    nc.scalar.dma_start(moved[n][0:rows, :], kcol[P - rows:P, :]).then_inc(s_dma, 16)
                nc.scalar.wait_ge(s_dma, 32 + 64 * (rnd + 1))
                for n in range(4):
                    i = 4 * rnd + n
                    rows = (i + 1) * GC
                    A.mark(nc.scalar.activation(toep[0:rows, :, i, :], gc(moved[n])[0:rows], ACT.Copy))
            uc, xs, tmp = rest[:, 0:2048], rest[:, 4096:6144], rest[:, 7168:8192]
            ident32 = ident[0:NJ, 0:NJ]
            vbuf = [tiny[0], tiny[1]]
            A.after()
            V.wait(A.last())
            V.after()
            for kt in range(KT):
                b = 4
                for i in range(TAPS):
                    src = xa[:, kt, :].rearrange("p (j i) -> p i j", i=TAPS)[:, i, :]
                    m = nc.tensor.transpose(PS[0:NJ, 2048 + i * P:2048 + (i + 1) * P], src, ident[:])
                V.wait(T.mark(m))
                vb = vbuf[kt % 2][0:NJ, :]
                V.mark(nc.vector.tensor_copy(
                    vb.rearrange("p (g i c) -> p i g c", g=8, i=TAPS),
                    PS[0:NJ, 2048:3072].rearrange("p (i g c) -> p i g c", i=TAPS, g=8)))
                T.wait(V.last())
                for g in range(8):
                    m = nc.tensor.transpose(PS[:, 3072 + g * NJ:3072 + (g + 1) * NJ],
                                            vb[:, g * P:(g + 1) * P], ident32)
                A.wait(T.mark(m))
                A.mark(nc.scalar.activation(uc[:, kt * 256:(kt + 1) * 256], PS[:, 3072:3328], ACT.Copy))
                T.wait(A.last())
            for g in range(GROUPS):
                m = nc.tensor.matmul(PS[:, g * NJ:(g + 1) * NJ], big2[:, g * P:(g + 1) * P],
                                     uc[:, g * NJ:(g + 1) * NJ], start=True, stop=True)
            z_done = T.mark(m)
            A.wait(z_done)
            A.mark(nc.scalar.activation(xs, PS[:, 0:2048], ACT.Copy))
            T.wait(A.last())
            V.wait(A.last())
            h4 = big2.rearrange("p (g i c) -> p g i c", g=GROUPS, i=TAPS)
            for i in range(TAPS):
                V.mark(V.then().tensor_tensor(gc(kcol), gc(csw), wide(powi[i + 1]), ALU.mult))
                V.mark(nc.vector.tensor_tensor(h4[:, :, i, :], gc(cs), wide(powr[i + 1]), ALU.mult))
                V.mark(V.then().tensor_tensor(h4[:, :, i, :], h4[:, :, i, :], gc(kcol), ALU.subtract))
            xj = xs.rearrange("p (g j) -> p g j", g=GROUPS)
            for lev in range(5):
                s_ = 2 ** lev
                n = NJ - s_
                pr_, pi_ = powr[8 + lev], powi[8 + lev]
                T.wait(V.last())
                for b in range(4):
                    m = nc.tensor.matmul(bank(b), jt[:], xs[:, b * 512:(b + 1) * 512], start=True, stop=True)
                V.wait(T.mark(m))
                jx = PS[:, 0:2048].rearrange("p (g j) -> p g j", g=GROUPS)
                t_ = PS[:, 2048:4096].rearrange("p (g j) -> p g j", g=GROUPS)
                V.mark(V.then().tensor_tensor(t_[:, :, s_:NJ], xj[:, :, 0:n],
                                              pr_.unsqueeze(2).to_broadcast([P, GROUPS, n]), ALU.mult))
                V.mark(V.then().tensor_tensor(xj[:, :, s_:NJ], xj[:, :, s_:NJ], t_[:, :, s_:NJ], ALU.add))
                V.mark(V.then().tensor_tensor(t_[:, :, s_:NJ], jx[:, :, 0:n],
                                              pi_.unsqueeze(2).to_broadcast([P, GROUPS, n]), ALU.mult))
                V.mark(V.then().tensor_tensor(xj[:, :, s_:NJ], xj[:, :, s_:NJ], t_[:, :, s_:NJ], ALU.add))
            T.wait(V.last())
            for g in range(GROUPS):
                nc.tensor.matmul(PS[:, g * NJ:(g + 1) * NJ], big1[:, g * P:(g + 1) * P], uc[:, g * NJ:(g + 1) * NJ],
                                 start=True, stop=False, skip_group_check=True)
                m = nc.tensor.matmul(PS[:, g * NJ + 1:(g + 1) * NJ], big2[:, g * P:(g + 1) * P],
                                     xj[:, g, 0:NJ - 1], start=False, stop=True, skip_group_check=True)
            A.wait(T.mark(m))
            A.mark(nc.scalar.activation(uc, PS[:, 0:2048], ACT.Copy))
            T.wait(A.last())
            V.wait(A.last())
            yt = [act_y[:, 0:S], act_y[:, S:2 * S]]
            done = {}
            for kt in range(KT):
                for g in range(8):
                    m = nc.tensor.transpose(PS[0:NJ, g * P:(g + 1) * P],
                                            uc[:, (kt * 8 + g) * NJ:(kt * 8 + g + 1) * NJ], ident[:])
                V.wait(T.mark(m))
                vb = vbuf[kt % 2][0:NJ, :]
                V.mark(nc.vector.tensor_copy(
                    vb.rearrange("p (i g c) -> p g i c", g=8, i=TAPS),
                    PS[0:NJ, 0:1024].rearrange("p (g i c) -> p g i c", i=TAPS, g=8)))
                T.wait(V.last())
                o = 1024 + (kt % 2) * 512
                for i in range(TAPS):
                    m = nc.tensor.transpose(PS[:, o + i * NJ:o + (i + 1) * NJ],
                                            vb[:, i * P:(i + 1) * P], ident32)
                V.wait(T.mark(m), done.get(kt - 2))
                yk = yt[kt % 2]
                V.mark(nc.vector.scalar_tensor_tensor(
                    yk.rearrange("p (j i) -> p j i", i=TAPS), xa[:, kt, :].rearrange("p (j i) -> p j i", i=TAPS),
                    par["ssm_d"][:, kt:kt + 1], PS[:, o:o + S].rearrange("p (i j) -> p j i", i=TAPS),
                    ALU.mult, ALU.add))
                A.wait(V.last())
                A.mark(nc.scalar.activation(yk, yk, ACT.Gelu_apprx_tanh))
                A.after()
                done[kt] = split_act(yk, kt, None)
            T.wait(V.last())

        def forget_gates(fw):
            z, a, cum = fw[0:16, 0:S], fw[0:16, S:2 * S], fw[0:16, 2 * S:3 * S]
            A.wait(A.last(), V.last())
            T.wait(V.last())
            wf = fw[:, 3 * S:3 * S + KT * 16].rearrange("p (k h) -> p k h", k=KT)
            nc.scalar.dma_start(wf, p["w_f"]).then_inc(s_par, 16)
            nc.tensor.wait_ge(s_par, 32)
            f = PS[0:16, 3584:3584 + S]
            for k in range(KT):
                m = nc.tensor.matmul(f, wf[:, k, :], xa[:, k, :], start=k == 0, stop=k == KT - 1)
            A.wait(T.mark(m))
            A.mark(nc.scalar.activation(z, f, ACT.Identity, bias=par["b_f"][0:16, :]))
            A.mark(A.then().activation(a, z, ACT.Abs))
            A.mark(A.then().activation(a, a, ACT.Exp, scale=-1.0))
            V.wait(A.mark(A.then().activation(a, a, ACT.Ln, bias=one[0:16, :])))
            V.mark(nc.vector.scalar_tensor_tensor(z, z, 0.0, a, ALU.min, ALU.subtract))
            V.mark(V.then().memset(a, 1.0))
            V.mark(V.then().tensor_tensor_scan(cum, a, z, 0.0, ALU.mult, ALU.add))
            V.mark(nc.vector.memset(f_parts[:].bitcast(F32), 0.0))
            for r in (0, 64):
                V.mark(V.then().tensor_copy(f_parts[r:r + 16, :], cum))
            V.mark(V.then().tensor_tensor(a, cum, f_parts[0:16, :].bitcast(F32), ALU.subtract))
            A.wait(V.last())
            for r in (32, 96):
                A.mark(nc.scalar.activation(f_parts[r:r + 16, :], a, ACT.Copy))
            V.mark(V.then().memset(f_sel[:].bitcast(F32), 0.0))
            for r in (0, 32, 64, 96):
                V.mark(V.then().tensor_copy(f_sel[r:r + 16, 0:16], ident[0:16, 0:16]))
                V.mark(nc.vector.tensor_scalar(f_sel[r:r + 16, 16:32], ident[0:16, 0:16], -1.0, None, ALU.mult))

        def fox(qk, vt, work):
            W = P + S
            we = [work[:, n * W:(n + 1) * W] for n in range(3)]
            wt = [work[:, n * W:(n + 1) * W] for n in (3, 4)]
            o = 5 * W
            later, st = work[:, o:o + P], work[:, o + P:o + P + 32]
            A.wait(V.last())
            V.wait(A.last())
            T.wait(A.last())
            V.mark(nc.vector.memset(later, -1e30))
            G.wait(V.last())
            T.wait(G.mark(G.then().affine_select(out=later, in_=later, compare_op=ALU.is_ge, fill=0.0, base=-1,
                                                 pattern=[[1, P]], channel_multiplier=-1)))
            T.wait(V.last())
            z_read, scaled, w_read, wt_done, pv, o_read = {}, {}, {}, {}, {}, {}

            def exps(h):
                n, po, pr = h % 2, HD * (h % 2), h // 2
                T.wait(z_read.get(h - 2))
                z = bank(n)
                for c, w, b in ((0, P, 0), (P, S, 1)):
                    zb = z[:, c:c + w]
                    nc.tensor.matmul(zb, qk[po:po + HD, pr, b * P:(b + 1) * P], qk[po:po + HD, 8 + pr, 0:w],
                                     start=True, stop=False, skip_group_check=True)
                    nc.tensor.matmul(zb, f_parts[po:po + 48, b * P:(b + 1) * P],
                                     f_sel[po:po + 48, h:h + 1].to_broadcast([48, w]),
                                     start=False, stop=False, skip_group_check=True)
                    nc.tensor.matmul(zb, f_sel[po:po + 48, 16 + h:17 + h].to_broadcast([48, P]),
                                     f_parts[po:po + 48, 0:w],
                                     start=False, stop=False, skip_group_check=True)
                    m = nc.tensor.matmul(z[:, c + w - P:c + w], ident[:], later, start=False, stop=True,
                                         skip_group_check=True)
                V.wait(T.mark(m), z_read.get(h - 2))
                sv = st[:, 8 * (h % 3):8 * (h % 3) + 8]
                V.wait(scaled.get(h - 3))
                V.mark(nc.vector.tensor_reduce(sv[:, 0:1], z[:, 0:P], AX.X, ALU.max, negate=True))
                V.mark(nc.vector.tensor_reduce(sv[:, 1:2], z[:, P:W], AX.X, ALU.max, negate=True))
                A.wait(V.last(), w_read.get(h - 3))
                A.mark(nc.scalar.activation(we[h % 3][:, 0:P], z[:, 0:P], ACT.Exp, bias=sv[:, 0:1],
                                            accum_out=sv[:, 2:3]))
                z_read[h] = A.mark(nc.scalar.activation(we[h % 3][:, P:W], z[:, P:W], ACT.Exp,
                                                        bias=sv[:, 1:2], accum_out=sv[:, 3:4]))

            def scale(h):
                w, sv = we[h % 3], st[:, 8 * (h % 3):8 * (h % 3) + 8]
                V.wait(z_read[h])
                V.mark(nc.vector.reciprocal(sv[:, 2:4], sv[:, 2:4]))
                V.mark(V.then().tensor_scalar(w[:, 0:P], w[:, 0:P], sv[:, 2:3], None, ALU.mult))
                scaled[h] = V.mark(nc.vector.tensor_scalar(w[:, P:W], w[:, P:W], sv[:, 3:4], None, ALU.mult))

            def turned(h):
                n = h % 2
                T.wait(scaled[h], wt_done.get(h - 2))
                wb = bank(2 + n)
                for c in (0, P, S):
                    m = nc.tensor.transpose(wb[:, c:c + P], we[h % 3][:, c:c + P], ident[:])
                w_read[h] = T.mark(m)
                A.wait(w_read[h], pv.get(h - 2))
                wt_done[h] = A.mark(nc.scalar.activation(wt[n], wb[:, 0:W], ACT.Copy))

            def values(h):
                n, pr = h % 2, h // 2
                if n == 0:
                    T.wait(o_read.get(pr - 2))
                pv[h] = attend_out(h, wt[n][:, 0:S], wt[n][:, S:W], vt, wt_done[h])
                if n:
                    o_read[pr] = split_pair(pr, pv[h])

            for step in range(HEADS + 2):
                if step < HEADS:
                    exps(step)
                if 1 <= step <= HEADS:
                    scale(step - 1)
                    turned(step - 1)
                if step >= 2:
                    values(step - 2)
            T.wait(o_read[HEADS // 2 - 1])

        def load_weights():
            sy = nc.sync
            q = a = 0
            first_w = [True, True]
            landed = {}

            def chunk(q_):
                s = None
                return s

            for turns, chunks, slots in segments:
                def turn(i):
                    step_q, step_a = chunks, len(slots)
                    units = list(enumerate(slots))
                    per = max(1, -(-len(units) // max(chunks, 1)))
                    for c in range(max(chunks, 1)):
                        if chunks:
                            qq = q + c if i is None else i * step_q + (q + c)
                            s = (q + c) % 2
                            if not (i is None and q + c < 2):
                                sy.wait_ge(w_lo_done, qq * 2 - 2)
                            src = p["w"][bass.ds(qq, 1), :, :] if i is not None else p["w"][qq:qq + 1, :, :]
                            sy.dma_start(stage[s][:], src.rearrange("a p n -> (a p) n")).then_inc(w_here[s], 16)
                        for u, s in units[c * per:(c + 1) * per]:
                            aa = a + u if i is None else i * step_a + (a + u)
                            sy.wait_ge(ada_sum, aa + 1)
                            src = p["ada"][bass.ds(aa, 1), :, :] if i is not None else p["ada"][aa:aa + 1, :, :]
                            sy.dma_start(ada[:, s, :], src.rearrange("a p n -> (a p) n")).then_inc(ada_here[s], 16)
                if turns > 1 and q < 2 and chunks:
                    assert (q, chunks) == (0, 2)
                    turn(None)
                    q += chunks
                    a += len(slots)
                    turns -= 1
                if turns == 1:
                    turn(None)
                elif turns:
                    with nc.sync.Fori(0, turns) as i:
                        turn(i)
                q += chunks * turns
                a += len(slots) * turns

        def finish(g=None):
            if g is not None:
                norm(g, None, split=False)
                A.wait(V.last())
                nc.scalar.dma_start(out, xa[:]).then_inc(s_out, 16)
            else:
                segments.append((1, 1, ()))
                A.wait(V.last())
                nc.scalar.dma_start(out, x[:]).then_inc(s_out, 16)
            nc.scalar.wait_ge(s_out, 16)
            load_weights()

        slots4, slots2 = (0, 1, 2, 3), (0, 1)
        segments.append((4, 0, slots4))
        with Loop(4) as i:
            ada_units(4, slots4, i)
            ada_sums(slots4, i)
            ada_cols(slots4, i)
        ada_advance(slots4, 4)
        nc.vector.wait_ge(s_par2, 16)
        nc.scalar.wait_ge(s_par2, 16)
        nc.scalar.wait_ge(s_x, 16)
        nc.vector.wait_ge(s_x, 16)
        mod_add(0, 16)
        A.wait(consts)
        T.wait(consts)
        V.wait(consts)
        gain_mod(par["norm_mix"][:, 0:KT], mod[:, 8:16])
        prep(0, 0)
        norm(gain, mod[:, 0:8])

        u, vt = carve(24 * S, NB * 512)
        u = u.rearrange("p (m t) -> p m t", m=24)
        vt = vt.rearrange("p (b n) -> p b n", b=NB)
        gemm(12, copy_evac(u), units=slots4, per={"A": 2})
        mod_add(16, 40)
        gemm(2, copy_evac_tm(vt), token_major=True, per={"A": 2})
        hgrn(u, vt)
        gemm(4, residual_evac(mod[:, 16:24]), per={"V": 4})
        gain_mod(par["norm_mlp"][:, 0:KT], mod[:, 32:40])
        norm(gain, mod[:, 24:32])

        def gate_mlp0():
            mod_add(40, 72)
            return mod[:, 40:48]
        mlp(gate_mlp0, slots4)
        if stop == "l0":
            return finish()

        gain_mod(par["norm_mix"][:, KT:2 * KT], mod[:, UNITS + 8:UNITS + 16])
        norm(gain, mod[:, UNITS:UNITS + 8])
        u, vt, work = carve(16 * S, NB * D, ARENA - 16 * S - NB * D)
        qk = u.rearrange("p (m t) -> p m t", m=16)
        vt = vt.rearrange("p (b n) -> p b n", b=NB)
        gemm(8, copy_evac(qk), units=slots4, per={"A": 2})
        gemm(4, copy_evac_tm(vt), token_major=True, units=slots4, per={"A": 2})
        mod_add(72, 96)
        stick_breaking(qk, vt, work)
        gemm(4, residual_evac(mod[:, UNITS + 16:UNITS + 24]), per={"V": 4})
        gain_mod(par["norm_mlp"][:, KT:2 * KT], mod[:, UNITS + 32:UNITS + 40])
        norm(gain, mod[:, UNITS + 24:UNITS + 32])
        mlp(lambda: mod[:, UNITS + 40:UNITS + 48])
        if stop == "l1":
            return finish()

        norm(par["mix_norm_2"][:, 0:KT], None)
        ssm()
        gemm(8, glu_evac([act_y[:, 0:S], act_y[:, S:2 * S]]), per={"V": 4, "A": 2})
        if stop == "m2":
            return finish()
        norm(par["mlp_norm_2"][:, 0:KT], None)
        mlp(lambda: None)
        if stop == "l2":
            return finish()

        norm(par["kv_norm_2"], None)
        u, vt, fox_f, work = carve(16 * S, NB * D, 1024, ARENA - 16 * S - NB * D - 1024)
        qk = u.rearrange("p (m t) -> p m t", m=16)
        vt = vt.rearrange("p (b n) -> p b n", b=NB)
        forget_gates(fox_f)
        gemm(4, copy_evac(qk[:, 8:16, :]), per={"A": 2})
        gemm(4, copy_evac_tm(vt), token_major=True, per={"A": 2})
        norm(par["mix_norm_2"][:, KT:2 * KT], None, same_x=True)
        gemm(4, copy_evac(qk[:, 0:8, :], HD ** -0.5), per={"A": 2})
        fox(qk, vt, work)
        gemm(4, residual_evac(None), per={"V": 4})
        norm(par["mlp_norm_2"][:, KT:2 * KT], None)
        mlp(lambda: None)
        finish(par["final_norm_2"])


def tiles(w):
    k, n = w.shape
    return w.reshape(k // P, P, n // CW, CW).transpose(2, 1, 0, 3).reshape(n // CW, P, -1)


def row_tiles(w):
    return w.reshape(-1, 2, P, D).transpose(0, 2, 1, 3).reshape(-1, P, 2 * D)


def mlp_tiles(w1, w2):
    a, b = tiles(w1), row_tiles(w2)
    mixed = np.stack([a[1:], b[:-1]], axis=1).reshape(-1, P, 2 * D)
    return [a[:1], mixed, b[-1:]]


def cols(v):
    v = np.asarray(v)
    return v.reshape(-1, P).T


def layout(i):
    g = {k: np.asarray(v) for k, v in i.items()}
    w_in = g["w_in_ab"][0]
    c5 = D // 2
    order = [w_in[:, n * c5:(n + 1) * c5] for n in (0, 1, 2, 3, 4, 6, 5)]
    qkv = g["w_qkv"][0]
    glu = g["ssm_w_glu_2"][0].reshape(D, 2, KT, P).transpose(0, 2, 1, 3).reshape(D, 2 * D)
    kvf = g["w_kvf_2"]
    parts = [tiles(np.concatenate(order, axis=1)), tiles(g["w_out_ab"][0])]
    parts += mlp_tiles(g["mlp_w1"][0], g["mlp_w2"][0])
    parts += [tiles(qkv), tiles(g["w_out_c"][0])]
    parts += mlp_tiles(g["mlp_w1"][1], g["mlp_w2"][1])
    parts += [tiles(glu)]
    parts += mlp_tiles(g["mlp_w1_2"][0], g["mlp_w2_2"][0])
    parts += [tiles(kvf[:, 0:2 * D]), tiles(g["attn_wq_2"][0]), tiles(g["attn_wo_2"][0])]
    parts += mlp_tiles(g["mlp_w1_2"][1], g["mlp_w2_2"][1])
    w = np.concatenate(parts)
    ada = g["ada_w"].reshape(2, KT, P, UNITS, P).transpose(0, 3, 2, 1, 4).reshape(2 * UNITS, P, D)
    x = g["x"][0].T.reshape(KT, P, S).transpose(1, 0, 2)
    both = lambda v: np.tile(v, 2)[:, None]
    pv = {"c": cols(g["c"]), "ada_b": cols(g["ada_b"]), "norm_mix": cols(g["norm_mix"]),
          "norm_mlp": cols(g["norm_mlp"]), "lb": cols(g["lb_logits"]), "hg_norm": cols(g["hg_norm"]),
          "conv_w": cols(g["conv_w"]), "q_norm": both(g["q_norm"][0]), "k_norm": both(g["k_norm"][0]),
          "mix_norm_2": cols(g["mix_norm_2"]), "mlp_norm_2": cols(g["mlp_norm_2"]),
          "kv_norm_2": cols(g["kv_norm_2"]), "final_norm_2": cols(g["final_norm_2"]),
          "ssm_d": cols(g["ssm_d_2"]), "b_f": np.tile(g["b_f_2"], P // HEADS)[:, None]}
    params = np.concatenate([pv[n] for n, _ in PARAM_COLS], axis=1)
    twice = lambda v: np.concatenate([v.T, v.T])
    ldt = np.broadcast_to(g["ssm_log_dt_2"][0], (P, GROUPS))
    b = [g["ssm_b_%s_2" % r][0].transpose(1, 0, 2).reshape(NSTATE, -1) for r in ("re", "im")]
    c = [g["ssm_c_%s_2" % r][0].transpose(2, 0, 1).reshape(NSTATE, -1) for r in ("re", "im")]
    ssm_in = np.concatenate([ldt, twice(g["ssm_a_re_2"][0]), twice(g["ssm_a_im_2"][0]),
                             np.concatenate(b), np.concatenate(b[::-1]),
                             np.concatenate(c), np.concatenate(c[::-1])], axis=1)
    w_f = kvf[:, 2 * D:].reshape(KT, P, HEADS).transpose(1, 0, 2)
    arrays = {"w": w, "ada": ada, "x": x, "params": params, "ssm_in": ssm_in, "w_f": w_f}
    return {"in_" + k: np.ascontiguousarray(v) for k, v in arrays.items()}


def kernel(**inputs):
    import concourse.bacc as bacc
    from concourse.bass_utils import run_bass_kernel_spmd

    nc = bacc.Bacc("TRN2", target_bir_lowering=False, num_devices=1)
    arrays = layout(inputs)
    p = {k[3:]: nc.dram_tensor(k, v.shape, F32, kind="ExternalInput").ap() for k, v in arrays.items()}
    out = nc.dram_tensor("out_0", (P, KT, S), F32, kind="ExternalOutput").ap()
    build(nc, p, out)
    r = run_bass_kernel_spmd(nc, [arrays], core_ids=[0])
    y = r.results[0]["out_0"]
    return np.ascontiguousarray(y.transpose(2, 1, 0).reshape(1, S, D))
```

```python
from contextlib import ExitStack

import numpy as np
import concourse.bass as bass
from concourse import mybir

F32 = mybir.dt.float32
F32R = mybir.dt.float32r
I32 = mybir.dt.int32
ALU = mybir.AluOpType
ACT = mybir.ActivationFunctionType
AX = mybir.AxisListType

P = 128
D = 1024
S = 256
KT = D // P
FF = 4 * D
CW = 2 * P
NB = S // P
EPS = 1e-6
UNITS = 6 * D // P
MLP_CHUNKS = FF // CW
HG_HEADS = 4
HEADS = 16
HD = D // HEADS
ARENA = 24576
GROUPS = 64
GC = 16
NSTATE = 64
TAPS = 8
NJ = S // TAPS
TWO_PI = 2.0 * np.pi
PI_A = 6.28125
PI_B = 0.001935303211212158
PI_C = TWO_PI - PI_A - PI_B
ROUND = 12582912.0


PARAM_COLS = [("c", KT), ("ada_b", 2 * UNITS), ("norm_mix", 2 * KT), ("norm_mlp", 2 * KT), ("lb", 12),
              ("hg_norm", 4), ("conv_w", 12), ("q_norm", 1), ("k_norm", 1), ("mix_norm_2", 2 * KT),
              ("mlp_norm_2", 2 * KT), ("kv_norm_2", KT), ("final_norm_2", KT), ("ssm_d", KT), ("b_f", 1)]
TOTAL = 14 + 4 + 32 + 12 + 4 + 32 + 8 + 32 + 8 + 4 + 4 + 32


class Mark:

    def __init__(self, lane, count, loop):
        self.lane, self.count, self.loop = lane, count, loop

    def value(self):
        if self.loop is None:
            return self.count
        i, per = self.loop
        return i * per + self.count


class Lane:

    def __init__(self, eng, sem):
        self.eng, self.sem, self.n, self.loop = eng, sem, 0, None

    def mark(self, ins):
        ins.then_inc(self.sem, 1)
        self.n += 1
        return Mark(self, self.n, self.loop)

    def wait(self, *marks):
        for m in marks:
            if m is not None:
                self.eng.wait_ge(m.lane.sem, m.value())

    def after(self):
        self.eng.wait_ge(self.sem, Mark(self, self.n, self.loop).value())

    def last(self):
        return Mark(self, self.n, self.loop)

    def then(self):
        self.after()
        return self.eng


def build(nc, p, out, stop=None):
    ctx = ExitStack()
    with ctx:
        def sb(name, shape, dt=F32):
            return ctx.enter_context(nc.sbuf_tensor(name, shape, dt))

        def sem(name):
            return ctx.enter_context(nc.semaphore(name))

        x = sb("x_res", [P, KT, S])
        xa = sb("x_scaled", [P, KT, S])
        hh = sb("act_hi", [P, KT, S], F32R)
        hl = sb("act_lo", [P, KT, S], F32R)
        stage = [sb(f"w_stage{s}", [P, 2048]) for s in range(2)]
        whi = [sb(f"w_hi{s}", [P, 2048], F32R) for s in range(2)]
        wlo = [sb(f"w_lo{s}", [P, 2048], F32R) for s in range(2)]
        ada = sb("ada_stage", [P, 4, KT * P])
        adacc = sb("ada_acc", [P, 4, P])
        mod = sb("mod", [P, 2 * UNITS])
        ident = sb("ident", [P, P])
        ones = sb("ones", [P, P])
        ones_h = sb("ones_h", [P, P])
        blk = sb("ones_blk", [P, P])
        eps = sb("eps", [P, 1])
        zero = sb("zero", [P, 1])
        one = sb("one", [P, 1])
        halfpi = sb("halfpi", [P, 1])
        jt = sb("rotate", [P, P])
        zr = sb("zero_r", [P, S], F32R)
        rstd = sb("rstd", [P, S])
        gain = sb("gain", [P, KT])
        small = sb("small", [P, 64])
        arena = sb("arena", [P, ARENA])
        PS = ctx.enter_context(nc.psum_tensor("PS", [P, 4096], F32))

        def bank(b, n=512, w=1):
            return PS[:, b * 512:b * 512 + n]

        V = Lane(nc.vector, sem("vector_done"))
        A = Lane(nc.scalar, sem("scalar_done"))
        T = Lane(nc.tensor, sem("tensor_done"))
        G = Lane(nc.gpsimd, sem("gpsimd_done"))
        lanes = [V, A, T, G]
        w_here = [sem(f"w_here{s}") for s in range(2)]
        w_hi_done = sem("w_hi_done")
        w_lo_done = sem("w_lo_done")
        w_used = sem("w_used")
        out_free = sem("out_free")
        ada_here = [sem(f"ada_here{s}") for s in range(4)]
        ada_mult = sem("ada_mult")
        ada_sum = sem("ada_sum")
        ada_col = sem("ada_col")
        s_par = sem("params_here")
        s_par2 = sem("params2_here")
        s_x = sem("x_here")
        s_dma = sem("ssm_params_here")
        s_shift = sem("taps_shifted")
        s_out = sem("out_written")

        class Loop:

            def __init__(self, count, **per):
                self.count, self.per = count, [per.get(k, 0) for k in "VATG"]

            def __enter__(self):
                self.cm = nc.Fori(0, self.count)
                i = self.cm.__enter__()
                self.n0 = [l.n for l in lanes]
                for l, q in zip(lanes, self.per):
                    l.loop = (i, q)
                return i

            def __exit__(self, *e):
                if e[0] is None:
                    got = [l.n - n for l, n in zip(lanes, self.n0)]
                    assert got == self.per, (got, self.per)
                for l, n, q in zip(lanes, self.n0, self.per):
                    l.loop = None
                    l.n = n + q * self.count
                return self.cm.__exit__(*e)

        par = {}
        off = 0
        PARS = [(n, w) for n, w in PARAM_COLS]
        ptile = sb("params", [P, sum(w for _, w in PARS)])
        for n, w in PARS:
            par[n] = ptile[:, off:off + w]
            off += w
        nc.sync.dma_start(par["c"], p["params"][:, 0:KT]).then_inc(s_par, 16)
        nc.scalar.dma_start(ptile[:, KT:], p["params"][:, KT:]).then_inc(s_par2, 16)
        nc.scalar.dma_start(x[:], p["x"]).then_inc(s_x, 16)
        G.mark(nc.gpsimd.memset(ident[:], 0.0))
        G.mark(G.then().memset(ones[:], 1.0 / D))
        G.mark(G.then().memset(ones_h[:], 1.0 / P))
        G.mark(G.then().memset(blk[:], 0.0))
        G.after()
        G.mark(G.then().memset(blk[0:64, 0:64], 1.0 / HD))
        G.mark(G.then().memset(blk[64:128, 64:128], 1.0 / HD))
        G.mark(G.then().affine_select(out=ident[:], in_=ident[:], compare_op=ALU.not_equal, fill=1.0,
                                       base=0, pattern=[[-1, P]], channel_multiplier=1))
        G.mark(G.then().memset(jt[:], 0.0))
        G.mark(G.then().affine_select(out=jt[:], in_=jt[:], compare_op=ALU.not_equal, fill=-1.0, base=-64,
                                      pattern=[[-1, P]], channel_multiplier=1))
        G.mark(G.then().affine_select(out=jt[:], in_=jt[:], compare_op=ALU.not_equal, fill=1.0, base=64,
                                      pattern=[[-1, P]], channel_multiplier=1))
        G.mark(G.then().memset(eps[:], EPS))
        G.mark(G.then().memset(zero[:], 0.0))
        G.mark(G.then().memset(one[:], 1.0))
        G.mark(G.then().memset(halfpi[:], float(np.pi / 2)))
        consts = G.mark(G.then().memset(zr[:].bitcast(F32), 0.0))
        masks = [arena[:, ARENA - 1024 + n * P:ARENA - 1024 + (n + 1) * P] for n in range(8)]
        G.mark(G.then().memset(arena[:, ARENA - 1024:ARENA], 0.0))
        for lev in range(7):
            c = 2 ** lev
            view = masks[lev].rearrange("p (n a c) -> p n a c", a=2, c=c)
            G.mark(G.then().memset(view[:, :, 1, :], 1.0))
        for lev in range(7):
            c = 2 ** lev
            n = P // (2 * c)
            view = masks[lev].rearrange("p (n r) -> p n r", n=n)
            G.mark(G.then().affine_select(out=view, in_=view, compare_op=ALU.is_ge, fill=0.0, base=0,
                                          pattern=[[-2 * c, n], [0, 2 * c]], channel_multiplier=1))
            G.mark(G.then().affine_select(out=view, in_=view, compare_op=ALU.is_ge, fill=0.0, base=c - 1,
                                          pattern=[[2 * c, n], [0, 2 * c]], channel_multiplier=-1))
        G.mark(G.then().tensor_copy(masks[7], ident[:]))
        nc.tensor.sem_inc(w_used, 2)
        nc.vector.sem_inc(out_free, 2)
        nc.vector.sem_inc(ada_sum, 4)
        nc.tensor.sem_inc(ada_col, 4)

        cact = small[:, 0:KT]
        nc.scalar.wait_ge(s_par, 16)
        silu_c = A.mark(nc.scalar.activation(small[:, 8:16], par["c"], ACT.Sigmoid))
        V.wait(silu_c)
        c_ready = V.mark(nc.vector.tensor_tensor(cact, small[:, 8:16], par["c"], ALU.mult))
        G.wait(c_ready)

        ada_slot = [0, 0, 0, 0]
        state = {"a": 0, "q": 0}
        segments = []

        def unit_index(slots, u, i):
            if i is None:
                return state["a"] + u
            if isinstance(i, tuple):
                return i[0] * 4 + (state["a"] + 2 * i[1] + u)
            return i * len(slots) + (state["a"] + u)

        def ada_units(n, slots, i=None):
            for u, s in enumerate(slots):
                r = i[0] if isinstance(i, tuple) else i
                land = ada_slot[s] + 1 if i is None else r + (ada_slot[s] + 1)
                t = ada[:, s, :].rearrange("p (k n) -> p k n", k=KT)
                nc.gpsimd.wait_ge(ada_here[s], land * 16)
                nc.gpsimd.tensor_tensor(t, t, cact.unsqueeze(2).to_broadcast([P, KT, P]),
                                        ALU.mult).then_inc(ada_mult, 1)

        def ada_sums(slots, i=None):
            for u, s in enumerate(slots):
                a = unit_index(slots, u, i)
                t = ada[:, s, :].rearrange("p (k n) -> p n k", k=KT)
                nc.vector.wait_ge(ada_mult, a + 1)
                nc.vector.wait_ge(ada_col, a + 1)
                nc.vector.tensor_reduce(adacc[:, s, :], t, AX.X, ALU.add).then_inc(ada_sum, 1)

        def ada_cols(slots, i=None):
            for u, s in enumerate(slots):
                a = unit_index(slots, u, i)
                nc.tensor.wait_ge(ada_sum, a + 5)
                nc.tensor.matmul(PS[:, bass.ds(a + 6 * 512, 1)] if i is not None
                                 else PS[:, 3072 + a:3073 + a],
                                 adacc[:, s, :], ones_f[:, 0:1], start=True, stop=True,
                                 skip_group_check=True).then_inc(ada_col, 1)

        def ada_advance(slots, turns=1):
            for s in slots:
                ada_slot[s] += turns
            state["a"] += len(slots) * turns

        ones_f = sb("ones_f", [P, 1])
        ones_ready = V.mark(nc.vector.memset(ones_f[:], 1.0))
        T.wait(ones_ready)

        def mod_add(a0, a1):
            nc.vector.wait_ge(ada_col, a1 + 4)
            return V.mark(nc.vector.tensor_tensor(mod[:, a0:a1], PS[:, 3072 + a0:3072 + a1],
                                                  par["ada_b"][:, a0:a1], ALU.add))

        def prep(q, s):
            nc.scalar.wait_ge(w_here[s], q * 8 + (16 - 8 * s))
            nc.scalar.wait_ge(w_used, q + 1)
            for h in range(2):
                c = slice(h * 1024, (h + 1) * 1024)
                nc.scalar.activation(whi[s][:, c], stage[s][:, c], ACT.Copy).then_inc(w_hi_done, 1)
                nc.vector.wait_ge(w_hi_done, q * 2 + (h + 1))
                nc.vector.tensor_tensor(wlo[s][:, c], stage[s][:, c], whi[s][:, c].bitcast(F32),
                                        ALU.subtract).then_inc(w_lo_done, 1)

        def half_ready(q, h):
            nc.tensor.wait_ge(w_lo_done, q * 2 + (h + 1))

        def up_products(q, s, o_of, token_major):
            wh = whi[s][:].rearrange("p (k n) -> p k n", k=KT)
            wl = wlo[s][:].rearrange("p (k n) -> p k n", k=KT)
            half_ready(q, 0)
            for t in range(2):
                o, c = o_of(t), slice(t * P, (t + 1) * P)
                for k in range(KT):
                    if t == 0 and k == KT // 2:
                        half_ready(q, 1)
                    for n, (w, a) in enumerate(((wh, hh), (wh, hl), (wl, hh))):
                        first, last = k == 0 and n == 0, k == KT - 1 and n == 2
                        if token_major:
                            m = nc.tensor.matmul(o, a[:, k, c], w[:, k, :], start=first, stop=last)
                        else:
                            m = nc.tensor.matmul(o, w[:, k, c], a[:, k, :], start=first, stop=last)
            m.then_inc(w_used, 1)

        def gemm_chunk(q, s, token_major):
            nc.tensor.wait_ge(out_free, q_out(q) + 1)
            up_products(q, s, lambda t: PS[:, s * 512 + t * S:s * 512 + (t + 1) * S], token_major)

        outs = {"n": 0}

        def q_out(q):
            return q - outs["n"]

        def gemm(n, evac, token_major=False, units=(), per=None, last=False):
            per = dict(per or {})
            segments.append((n // 2, 2, tuple(units)))
            q0 = state["q"]
            with Loop(n // 2, **per) as i:
                for s in range(2):
                    q = i * 2 + (q0 + s)
                    half = units[s * len(units) // 2:(s + 1) * len(units) // 2]
                    prep(q + 1, 1 - s)
                    gemm_chunk(q, s, token_major)
                    if s == 0 and units:
                        ada_units(len(units), units, i)
                        ada_sums(units, i)
                    if s == 1 and units:
                        ada_cols(units, i)
                    evac(i, s, q)
            if units:
                ada_advance(units, n // 2)
            state["q"] += n

        def product_ready(lane, q):
            lane.eng.wait_ge(w_used, q + 3)

        def norm(gain_of, shift_cols, same_x=False, split=True, squares=None):
            sq = squares if squares is not None else arena[:, 0:KT * S].rearrange("p (k t) -> p k t", k=KT)
            sums = PS[:, 7 * 512:7 * 512 + S]
            A.wait(V.last())
            A.wait(T.last())
            V.wait(A.last())
            if not same_x:
                for k in range(KT):
                    m = A.mark(nc.scalar.activation(sq[:, k, :], x[:, k, :], ACT.Square))
                    T.wait(m)
                    mm = nc.tensor.matmul(sums, ones[:], sq[:, k, :], start=k == 0, stop=k == KT - 1)
                summed = T.mark(mm)
            for k in range(KT):
                scaled = A.mark(nc.scalar.activation(xa[:, k, :], x[:, k, :], ACT.Copy,
                                                     scale=gain_of[:, k:k + 1]))
            if not same_x:
                A.wait(summed)
                root = A.mark(nc.scalar.activation(rstd[:, 0:S], sums, ACT.Sqrt, bias=eps[:]))
                V.wait(root)
                V.mark(nc.vector.reciprocal(rstd[:, 0:S], rstd[:, 0:S]))
                V.after()
            V.wait(scaled)
            prods = []
            for k in range(KT):
                prods.append(V.mark(nc.vector.tensor_tensor(xa[:, k, :], xa[:, k, :], rstd[:, 0:S], ALU.mult)))
            if not split:
                return
            for k in range(KT):
                sh = shift_cols[:, k:k + 1] if shift_cols is not None else zero[:]
                A.wait(prods[k])
                hi = A.mark(nc.scalar.activation(hh[:, k, :], xa[:, k, :], ACT.Identity, bias=sh))
                V.wait(hi)
                lo = V.mark(nc.vector.scalar_tensor_tensor(hl[:, k, :], xa[:, k, :], sh,
                                                           hh[:, k, :].bitcast(F32), ALU.add, ALU.subtract))
            T.wait(lo)

        def gain_mod(g, scale_cols):
            V.after()
            V.mark(nc.vector.scalar_tensor_tensor(gain[:], scale_cols, 1.0, g, ALU.add, ALU.mult))

        def split_act(src, k, waits):
            A.wait(waits)
            hi = A.mark(nc.scalar.activation(hh[:, k, :], src, ACT.Copy))
            V.wait(hi)
            return V.mark(nc.vector.tensor_tensor(hl[:, k, :], src, hh[:, k, :].bitcast(F32), ALU.subtract))

        def residual_evac(gate_cols):
            def evac(i, s, q):
                product_ready(V, q)
                for t in range(2):
                    tile = i * 4 + (2 * s + t)
                    xt = x[:, bass.ds(tile, 1), :].rearrange("p a t -> p (a t)")
                    src = PS[:, s * 512 + t * S:s * 512 + (t + 1) * S]
                    g = gate_cols[:, bass.ds(tile, 1)] if gate_cols is not None else one[:]
                    m = nc.vector.scalar_tensor_tensor(xt, src, g, xt, ALU.mult, ALU.add)
                    V.mark(m)
                V.after()
                nc.vector.sem_inc(out_free, 1)
            return evac

        f_parts = sb("forget_parts", [112, S], F32R)
        f_sel = sb("forget_select", [112, 32], F32R)
        act_a = sb("mlp_relu", [P, 2 * S])
        act_y = act_a
        ah = sb("mlp_hi", [P, 2 * S], F32R)
        al = sb("mlp_lo", [P, 2 * S], F32R)

        def mlp(gate_of, units=(), between=None, turns_before=0):
            q0 = state["q"]
            segments.append((1, 1, ()))
            segments.append((MLP_CHUNKS // 2 - 1, 4, tuple(units)))
            segments.append((1, 2, tuple(units[:2])))
            segments.append((1, 1, tuple(units[2:])))
            T.wait(V.last())
            for b in range(4):
                for t in range(2):
                    nc.tensor.matmul(PS[:, b * 512 + t * S:b * 512 + (t + 1) * S], zr[:, 0:P], zr[:],
                                     start=t == 0, stop=False, skip_group_check=True)

            def up(q, s):
                up_products(q, s, lambda t: PS[:, 2048 + t * S:2048 + (t + 1) * S], False)

            def hidden(q, waits):
                product_ready(A, q)
                A.wait(waits)
                V.wait(A.mark(nc.scalar.activation(act_a[:], bank(4), ACT.Relu)))
                V.mark(nc.vector.tensor_tensor(act_a[:], act_a[:], act_a[:], ALU.mult))

            def split_hidden(squared, q_before):
                A.wait(squared)
                product_ready(A, q_before)
                V.wait(A.mark(nc.scalar.activation(ah[:], act_a[:], ACT.Copy)))
                return V.mark(nc.vector.tensor_tensor(al[:], act_a[:], ah[:].bitcast(F32), ALU.subtract))

            def down(q, s, lo):
                wh = whi[s][:].rearrange("p (k n) -> p k n", k=2)
                wl = wlo[s][:].rearrange("p (k n) -> p k n", k=2)
                T.wait(lo)
                for kk in range(2):
                    half_ready(q, kk)
                    a_h, a_l = ah[:, kk * S:(kk + 1) * S], al[:, kk * S:(kk + 1) * S]
                    for n in range(KT):
                        c = slice(n * P, (n + 1) * P)
                        for w, a in ((wh, a_h), (wh, a_l), (wl, a_h)):
                            m = nc.tensor.matmul(PS[:, n * S:(n + 1) * S], w[:, kk, c], a, start=False,
                                                 stop=False, skip_group_check=True)
                m.then_inc(w_used, 1)

            def turn(q, i, last_al, slots):
                relu = A.last()
                lo = split_hidden(V.last(), q - 1)
                T.wait(relu)
                up(q, 1)
                prep(q + 1, 0)
                down(q + 1, 0, lo)
                if slots:
                    ada_units(len(slots), slots, i)
                hidden(q, lo)
                prep(q + 2, 1)
                if slots:
                    ada_sums(slots, i)
                    ada_cols(slots, i)

            prep(q0 + 1, 1)
            up(q0, 0)
            hidden(q0, None)
            both = (units[:2], units[2:])
            if between is not None:
                with Loop(turns_before, V=4, A=4) as i:
                    for n in range(2):
                        turn(i * 4 + (q0 + 1 + 2 * n), None, None, ())
                between()
            with Loop(MLP_CHUNKS // 2 - 1 - turns_before, V=4, A=4) as i:
                for n in range(2):
                    turn(i * 4 + (q0 + 4 * turns_before + 1 + 2 * n), (i, n) if units else i, None, both[n])
            if units:
                ada_advance(units, MLP_CHUNKS // 2 - 1)
            q = q0 + 2 * MLP_CHUNKS - 3
            turn(q, None, None, both[0])
            if units:
                ada_advance(both[0])
            q += 2
            lo = split_hidden(V.last(), q - 1)
            if units:
                ada_units(2, both[1])
                ada_sums(both[1])
            if q + 1 < TOTAL:
                prep(q + 1, 0)
            down(q, 1, lo)
            if units:
                ada_cols(both[1])
                ada_advance(both[1])
            state["q"] += 2 * MLP_CHUNKS
            outs["n"] += 2 * MLP_CHUNKS
            product_ready(V, q)
            g = gate_of()
            V.after()
            for n in range(KT):
                V.mark(nc.vector.scalar_tensor_tensor(x[:, n, :], PS[:, n * S:(n + 1) * S],
                                                      g[:, n:n + 1] if g is not None else one[:],
                                                      x[:, n, :], ALU.mult, ALU.add))
            V.after()

        def copy_evac(dst, scale=1.0):
            def evac(i, s, q):
                product_ready(A, q)
                o = dst[:, bass.ds(i * 4 + 2 * s, 2), :]
                A.mark(nc.scalar.activation(o, bank(s).rearrange("p (a t) -> p a t", a=2), ACT.Copy,
                                            scale=scale))
                A.after()
                nc.scalar.sem_inc(out_free, 1)
            return evac

        def copy_evac_tm(dst):
            def evac(i, s, q):
                product_ready(A, q)
                o = dst[:, :, bass.ds(i * 2 * CW + s * CW, CW)]
                A.mark(nc.scalar.activation(o, bank(s).rearrange("p (a t) -> p a t", a=2), ACT.Copy))
                A.after()
                nc.scalar.sem_inc(out_free, 1)
            return evac

        def carve(*sizes):
            o, got = 0, []
            for n in sizes:
                got.append(arena[:, o:o + n])
                o += n
            assert o <= ARENA, o
            return got

        def hgrn(u, vt):
            ab, ac, acth, hq, hf, hg = (u[:, 4 * n:4 * n + 4, :] for n in range(6))
            o = 24 * S + NB * 512
            pre, suf, ql, kl, kk, sc0, sc1, y, t1 = [arena[:, o + n * 1024:o + (n + 1) * 1024] for n in range(9)]
            heads = lambda t: t.rearrange("p (h t) -> p h t", h=HG_HEADS)
            A.wait(V.last())
            V.wait(A.last())
            sig = A.mark(nc.scalar.activation(hf, hf, ACT.Sigmoid))
            sig_g = A.mark(nc.scalar.activation(heads(y), hg, ACT.Sigmoid))
            lg = par["lb"]
            lb, oml, tmp, ex = small[:, 16:20], small[:, 20:24], small[:, 24:28], small[:, 28:40]
            V.mark(nc.vector.tensor_tensor(tmp, lg[:, 0:4], lg[:, 4:8], ALU.max))
            V.mark(V.then().tensor_tensor(tmp, tmp, lg[:, 8:12], ALU.max))
            for r in range(3):
                V.mark(V.then().tensor_tensor(ex[:, 4 * r:4 * r + 4], lg[:, 4 * r:4 * r + 4], tmp, ALU.subtract))
            A.wait(V.last())
            V.wait(A.mark(nc.scalar.activation(ex, ex, ACT.Exp)))
            V.mark(nc.vector.tensor_tensor(tmp, ex[:, 0:4], ex[:, 4:8], ALU.add))
            V.mark(V.then().tensor_tensor(tmp, tmp, ex[:, 8:12], ALU.add))
            V.mark(V.then().reciprocal(tmp, tmp))
            V.mark(V.then().tensor_tensor(lb, ex[:, 0:4], tmp, ALU.mult))
            V.mark(V.then().tensor_scalar(oml, lb, -1.0, 1.0, ALU.mult, ALU.add))
            V.wait(sig)
            V.after()
            for h in range(HG_HEADS):
                V.mark(nc.vector.tensor_scalar(heads(pre)[:, h, :], hf[:, h, :], oml[:, h:h + 1],
                                               lb[:, h:h + 1], ALU.mult, ALU.add))
            V.mark(V.then().tensor_scalar(kk, pre, -1.0, 1.0, ALU.mult, ALU.add))
            V.mark(nc.vector.memset(suf, 1.0))
            V.mark(nc.vector.memset(ql, 0.0))
            V.mark(nc.vector.memset(kl, 0.0))
            V.mark(nc.vector.memset(sc0, 0.0))
            V.mark(nc.vector.memset(sc1[:, 0:512], 0.0))
            sc0h = sc0.rearrange("p (h t) -> p h t", h=HG_HEADS)
            sc1h = sc1[:, 0:512].rearrange("p (h t) -> p h t", h=HG_HEADS)

            def block_scores(key, query, mask, waits):
                T.wait(waits)
                for b in range(NB):
                    for h in range(HG_HEADS):
                        cols = slice(h * S + b * P, h * S + (b + 1) * P)
                        m = nc.tensor.matmul(PS[:, (2 + b) * 512 + h * P:(2 + b) * 512 + (h + 1) * P],
                                             key[:, cols], query[:, cols], start=True, stop=True)
                V.wait(T.mark(m))
                for b, dst in ((0, sc0h[:, :, 0:P]), (1, sc1h)):
                    V.mark(V.then().copy_predicated(
                        dst, mask.bitcast(I32).unsqueeze(1).to_broadcast([P, HG_HEADS, P]),
                        bank(2 + b).rearrange("p (h t) -> p h t", h=HG_HEADS)))

            hqf = u[:, 12:16, :].rearrange("p h t -> p (h t)")
            block_scores(kk, hqf, masks[7], V.last())
            c = 1
            for lev in range(8):
                seg = lambda t: t.rearrange("p (n a c) -> p n a c", a=2, c=c)
                n = HG_HEADS * S // (2 * c)
                V.after()
                left_total = seg(pre)[:, :, 0, c - 1:c].to_broadcast([P, n, c])
                right_total = seg(pre)[:, :, 1, c - 1:c].to_broadcast([P, n, c])
                V.mark(nc.vector.tensor_tensor(seg(ql)[:, :, 1, :], seg(hqf)[:, :, 1, :],
                                               seg(pre)[:, :, 1, :], ALU.mult))
                V.mark(nc.vector.tensor_tensor(seg(kl)[:, :, 0, :], seg(kk)[:, :, 0, :],
                                               seg(suf)[:, :, 0, :], ALU.mult))
                scaled = V.last()
                if lev < 7:
                    V.mark(V.then().tensor_tensor(seg(suf)[:, :, 0, :], seg(suf)[:, :, 0, :], right_total,
                                                  ALU.mult))
                    V.mark(V.then().tensor_tensor(seg(pre)[:, :, 1, :], seg(pre)[:, :, 1, :], left_total,
                                                  ALU.mult))
                    block_scores(kl, ql, masks[lev], scaled)
                else:
                    T.wait(scaled)
                    for h in range(HG_HEADS):
                        m = nc.tensor.matmul(PS[:, 1024 + h * P:1024 + (h + 1) * P], kl[:, h * S:h * S + P],
                                             ql[:, h * S + P:(h + 1) * S], start=True, stop=True)
                    V.wait(T.mark(m))
                    V.mark(V.then().tensor_copy(sc0h[:, :, P:S], bank(2).rearrange("p (h t) -> p h t", h=HG_HEADS)))
                c *= 2
            T.wait(V.last())
            for h in range(HG_HEADS):
                o_h = PS[:, 2048 + h * S:2048 + (h + 1) * S]
                nc.tensor.matmul(o_h, vt[:, 0, h * P:(h + 1) * P], sc0h[:, h, :], start=True, stop=False,
                                 skip_group_check=True)
                m = nc.tensor.matmul(o_h[:, P:S], vt[:, 1, h * P:(h + 1) * P], sc1h[:, h, :], start=False,
                                     stop=True, skip_group_check=True)
            o_done = T.mark(m)
            A.wait(o_done)
            sq = A.mark(nc.scalar.activation(ql, PS[:, 2048:3072], ACT.Square))
            T.wait(sq)
            for b in range(2):
                m = nc.tensor.matmul(bank(2 + b), ones_h[:], ql[:, b * 512:(b + 1) * 512], start=True, stop=True)
            A.wait(T.mark(m))
            V.wait(A.mark(nc.scalar.activation(kl, PS[:, 1024:2048], ACT.Sqrt, bias=eps[:])))
            V.wait(sig_g)
            V.mark(V.then().reciprocal(kl, kl))
            V.mark(nc.vector.tensor_tensor(heads(y), heads(y), hg, ALU.mult))
            for h in range(HG_HEADS):
                V.after()
                V.mark(nc.vector.scalar_tensor_tensor(heads(t1)[:, h, :], PS[:, 2048 + h * S:2048 + (h + 1) * S],
                                                      par["hg_norm"][:, h:h + 1], heads(kl)[:, h, :],
                                                      ALU.mult, ALU.mult))
            V.mark(V.then().tensor_tensor(y, y, t1, ALU.mult))
            for h in range(HG_HEADS):
                split_act(heads(y)[:, h, :], 4 + h, V.last())
            cw = par["conv_w"]
            p_, cv = ql, kl
            V.mark(nc.vector.tensor_tensor(heads(p_), ac, acth, ALU.mult))
            for m_ in range(4):
                V.mark(V.then().tensor_scalar(heads(cv)[:, m_, :], heads(p_)[:, m_, :], cw[:, 8 + m_:9 + m_],
                                              None, ALU.mult))
            for tap, sh in ((1, 1), (0, 2)):
                for m_ in range(4):
                    d = heads(cv)[:, m_, sh:S]
                    V.after()
                    V.mark(nc.vector.scalar_tensor_tensor(d, heads(p_)[:, m_, 0:S - sh],
                                                          cw[:, 4 * tap + m_:4 * tap + m_ + 1], d,
                                                          ALU.mult, ALU.add))
            V.mark(V.then().tensor_tensor(heads(cv), heads(cv), ab, ALU.mult))
            for m_ in range(4):
                lo = split_act(heads(cv)[:, m_, :], m_, V.last())
            T.wait(lo)

        def attend_out(h, w_s0, w_s1, vt, waits):
            po, pr = HD * (h % 2), h // 2
            o = PS[po:po + HD, (6 + pr % 2) * 512:(6 + pr % 2) * 512 + S]
            T.wait(waits)
            nc.tensor.matmul(o, vt[:, 0, h * HD:(h + 1) * HD], w_s0, start=True, stop=False,
                             skip_group_check=True)
            return T.mark(nc.tensor.matmul(o[:, P:S], vt[:, 1, h * HD:(h + 1) * HD], w_s1, start=False,
                                           stop=True, skip_group_check=True))

        def split_pair(pr, waits):
            return split_act(PS[:, (6 + pr % 2) * 512:(6 + pr % 2) * 512 + S], pr, waits)

        def scores(h, qk, b_of, waits, stop=True):
            po, pr = HD * (h % 2), h // 2
            T.wait(*waits)
            z = bank(b_of)
            nc.tensor.matmul(z[:, 0:P], qk[po:po + HD, pr, 0:P], qk[po:po + HD, 8 + pr, 0:P], start=True,
                             stop=stop, skip_group_check=True)
            return nc.tensor.matmul(z[:, P:P + S], qk[po:po + HD, pr, P:S], qk[po:po + HD, 8 + pr, :],
                                    start=True, stop=stop, skip_group_check=True)

        def stick_breaking(qk, vt, work, side):
            A.wait(V.last())
            V.wait(A.last())
            T.wait(A.last())
            sq2 = [work[:, 0:512], work[:, 512:1024]]
            rs2 = [work[:, 1024:1536], work[:, 1536:2048]]
            used = [None, None]
            freed = [None, None]
            for n in range(8):
                src = qk[:, 2 * n:2 * n + 2, :].rearrange("p m t -> p (m t)")
                A.wait(used[n % 2])
                T.wait(A.mark(nc.scalar.activation(sq2[n % 2], src, ACT.Square)))
                m = T.mark(nc.tensor.matmul(bank(2 + n % 2), blk[:], sq2[n % 2], start=True, stop=True))
                used[n % 2] = m
                A.wait(m, freed[n % 2])
                V.wait(A.mark(nc.scalar.activation(rs2[n % 2], bank(2 + n % 2), ACT.Sqrt, bias=eps[:])))
                V.mark(nc.vector.reciprocal(rs2[n % 2], rs2[n % 2]))
                g = par["q_norm"] if n < 4 else par["k_norm"]
                freed[n % 2] = V.mark(V.then().scalar_tensor_tensor(src, src, g, rs2[n % 2], ALU.mult, ALU.mult))
            A.wait(V.last())
            W = P + S
            bt = [work[:, n * W:(n + 1) * W] for n in (0, 1)]
            om = [work[:, n * W:(n + 1) * W] for n in (2, 3)]
            o = 4 * W
            pr_ = [work[:, o + n * (W + 2):o + (n + 1) * (W + 2)] for n in (0, 1)]
            o += 2 * (W + 2)
            wt = [work[:, o + n * W:o + (n + 1) * W] for n in (0, 1)]
            o += 2 * W
            late, keep = work[:, o:o + S], work[:, o + S:o + S + W]
            V.mark(V.then().memset(late[:, 0:P], 0.0))
            V.mark(nc.vector.memset(late[:, P:S], 1.0))
            V.mark(nc.vector.memset(keep, 1.0))
            G.wait(V.last())
            G.mark(G.then().affine_select(out=late[:, P:S], in_=late[:, P:S], compare_op=ALU.is_ge, fill=0.0,
                                           base=0, pattern=[[1, P]], channel_multiplier=-1))
            for c in (0, S):
                G.mark(G.then().affine_select(out=keep[:, c:c + P], in_=keep[:, c:c + P], compare_op=ALU.is_ge,
                                               fill=0.0, base=-1, pattern=[[1, P]], channel_multiplier=-1))
            for n in (0, 1):
                V.mark(nc.vector.memset(pr_[n][:, P:P + 1], 1.0))
                V.mark(nc.vector.memset(pr_[n][:, W + 1:W + 2], 1.0))
            V.wait(G.last())
            T.wait(V.last())
            z_read, w_done, w_read, wt_done, pv, o_read = {}, {}, {}, {}, {}, {}

            def weights(h):
                n = h % 2
                zz = T.mark(scores(h, qk, n, (z_read.get(h - 2),)))
                A.wait(zz, w_read.get(h - 2))
                A.mark(nc.scalar.activation(bt[n], bank(n)[:, 0:W], ACT.Sigmoid, scale=HD ** -0.5))
                z_read[h] = A.mark(nc.scalar.activation(om[n], bank(n)[:, 0:W], ACT.Sigmoid,
                                                        scale=-HD ** -0.5))
                V.wait(z_read[h])
                q = pr_[n]
                V.mark(nc.vector.tensor_tensor_scan(q[:, 0:P][:, ::-1], om[n][:, 0:P][:, ::-1],
                                                    late[:, P:S][:, ::-1], 1.0, ALU.mult, ALU.max))
                V.mark(nc.vector.tensor_tensor_scan(q[:, P + 1:W + 1][:, ::-1], om[n][:, P:W][:, ::-1],
                                                    late[:, ::-1], 1.0, ALU.mult, ALU.max))
                V.mark(V.then().tensor_tensor(bt[n][:, 0:P], bt[n][:, 0:P], q[:, 1:P + 1], ALU.mult))
                w_done[h] = V.mark(nc.vector.tensor_tensor(bt[n][:, P:W], bt[n][:, P:W],
                                                           q[:, P + 2:W + 2], ALU.mult))

            def turned(h):
                n = h % 2
                T.wait(w_done[h], wt_done.get(h - 2))
                wb = bank(2 + n)
                for c in (0, P, S):
                    m = nc.tensor.transpose(wb[:, c:c + P], bt[n][:, c:c + P], ident[:])
                w_read[h] = T.mark(m)
                V.wait(w_read[h], pv.get(h - 2))
                wt_done[h] = V.mark(nc.vector.tensor_tensor(wt[n], wb[:, 0:W], keep, ALU.mult))

            def values(h):
                n, pr = h % 2, h // 2
                if n == 0:
                    T.wait(o_read.get(pr - 2))
                pv[h] = attend_out(h, wt[n][:, 0:S], wt[n][:, S:W], vt, wt_done[h])
                if n:
                    o_read[pr] = split_pair(pr, pv[h])

            for step in range(HEADS + 2):
                if step < HEADS:
                    weights(step)
                if step in side:
                    side[step]()
                if 1 <= step <= HEADS:
                    turned(step - 1)
                if step >= 2:
                    values(step - 2)
            T.wait(o_read[HEADS // 2 - 1])

        def glu_evac(sg):
            def evac(i, s, q):
                product_ready(A, q)
                A.wait(V.last())
                V.wait(A.mark(nc.scalar.activation(sg[s], PS[:, s * 512 + S:s * 512 + 2 * S], ACT.Sigmoid)))
                V.mark(nc.vector.tensor_tensor(sg[s], PS[:, s * 512:s * 512 + S], sg[s], ALU.mult))
                xt = x[:, bass.ds(i * 2 + s, 1), :].rearrange("p a t -> p (a t)")
                V.mark(V.then().tensor_tensor(xt, xt, sg[s], ALU.add))
                V.after()
                nc.vector.sem_inc(out_free, 1)
            return evac

        wide = lambda t: t.unsqueeze(2).to_broadcast([P, GROUPS, GC])
        gc = lambda t: t.rearrange("p (g c) -> p g c", g=GROUPS)
        gic = lambda t: t.rearrange("p (g i c) -> p g i c", g=GROUPS, i=TAPS)
        to_out, toep, to_state = [arena[:, n * 8192:(n + 1) * 8192] for n in range(3)]
        bs, bsw, cs, csw, b_bar, jb_bar = [arena[:, 10240 + n * 1024:11264 + n * 1024] for n in range(6)]
        adaf = ada[:].rearrange("p s n -> p (s n)")
        small_of = lambda n: adaf[:, n * 64:(n + 1) * 64]
        powr = [small_of(n) for n in range(13)]
        powi = [small_of(n) for n in range(13, 26)]
        ldt, are, aim = [small_of(n) for n in range(26, 29)]
        dt, er, th, rn, co, si, den, wr, wi, nr, tt, tu = [small_of(n) for n in range(29, 41)]
        prod = adaf[:, 3072:4096]
        taps = prod
        sgn, nsgn = small[:, 40:41], small[:, 41:42]
        act_squares = adaf[:, 2048:4096].rearrange("p (k t) -> p k t", k=KT)
        ssm_marks = {}

        def gtt(o, a, b, op, after=True):
            return G.mark((G.then() if after else nc.gpsimd).tensor_tensor(o, a, b, op))

        def ssm_load():
            w0 = GROUPS * 3
            A.wait(V.last())
            nc.scalar.dma_start(adaf[:, 26 * 64:29 * 64], p["ssm_in"][:, 0:w0]).then_inc(s_dma, 16)
            nc.scalar.dma_start(arena[:, 10240:14336], p["ssm_in"][:, w0:w0 + 4096]).then_inc(s_dma, 16)

        def ssm_steps():
            nc.scalar.wait_ge(s_dma, 32)
            ssm_marks["dt"] = A.mark(nc.scalar.activation(dt, ldt, ACT.Exp))

        def ssm_angles():
            nc.vector.wait_ge(s_dma, 32)
            V.wait(ssm_marks["dt"])
            V.mark(nc.vector.memset(small[0:64, 40:41], -1.0))
            V.mark(nc.vector.memset(small[64:128, 40:41], 1.0))
            V.mark(nc.vector.memset(small[0:64, 41:42], 1.0))
            V.mark(nc.vector.memset(small[64:128, 41:42], -1.0))
            V.mark(nc.vector.tensor_tensor(den, are, are, ALU.mult))
            V.mark(nc.vector.tensor_tensor(tt, aim, aim, ALU.mult))
            V.mark(nc.vector.tensor_tensor(er, are, dt, ALU.mult))
            V.mark(nc.vector.tensor_tensor(th, aim, dt, ALU.mult))
            V.mark(V.then().tensor_tensor(den, den, tt, ALU.add))
            V.mark(nc.vector.tensor_scalar(rn, th, 1.0 / TWO_PI, ROUND, ALU.mult, ALU.add))
            V.mark(V.then().tensor_scalar(rn, rn, -ROUND, None, ALU.add))
            V.mark(nc.vector.reciprocal(den, den))
            for part in (PI_A, PI_B, PI_C):
                V.mark(V.then().scalar_tensor_tensor(th, rn, -part, th, ALU.mult, ALU.add))
            ssm_marks["angle"] = V.mark(V.then().tensor_scalar(th, th, -3.1415925, 3.1415925, ALU.max, ALU.min))

        def ssm_rotations():
            A.wait(ssm_marks["angle"])
            A.mark(nc.scalar.activation(er, er, ACT.Exp))
            A.mark(nc.scalar.activation(si, th, ACT.Sin))
            A.mark(nc.scalar.activation(co, th, ACT.Abs))
            ssm_marks["rotation"] = A.mark(A.then().activation(co, co, ACT.Sin, scale=-1.0, bias=halfpi[:]))

        def ssm_inputs_to_states():
            G.wait(ssm_marks["rotation"])
            nc.gpsimd.wait_ge(s_dma, 32)
            lr, li = powr[1], powi[1]
            gtt(lr, er, co, ALU.mult)
            gtt(li, er, si, ALU.mult, False)
            G.mark(nc.gpsimd.memset(powr[0], 1.0))
            G.mark(nc.gpsimd.memset(powi[0], 0.0))

            def cmul(o_r, o_i, a_r, a_i, b_r, b_i):
                gtt(tt, a_i, b_i, ALU.mult)
                gtt(tu, a_i, b_r, ALU.mult, False)
                gtt(o_r, a_r, b_r, ALU.mult, False)
                gtt(o_i, a_r, b_i, ALU.mult, False)
                gtt(o_r, o_r, tt, ALU.subtract)
                gtt(o_i, o_i, tu, ALU.add, False)

            for k in range(2, 9):
                cmul(powr[k], powi[k], powr[k // 2], powi[k // 2], powr[k - k // 2], powi[k - k // 2])
            for k in range(9, 12):
                cmul(powr[k], powi[k], powr[k - 1], powi[k - 1], powr[k - 1], powi[k - 1])
            G.mark(G.then().tensor_scalar(nr, lr, -1.0, None, ALU.add))
            gtt(wr, nr, are, ALU.mult)
            gtt(tt, li, aim, ALU.mult, False)
            gtt(wi, li, are, ALU.mult, False)
            gtt(tu, nr, aim, ALU.mult, False)
            gtt(wr, wr, tt, ALU.add)
            gtt(wi, wi, tu, ALU.subtract, False)
            gtt(wr, wr, den, ALU.mult)
            gtt(wi, wi, den, ALU.mult, False)
            G.mark(nc.gpsimd.tensor_scalar(bsw, bsw, sgn, None, ALU.mult))
            G.mark(nc.gpsimd.tensor_scalar(cs, cs, nsgn, None, ALU.mult))
            gtt(gc(b_bar), gc(bs), wide(wr), ALU.mult)
            gtt(gc(prod), gc(bsw), wide(wi), ALU.mult, False)
            gtt(b_bar, b_bar, prod, ALU.add)
            gtt(gc(jb_bar), gc(bsw), wide(wr), ALU.mult, False)
            gtt(gc(prod), gc(bs), wide(wi), ALU.mult)
            gtt(jb_bar, jb_bar, prod, ALU.subtract)
            for i in range(TAPS):
                gtt(gc(prod), gc(jb_bar), wide(powi[7 - i]), ALU.mult)
                gtt(gic(to_state)[:, :, i, :], gc(b_bar), wide(powr[7 - i]), ALU.mult, False)
                ssm_marks["to_state"] = gtt(gic(to_state)[:, :, i, :], gic(to_state)[:, :, i, :], gc(prod), ALU.add)

        def ssm_states_to_outputs():
            G.wait(T.last(), V.last())
            for i in range(TAPS):
                gtt(gc(prod), gc(csw), wide(powi[i + 1]), ALU.mult)
                gtt(gic(to_out)[:, :, i, :], gc(cs), wide(powr[i + 1]), ALU.mult, False)
                ssm_marks["to_out"] = gtt(gic(to_out)[:, :, i, :], gic(to_out)[:, :, i, :], gc(prod), ALU.subtract)

        def ssm_taps():
            T.wait(ssm_marks["to_state"])
            for g in range(GROUPS):
                m = nc.tensor.matmul(PS[:, 2560 + g * GC:2560 + (g + 1) * GC], to_state[:, g * P:(g + 1) * P],
                                     cs[:, g * GC:(g + 1) * GC], start=True, stop=True)
            A.wait(T.mark(m), ssm_marks["to_out"])
            ssm_marks["taps"] = A.mark(nc.scalar.activation(taps, PS[:, 2560:3584], ACT.Copy))
            read = {5: ssm_marks["taps"], 6: ssm_marks["taps"], 7: None}
            for n in range(GROUPS // 4):
                b = (7, 5, 6)[n % 3]
                cols = slice(n * 512, (n + 1) * 512)
                T.wait(read[b])
                for g in range(4):
                    m = nc.tensor.transpose(PS[:, b * 512 + g * P:b * 512 + (g + 1) * P],
                                            to_state[:, (4 * n + g) * P:(4 * n + g + 1) * P], ident[:])
                m = T.mark(m)
                if n % 2:
                    V.wait(m)
                    read[b] = V.mark(nc.vector.tensor_copy(to_state[:, cols], bank(b)))
                else:
                    A.wait(m)
                    read[b] = A.mark(nc.scalar.activation(to_state[:, cols], bank(b), ACT.Copy))

        def ssm_toeplitz():
            G.wait(ssm_marks["taps"])
            G.mark(G.then().memset(toep, 0.0))
            G.mark(G.then().tensor_copy(gic(toep)[:, :, TAPS - 1, :], gc(taps)))
            xf = xa[:].rearrange("p k t -> p (k t)")
            moved = [xf[:, 0:1024], xf[:, 1024:2048], adaf[:, 2048:3072]]
            count = 0
            for blocks in ((0, 1, 2), (3, 4, 5), (6,)):
                G.after()
                for n, i in enumerate(blocks):
                    rows = (i + 1) * GC
                    nc.gpsimd.dma_start(moved[n][0:rows, :], taps[P - rows:P, :]).then_inc(s_shift, 16)
                    count += 16
                nc.gpsimd.wait_ge(s_shift, count)
                for n, i in enumerate(blocks):
                    rows = (i + 1) * GC
                    G.mark(nc.gpsimd.tensor_copy(gic(toep)[0:rows, :, i, :], gc(moved[n])[0:rows]))

        def ssm():
            uc = adaf[:, 2048:4096]
            xs = to_state[:, 0:2048]
            t_ = to_state[:, 2048:4096]
            ident32 = ident[0:NJ, 0:NJ]
            T.wait(V.last(), G.last())
            A.wait(V.last())
            V.wait(T.last(), A.last())
            half = [act_a[0:NJ, :], adacc[0:NJ].rearrange("p s n -> p (s n)")]
            turned, read1, read2 = {}, {}, {}

            def tokens_out(kt):
                b = 2 * (kt % 2)
                T.wait(read1.get(kt - 2))
                for i in range(TAPS):
                    src = xa[:, kt, :].rearrange("p (j i) -> p i j", i=TAPS)[:, i, :]
                    m = nc.tensor.transpose(PS[0:NJ, b * 512 + i * P:b * 512 + (i + 1) * P], src, ident[:])
                return T.mark(m)

            def groups_in(kt, out_done):
                b = 4 + kt % 2
                v = PS[0:NJ, kt % 2 * 1024:kt % 2 * 1024 + 1024].rearrange("p (i g c) -> p i g c", i=TAPS, g=8)
                V.wait(out_done)
                for n in range(2):
                    V.wait(turned.get((kt - 1, n)))
                    read1[kt] = V.mark(nc.vector.tensor_copy(
                        half[n].rearrange("p (g i c) -> p i g c", g=4, i=TAPS), v[:, :, 4 * n:4 * n + 4, :]))
                    T.wait(read1[kt], read2.get(kt - 2))
                    for g in range(4):
                        o = b * 512 + (4 * n + g) * NJ
                        m = nc.tensor.transpose(PS[:, o:o + NJ], half[n][:, g * P:(g + 1) * P], ident32)
                    turned[kt, n] = T.mark(m)
                A.wait(turned[kt, 1])
                read2[kt] = A.mark(nc.scalar.activation(uc[:, kt * 256:(kt + 1) * 256],
                                                        PS[:, b * 512:b * 512 + 256], ACT.Copy))

            out_done = tokens_out(0)
            for kt in range(KT):
                ready = out_done
                if kt + 1 < KT:
                    out_done = tokens_out(kt + 1)
                groups_in(kt, ready)
            T.wait(A.last())
            T.wait(V.last())
            state_read = []
            for b in range(4):
                for g in range(16 * b, 16 * b + 16):
                    m = nc.tensor.matmul(PS[:, g * NJ:(g + 1) * NJ], to_state[:, g * P:(g + 1) * P],
                                         uc[:, g * NJ:(g + 1) * NJ], start=True, stop=True)
                added = T.mark(m)
            for g in range(GROUPS):
                m = nc.tensor.matmul(PS[:, 2048 + g * NJ:2048 + (g + 1) * NJ], toep[:, g * P:(g + 1) * P],
                                     uc[:, g * NJ:(g + 1) * NJ], start=g % 16 == 0, stop=False,
                                     skip_group_check=True)
            own = T.mark(m)
            V.wait(added)
            A.wait(added)
            V.mark(nc.vector.tensor_copy(xs[:, 0:1024], PS[:, 0:1024]))
            A.mark(nc.scalar.activation(xs[:, 1024:2048], PS[:, 1024:2048], ACT.Copy))
            xj = xs.rearrange("p (g j) -> p g j", g=GROUPS)
            tj = t_.rearrange("p (g j) -> p g j", g=GROUPS)
            steps = [(d, 2 ** d - 1, 2 ** (d + 1), NJ // 2 ** (d + 1) - (d == 3)) for d in range(4)]
            steps += [(d, 2 ** (d + 1) - 1, 2 ** (d + 1), NJ // 2 ** (d + 1) - 1) for d in (3, 2, 1, 0)]
            T.wait(A.last())
            V.wait(A.last())
            for d, first, gap, n in steps:
                at = lambda t, o: t[:, :, o:o + gap * (n - 1) + 1:gap]
                src, dst, tmp = at(xj, first), at(xj, first + 2 ** d), tj[:, :, 0:n]
                pr_, pi_ = [w[8 + d].unsqueeze(2).to_broadcast([P, GROUPS, n]) for w in (powr, powi)]
                T.wait(V.last())
                m = None
                step_g = min(GROUPS, 512 // n)
                while GROUPS % step_g:
                    step_g -= 1
                jn = []
                for b, g in enumerate(range(0, GROUPS, step_g)):
                    o = PS[:, b * 512:b * 512 + step_g * n]
                    m = nc.tensor.matmul(o.rearrange("p (g j) -> p g j", j=n), jt[:], src[:, g:g + step_g, :],
                                         start=True, stop=True)
                    jn.append((o, g))
                turned_all = T.mark(m)
                V.mark(V.then().tensor_tensor(tmp, src, pr_, ALU.mult))
                V.mark(V.then().tensor_tensor(dst, dst, tmp, ALU.add))
                V.wait(turned_all)
                V.after()
                for o, g in jn:
                    V.mark(nc.vector.tensor_tensor(tmp[:, g:g + step_g, :], o.rearrange("p (g j) -> p g j", j=n),
                                                   pi_[:, g:g + step_g, :], ALU.mult))
                V.mark(V.then().tensor_tensor(dst, dst, tmp, ALU.add))
            T.wait(V.last())
            ys = to_state[:, 4096:6144]
            y_here = []
            for b in range(4):
                for g in range(16 * b, 16 * b + 16):
                    m = nc.tensor.matmul(PS[:, 2048 + g * NJ + 1:2048 + (g + 1) * NJ], to_out[:, g * P:(g + 1) * P],
                                         xj[:, g, 0:NJ - 1], start=False, stop=True, skip_group_check=True)
                m = T.mark(m)
                c = slice(b * 512, (b + 1) * 512)
                A.wait(m)
                y_here.append(A.mark(nc.scalar.activation(ys[:, c], bank(4 + b), ACT.Copy)))
            yt = [act_y[:, 0:S], act_y[:, S:2 * S]]
            vbuf = [to_state[0:NJ, 0:1024], to_state[0:NJ, 1024:2048]]
            split, turned, read1, added = {}, {}, {}, {}
            V.wait(T.last())

            def chunks_out(kt):
                b = 2 * (kt % 2)
                T.wait(y_here[kt // 2], read1.get(kt - 2))
                for g in range(8):
                    m = nc.tensor.transpose(PS[0:NJ, b * 512 + g * P:b * 512 + (g + 1) * P],
                                            ys[:, (kt * 8 + g) * NJ:(kt * 8 + g + 1) * NJ], ident[:])
                V.wait(T.mark(m), turned.get(kt - 2))
                read1[kt] = V.mark(nc.vector.tensor_copy(
                    vbuf[kt % 2].rearrange("p (i g c) -> p g i c", g=8, i=TAPS),
                    PS[0:NJ, b * 512:b * 512 + 1024].rearrange("p (g i c) -> p g i c", i=TAPS, g=8)))

            def features_in(kt):
                b = 4 + kt % 2
                T.wait(read1[kt], added.get(kt - 2), y_here[3])
                o = b * 512
                for i in range(TAPS):
                    m = nc.tensor.transpose(PS[:, o + i * NJ:o + (i + 1) * NJ],
                                            vbuf[kt % 2][:, i * P:(i + 1) * P], ident32)
                turned[kt] = T.mark(m)
                V.wait(turned[kt], split.get(kt - 2))
                yk = yt[kt % 2]
                added[kt] = V.mark(nc.vector.scalar_tensor_tensor(
                    yk.rearrange("p (j i) -> p j i", i=TAPS), xa[:, kt, :].rearrange("p (j i) -> p j i", i=TAPS),
                    par["ssm_d"][:, kt:kt + 1], PS[:, o:o + S].rearrange("p (i j) -> p j i", i=TAPS),
                    ALU.mult, ALU.add))
                A.wait(added[kt])
                A.mark(nc.scalar.activation(yk, yk, ACT.Gelu_apprx_tanh))

            for kt in range(KT + 1):
                if kt < KT:
                    chunks_out(kt)
                if kt:
                    features_in(kt - 1)
                    split[kt - 1] = split_act(yt[(kt - 1) % 2], kt - 1, A.last())
            T.wait(V.last())

        def forget_gates(fw):
            z, a, cum = fw[0:16, 0:S], fw[0:16, S:2 * S], fw[0:16, 2 * S:3 * S]
            A.wait(A.last(), V.last())
            T.wait(V.last())
            wf = fw[:, 3 * S:3 * S + KT * 16].rearrange("p (k h) -> p k h", k=KT)
            nc.scalar.dma_start(wf, p["w_f"]).then_inc(s_par, 16)
            nc.tensor.wait_ge(s_par, 32)
            f = PS[0:16, 3584:3584 + S]
            for k in range(KT):
                m = nc.tensor.matmul(f, wf[:, k, :], xa[:, k, :], start=k == 0, stop=k == KT - 1)
            A.wait(T.mark(m))
            A.mark(nc.scalar.activation(z, f, ACT.Identity, bias=par["b_f"][0:16, :]))
            A.mark(A.then().activation(a, z, ACT.Abs))
            A.mark(A.then().activation(a, a, ACT.Exp, scale=-1.0))
            V.wait(A.mark(A.then().activation(a, a, ACT.Ln, bias=one[0:16, :])))
            V.mark(nc.vector.scalar_tensor_tensor(z, z, 0.0, a, ALU.min, ALU.subtract))
            V.mark(V.then().memset(a, 1.0))
            V.mark(V.then().tensor_tensor_scan(cum, a, z, 0.0, ALU.mult, ALU.add))
            V.mark(nc.vector.memset(f_parts[:].bitcast(F32), 0.0))
            for r in (0, 64):
                V.mark(V.then().tensor_copy(f_parts[r:r + 16, :], cum))
            V.mark(V.then().tensor_tensor(a, cum, f_parts[0:16, :].bitcast(F32), ALU.subtract))
            A.wait(V.last())
            for r in (32, 96):
                A.mark(nc.scalar.activation(f_parts[r:r + 16, :], a, ACT.Copy))
            V.mark(V.then().memset(f_sel[:].bitcast(F32), 0.0))
            for r in (0, 32, 64, 96):
                V.mark(V.then().tensor_copy(f_sel[r:r + 16, 0:16], ident[0:16, 0:16]))
                V.mark(nc.vector.tensor_scalar(f_sel[r:r + 16, 16:32], ident[0:16, 0:16], -1.0, None, ALU.mult))

        def fox(qk, vt, work):
            W = P + S
            we = [work[:, n * W:(n + 1) * W] for n in range(3)]
            wt = [work[:, n * W:(n + 1) * W] for n in (3, 4)]
            o = 5 * W
            later, st = work[:, o:o + P], work[:, o + P:o + P + 32]
            A.wait(V.last())
            V.wait(A.last())
            T.wait(A.last())
            V.mark(nc.vector.memset(later, -1e30))
            G.wait(V.last())
            T.wait(G.mark(G.then().affine_select(out=later, in_=later, compare_op=ALU.is_ge, fill=0.0, base=-1,
                                                 pattern=[[1, P]], channel_multiplier=-1)))
            T.wait(V.last())
            z_read, scaled, w_read, wt_done, pv, o_read = {}, {}, {}, {}, {}, {}

            def exps(h):
                n, po, pr = h % 2, HD * (h % 2), h // 2
                T.wait(z_read.get(h - 2))
                z = bank(n)
                for c, w, b in ((0, P, 0), (P, S, 1)):
                    zb = z[:, c:c + w]
                    nc.tensor.matmul(zb, qk[po:po + HD, pr, b * P:(b + 1) * P], qk[po:po + HD, 8 + pr, 0:w],
                                     start=True, stop=False, skip_group_check=True)
                    nc.tensor.matmul(zb, f_parts[po:po + 48, b * P:(b + 1) * P],
                                     f_sel[po:po + 48, h:h + 1].to_broadcast([48, w]),
                                     start=False, stop=False, skip_group_check=True)
                    nc.tensor.matmul(zb, f_sel[po:po + 48, 16 + h:17 + h].to_broadcast([48, P]),
                                     f_parts[po:po + 48, 0:w],
                                     start=False, stop=False, skip_group_check=True)
                    m = nc.tensor.matmul(z[:, c + w - P:c + w], ident[:], later, start=False, stop=True,
                                         skip_group_check=True)
                V.wait(T.mark(m), z_read.get(h - 2))
                sv = st[:, 8 * (h % 3):8 * (h % 3) + 8]
                V.wait(scaled.get(h - 3))
                V.mark(nc.vector.tensor_reduce(sv[:, 0:1], z[:, 0:P], AX.X, ALU.max, negate=True))
                V.mark(nc.vector.tensor_reduce(sv[:, 1:2], z[:, P:W], AX.X, ALU.max, negate=True))
                A.wait(V.last(), w_read.get(h - 3))
                A.mark(nc.scalar.activation(we[h % 3][:, 0:P], z[:, 0:P], ACT.Exp, bias=sv[:, 0:1],
                                            accum_out=sv[:, 2:3]))
                z_read[h] = A.mark(nc.scalar.activation(we[h % 3][:, P:W], z[:, P:W], ACT.Exp,
                                                        bias=sv[:, 1:2], accum_out=sv[:, 3:4]))

            def scale(h):
                w, sv = we[h % 3], st[:, 8 * (h % 3):8 * (h % 3) + 8]
                V.wait(z_read[h])
                V.mark(nc.vector.reciprocal(sv[:, 2:4], sv[:, 2:4]))
                V.mark(V.then().tensor_scalar(w[:, 0:P], w[:, 0:P], sv[:, 2:3], None, ALU.mult))
                scaled[h] = V.mark(nc.vector.tensor_scalar(w[:, P:W], w[:, P:W], sv[:, 3:4], None, ALU.mult))

            def turned(h):
                n = h % 2
                T.wait(scaled[h], wt_done.get(h - 2))
                wb = bank(2 + n)
                for c in (0, P, S):
                    m = nc.tensor.transpose(wb[:, c:c + P], we[h % 3][:, c:c + P], ident[:])
                w_read[h] = T.mark(m)
                A.wait(w_read[h], pv.get(h - 2))
                wt_done[h] = A.mark(nc.scalar.activation(wt[n], wb[:, 0:W], ACT.Copy))

            def values(h):
                n, pr = h % 2, h // 2
                if n == 0:
                    T.wait(o_read.get(pr - 2))
                pv[h] = attend_out(h, wt[n][:, 0:S], wt[n][:, S:W], vt, wt_done[h])
                if n:
                    o_read[pr] = split_pair(pr, pv[h])

            for step in range(HEADS + 2):
                if step < HEADS:
                    exps(step)
                if 1 <= step <= HEADS:
                    scale(step - 1)
                    turned(step - 1)
                if step >= 2:
                    values(step - 2)
            T.wait(o_read[HEADS // 2 - 1])

        def load_weights():
            sy = nc.sync
            q = a = 0
            first_w = [True, True]
            landed = {}

            def chunk(q_):
                s = None
                return s

            for turns, chunks, slots in segments:
                def turn(i):
                    step_q, step_a = chunks, len(slots)
                    units = list(enumerate(slots))
                    per = max(1, -(-len(units) // max(chunks, 1)))
                    for c in range(max(chunks, 1)):
                        if chunks:
                            qq = q + c if i is None else i * step_q + (q + c)
                            s = (q + c) % 2
                            if not (i is None and q + c < 2):
                                sy.wait_ge(w_lo_done, qq * 2 - 2)
                            src = p["w"][bass.ds(qq, 1), :, :] if i is not None else p["w"][qq:qq + 1, :, :]
                            sy.dma_start(stage[s][:], src.rearrange("a p n -> (a p) n")).then_inc(w_here[s], 16)
                        for u, s in units[c * per:(c + 1) * per]:
                            aa = a + u if i is None else i * step_a + (a + u)
                            sy.wait_ge(ada_sum, aa + 1)
                            src = p["ada"][bass.ds(aa, 1), :, :] if i is not None else p["ada"][aa:aa + 1, :, :]
                            sy.dma_start(ada[:, s, :], src.rearrange("a p n -> (a p) n")).then_inc(ada_here[s], 16)
                if turns > 1 and q < 2 and chunks:
                    assert (q, chunks) == (0, 2)
                    turn(None)
                    q += chunks
                    a += len(slots)
                    turns -= 1
                if turns == 1:
                    turn(None)
                elif turns:
                    with nc.sync.Fori(0, turns) as i:
                        turn(i)
                q += chunks * turns
                a += len(slots) * turns

        def finish(g=None):
            if g is not None:
                norm(g, None, split=False)
                A.wait(V.last())
                nc.scalar.dma_start(out, xa[:]).then_inc(s_out, 16)
            else:
                segments.append((1, 1, ()))
                A.wait(V.last())
                nc.scalar.dma_start(out, x[:]).then_inc(s_out, 16)
            nc.scalar.wait_ge(s_out, 16)
            load_weights()

        slots4, slots2 = (0, 1, 2, 3), (0, 1)
        segments.append((4, 0, slots4))
        with Loop(4) as i:
            ada_units(4, slots4, i)
            ada_sums(slots4, i)
            ada_cols(slots4, i)
        ada_advance(slots4, 4)
        nc.vector.wait_ge(s_par2, 16)
        nc.scalar.wait_ge(s_par2, 16)
        nc.scalar.wait_ge(s_x, 16)
        nc.vector.wait_ge(s_x, 16)
        mod_add(0, 16)
        A.wait(consts)
        T.wait(consts)
        V.wait(consts)
        gain_mod(par["norm_mix"][:, 0:KT], mod[:, 8:16])
        prep(0, 0)
        norm(gain, mod[:, 0:8])

        u, vt = carve(24 * S, NB * 512)
        u = u.rearrange("p (m t) -> p m t", m=24)
        vt = vt.rearrange("p (b n) -> p b n", b=NB)
        gemm(12, copy_evac(u), units=slots4, per={"A": 2})
        mod_add(16, 40)
        gemm(2, copy_evac_tm(vt), token_major=True, per={"A": 2})
        hgrn(u, vt)
        gemm(4, residual_evac(mod[:, 16:24]), per={"V": 4})
        gain_mod(par["norm_mlp"][:, 0:KT], mod[:, 32:40])
        norm(gain, mod[:, 24:32])

        def gate_mlp0():
            mod_add(40, 72)
            return mod[:, 40:48]
        mlp(gate_mlp0, slots4)
        if stop == "l0":
            return finish()

        gain_mod(par["norm_mix"][:, KT:2 * KT], mod[:, UNITS + 8:UNITS + 16])
        norm(gain, mod[:, UNITS:UNITS + 8])
        u, vt, work = carve(16 * S, NB * D, ARENA - 16 * S - NB * D)
        qk = u.rearrange("p (m t) -> p m t", m=16)
        vt = vt.rearrange("p (b n) -> p b n", b=NB)
        gemm(8, copy_evac(qk), units=slots4, per={"A": 2})
        gemm(4, copy_evac_tm(vt), token_major=True, units=slots4, per={"A": 2})
        mod_add(72, 96)
        ssm_load()
        stick_breaking(qk, vt, work, {2: ssm_steps, 5: ssm_angles, 8: ssm_rotations})
        ssm_inputs_to_states()
        gemm(4, residual_evac(mod[:, UNITS + 16:UNITS + 24]), per={"V": 4})
        gain_mod(par["norm_mlp"][:, KT:2 * KT], mod[:, UNITS + 32:UNITS + 40])
        norm(gain, mod[:, UNITS + 24:UNITS + 32])
        ssm_states_to_outputs()
        mlp(lambda: mod[:, UNITS + 40:UNITS + 48], between=ssm_taps, turns_before=4)
        ssm_toeplitz()
        if stop == "l1":
            return finish()

        A.wait(G.last())
        norm(par["mix_norm_2"][:, 0:KT], None, split=False,
             squares=act_squares)
        ssm()
        gemm(8, glu_evac([act_y[:, 0:S], act_y[:, S:2 * S]]), per={"V": 4, "A": 2})
        if stop == "m2":
            return finish()
        norm(par["mlp_norm_2"][:, 0:KT], None)
        mlp(lambda: None)
        if stop == "l2":
            return finish()

        norm(par["kv_norm_2"], None)
        u, vt, fox_f, work = carve(16 * S, NB * D, 1024, ARENA - 16 * S - NB * D - 1024)
        qk = u.rearrange("p (m t) -> p m t", m=16)
        vt = vt.rearrange("p (b n) -> p b n", b=NB)
        forget_gates(fox_f)
        gemm(4, copy_evac(qk[:, 8:16, :]), per={"A": 2})
        gemm(4, copy_evac_tm(vt), token_major=True, per={"A": 2})
        norm(par["mix_norm_2"][:, KT:2 * KT], None, same_x=True)
        gemm(4, copy_evac(qk[:, 0:8, :], HD ** -0.5), per={"A": 2})
        fox(qk, vt, work)
        gemm(4, residual_evac(None), per={"V": 4})
        norm(par["mlp_norm_2"][:, KT:2 * KT], None)
        mlp(lambda: None)
        finish(par["final_norm_2"])


def tiles(w):
    k, n = w.shape
    return w.reshape(k // P, P, n // CW, CW).transpose(2, 1, 0, 3).reshape(n // CW, P, -1)


def row_tiles(w):
    return w.reshape(-1, 2, P, D).transpose(0, 2, 1, 3).reshape(-1, P, 2 * D)


def mlp_tiles(w1, w2):
    a, b = tiles(w1), row_tiles(w2)
    mixed = np.stack([a[1:], b[:-1]], axis=1).reshape(-1, P, 2 * D)
    return [a[:1], mixed, b[-1:]]


def cols(v):
    v = np.asarray(v)
    return v.reshape(-1, P).T


def layout(i):
    g = {k: np.asarray(v) for k, v in i.items()}
    w_in = g["w_in_ab"][0]
    c5 = D // 2
    order = [w_in[:, n * c5:(n + 1) * c5] for n in (0, 1, 2, 3, 4, 6, 5)]
    qkv = g["w_qkv"][0]
    glu = g["ssm_w_glu_2"][0].reshape(D, 2, KT, P).transpose(0, 2, 1, 3).reshape(D, 2 * D)
    kvf = g["w_kvf_2"]
    parts = [tiles(np.concatenate(order, axis=1)), tiles(g["w_out_ab"][0])]
    parts += mlp_tiles(g["mlp_w1"][0], g["mlp_w2"][0])
    parts += [tiles(qkv), tiles(g["w_out_c"][0])]
    parts += mlp_tiles(g["mlp_w1"][1], g["mlp_w2"][1])
    parts += [tiles(glu)]
    parts += mlp_tiles(g["mlp_w1_2"][0], g["mlp_w2_2"][0])
    parts += [tiles(kvf[:, 0:2 * D]), tiles(g["attn_wq_2"][0]), tiles(g["attn_wo_2"][0])]
    parts += mlp_tiles(g["mlp_w1_2"][1], g["mlp_w2_2"][1])
    w = np.concatenate(parts)
    ada = g["ada_w"].reshape(2, KT, P, UNITS, P).transpose(0, 3, 2, 1, 4).reshape(2 * UNITS, P, D)
    x = g["x"][0].T.reshape(KT, P, S).transpose(1, 0, 2)
    both = lambda v: np.tile(v, 2)[:, None]
    pv = {"c": cols(g["c"]), "ada_b": cols(g["ada_b"]), "norm_mix": cols(g["norm_mix"]),
          "norm_mlp": cols(g["norm_mlp"]), "lb": cols(g["lb_logits"]), "hg_norm": cols(g["hg_norm"]),
          "conv_w": cols(g["conv_w"]), "q_norm": both(g["q_norm"][0]), "k_norm": both(g["k_norm"][0]),
          "mix_norm_2": cols(g["mix_norm_2"]), "mlp_norm_2": cols(g["mlp_norm_2"]),
          "kv_norm_2": cols(g["kv_norm_2"]), "final_norm_2": cols(g["final_norm_2"]),
          "ssm_d": cols(g["ssm_d_2"]), "b_f": np.tile(g["b_f_2"], P // HEADS)[:, None]}
    params = np.concatenate([pv[n] for n, _ in PARAM_COLS], axis=1)
    twice = lambda v: np.concatenate([v.T, v.T])
    ldt = np.broadcast_to(g["ssm_log_dt_2"][0], (P, GROUPS))
    b = [g["ssm_b_%s_2" % r][0].transpose(1, 0, 2).reshape(NSTATE, -1) for r in ("re", "im")]
    c = [g["ssm_c_%s_2" % r][0].transpose(2, 0, 1).reshape(NSTATE, -1) for r in ("re", "im")]
    ssm_in = np.concatenate([ldt, twice(g["ssm_a_re_2"][0]), twice(g["ssm_a_im_2"][0]),
                             np.concatenate(b), np.concatenate(b[::-1]),
                             np.concatenate(c), np.concatenate(c[::-1])], axis=1)
    w_f = kvf[:, 2 * D:].reshape(KT, P, HEADS).transpose(1, 0, 2)
    arrays = {"w": w, "ada": ada, "x": x, "params": params, "ssm_in": ssm_in, "w_f": w_f}
    return {"in_" + k: np.ascontiguousarray(v) for k, v in arrays.items()}


def kernel(**inputs):
    import concourse.bacc as bacc
    from concourse.bass_utils import run_bass_kernel_spmd

    nc = bacc.Bacc("TRN2", target_bir_lowering=False, num_devices=1)
    arrays = layout(inputs)
    p = {k[3:]: nc.dram_tensor(k, v.shape, F32, kind="ExternalInput").ap() for k, v in arrays.items()}
    out = nc.dram_tensor("out_0", (P, KT, S), F32, kind="ExternalOutput").ap()
    build(nc, p, out)
    r = run_bass_kernel_spmd(nc, [arrays], core_ids=[0])
    y = r.results[0]["out_0"]
    return np.ascontiguousarray(y.transpose(2, 1, 0).reshape(1, S, D))
```

```python
from contextlib import ExitStack

import numpy as np
import concourse.bass as bass
from concourse import mybir

F32 = mybir.dt.float32
F32R = mybir.dt.float32r
I32 = mybir.dt.int32
ALU = mybir.AluOpType
ACT = mybir.ActivationFunctionType
AX = mybir.AxisListType

P = 128
D = 1024
S = 256
KT = D // P
FF = 4 * D
CW = 2 * P
NB = S // P
EPS = 1e-6
UNITS = 6 * D // P
START_UNITS = 2 * KT
MLP_CHUNKS = FF // CW
HG_HEADS = 4
HEADS = 16
HD = D // HEADS
ARENA = 24576
GROUPS = 64
GC = 16
NSTATE = 64
TAPS = 8
NJ = S // TAPS
TWO_PI = 2.0 * np.pi
PI_A = 6.28125
PI_B = 0.001935303211212158
PI_C = TWO_PI - PI_A - PI_B
ROUND = 12582912.0


PARAM_COLS = [("c", KT), ("ada_b", 2 * UNITS), ("norm_mix", 2 * KT), ("norm_mlp", 2 * KT), ("lb", 12),
              ("hg_norm", 4), ("conv_w", 12), ("q_norm", 1), ("k_norm", 1), ("mix_norm_2", 2 * KT),
              ("mlp_norm_2", 2 * KT), ("kv_norm_2", KT), ("final_norm_2", KT), ("ssm_d", KT), ("b_f", 1)]
TOTAL = 14 + 4 + 32 + 12 + 4 + 32 + 8 + 32 + 8 + 4 + 4 + 32


class Mark:

    def __init__(self, lane, count, loop):
        self.lane, self.count, self.loop = lane, count, loop

    def value(self):
        if self.loop is None:
            return self.count
        i, per = self.loop
        return i * per + self.count


class Lane:

    def __init__(self, eng, sem):
        self.eng, self.sem, self.n, self.loop = eng, sem, 0, None

    def mark(self, ins):
        ins.then_inc(self.sem, 1)
        self.n += 1
        return Mark(self, self.n, self.loop)

    def wait(self, *marks):
        for m in marks:
            if m is not None:
                self.eng.wait_ge(m.lane.sem, m.value())

    def after(self):
        self.eng.wait_ge(self.sem, Mark(self, self.n, self.loop).value())

    def last(self):
        return Mark(self, self.n, self.loop)

    def then(self):
        self.after()
        return self.eng


def build(nc, p, out):
    ctx = ExitStack()
    with ctx:
        def sb(name, shape, dt=F32):
            return ctx.enter_context(nc.sbuf_tensor(name, shape, dt))

        def sem(name):
            return ctx.enter_context(nc.semaphore(name))

        x = sb("x_res", [P, KT, S])
        xa = sb("x_scaled", [P, KT, S])
        hh = sb("act_hi", [P, KT, S], F32R)
        hl = sb("act_lo", [P, KT, S], F32R)
        stage = [sb(f"w_stage{s}", [P, 2048]) for s in range(2)]
        whi = [sb(f"w_hi{s}", [P, 2048], F32R) for s in range(2)]
        wlo = [sb(f"w_lo{s}", [P, 2048], F32R) for s in range(2)]
        ada = sb("ada_stage", [P, 4, KT * P])
        adacc = sb("ada_acc", [P, 4, P])
        mod = sb("mod", [P, 2 * UNITS])
        ident = sb("ident", [P, P])
        ones = sb("ones", [P, P])
        ones_h = sb("ones_h", [P, P])
        blk = sb("ones_blk", [P, P])
        eps = sb("eps", [P, 1])
        zero = sb("zero", [P, 1])
        one = sb("one", [P, 1])
        halfpi = sb("halfpi", [P, 1])
        jt = sb("rotate", [P, P])
        zr = sb("zero_r", [P, S], F32R)
        rstd = sb("rstd", [P, S])
        gain = sb("gain", [P, KT])
        small = sb("small", [P, 64])
        arena = sb("arena", [P, ARENA])
        PS = ctx.enter_context(nc.psum_tensor("PS", [P, 4096], F32))

        def bank(b, n=512, w=1):
            return PS[:, b * 512:b * 512 + n]

        V = Lane(nc.vector, sem("vector_done"))
        A = Lane(nc.scalar, sem("scalar_done"))
        T = Lane(nc.tensor, sem("tensor_done"))
        G = Lane(nc.gpsimd, sem("gpsimd_done"))
        lanes = [V, A, T, G]
        w_here = [sem(f"w_here{s}") for s in range(2)]
        w_hi_done = sem("w_hi_done")
        w_lo_done = sem("w_lo_done")
        w_used = sem("w_used")
        out_free = sem("out_free")
        ada_here = [sem(f"ada_here{s}") for s in range(4)]
        ada_mult = sem("ada_mult")
        start_sum = sem("start_sum")
        ada_sum = sem("ada_sum")
        ada_col = sem("ada_col")
        s_par = sem("params_here")
        s_par2 = sem("params2_here")
        s_x = sem("x_here")
        s_dma = sem("ssm_params_here")
        s_shift = sem("taps_shifted")
        s_out = sem("out_written")

        class Loop:

            def __init__(self, count, gpsimd=False, **per):
                self.count, self.per = count, [per.get(k, 0) for k in "VATG"]
                e = mybir.EngineType
                self.engines = (e.DVE, e.Activation, e.PE) + ((e.Pool,) if gpsimd else ())

            def __enter__(self):
                self.cm = nc.Fori(0, self.count, engines=self.engines)
                i = self.cm.__enter__()
                self.n0 = [l.n for l in lanes]
                for l, q in zip(lanes, self.per):
                    l.loop = (i, q)
                return i

            def __exit__(self, *e):
                if e[0] is None:
                    got = [l.n - n for l, n in zip(lanes, self.n0)]
                    assert got == self.per, (got, self.per)
                for l, n, q in zip(lanes, self.n0, self.per):
                    l.loop = None
                    l.n = n + q * self.count
                return self.cm.__exit__(*e)

        par = {}
        off = 0
        PARS = [(n, w) for n, w in PARAM_COLS]
        ptile = sb("params", [P, sum(w for _, w in PARS)])
        for n, w in PARS:
            par[n] = ptile[:, off:off + w]
            off += w
        nc.sync.dma_start(par["c"], p["params"][:, 0:KT]).then_inc(s_par, 16)
        nc.scalar.dma_start(ptile[:, KT:], p["params"][:, KT:]).then_inc(s_par2, 16)
        nc.scalar.dma_start(x[:], p["x"]).then_inc(s_x, 16)
        G.mark(nc.gpsimd.memset(ident[:], 0.0))
        G.mark(G.then().memset(ones[:], 1.0 / D))
        G.mark(G.then().memset(ones_h[:], 1.0 / P))
        G.mark(G.then().memset(blk[:], 0.0))
        G.after()
        G.mark(G.then().memset(blk[0:64, 0:64], 1.0 / HD))
        G.mark(G.then().memset(blk[64:128, 64:128], 1.0 / HD))
        G.mark(G.then().affine_select(out=ident[:], in_=ident[:], compare_op=ALU.not_equal, fill=1.0,
                                       base=0, pattern=[[-1, P]], channel_multiplier=1))
        G.mark(G.then().memset(jt[:], 0.0))
        G.mark(G.then().affine_select(out=jt[:], in_=jt[:], compare_op=ALU.not_equal, fill=-1.0, base=-64,
                                      pattern=[[-1, P]], channel_multiplier=1))
        G.mark(G.then().affine_select(out=jt[:], in_=jt[:], compare_op=ALU.not_equal, fill=1.0, base=64,
                                      pattern=[[-1, P]], channel_multiplier=1))
        G.mark(G.then().memset(eps[:], EPS))
        G.mark(G.then().memset(zero[:], 0.0))
        G.mark(G.then().memset(one[:], 1.0))
        G.mark(G.then().memset(halfpi[:], float(np.pi / 2)))
        consts = G.mark(G.then().memset(zr[:].bitcast(F32), 0.0))
        nc.tensor.sem_inc(w_used, 2)
        nc.vector.sem_inc(out_free, 2)
        nc.vector.sem_inc(start_sum, 4)
        nc.gpsimd.sem_inc(ada_sum, START_UNITS + 4)
        nc.tensor.sem_inc(ada_col, 4)

        cact = small[:, 0:KT]
        nc.scalar.wait_ge(s_par, 16)
        silu_c = A.mark(nc.scalar.activation(small[:, 8:16], par["c"], ACT.Sigmoid))
        V.wait(silu_c)
        c_ready = V.mark(nc.vector.tensor_tensor(cact, small[:, 8:16], par["c"], ALU.mult))
        G.wait(c_ready)

        ada_slot = [0, 0, 0, 0]
        state = {"a": 0, "q": 0, "ahead": 0}
        segments = []

        def unit_index(slots, u, i):
            if i is None:
                return state["a"] + u
            if isinstance(i, tuple):
                return i[0] * 4 + (state["a"] + 2 * i[1] + u)
            return i * len(slots) + (state["a"] + u)

        def ada_units(slots, i=None, sums=True):
            for u, s in enumerate(slots):
                a = unit_index(slots, u, i)
                r = i[0] if isinstance(i, tuple) else i
                land = ada_slot[s] + 1 if i is None else r + (ada_slot[s] + 1)
                t = ada[:, s, :].rearrange("p (k n) -> p k n", k=KT)
                nc.gpsimd.wait_ge(ada_here[s], land * 16)
                nc.gpsimd.tensor_tensor(t, t, cact.unsqueeze(2).to_broadcast([P, KT, P]),
                                        ALU.mult).then_inc(ada_mult, 1 if sums else 4)
                if sums:
                    for step, n in ((1, 4), (2, 2)):
                        nc.gpsimd.wait_ge(ada_mult, a * 3 + step)
                        nc.gpsimd.tensor_tensor(t[:, 0:n, :], t[:, 0:n, :], t[:, n:2 * n, :],
                                                ALU.add).then_inc(ada_mult, 1)
                    nc.gpsimd.wait_ge(ada_mult, a * 3 + 3)
                    nc.gpsimd.wait_ge(ada_col, a + 1)
                    nc.gpsimd.tensor_tensor(adacc[:, s, :], t[:, 0, :], t[:, 1, :], ALU.add).then_inc(ada_sum, 1)

        def ada_sums(slots, i=None):
            for u, s in enumerate(slots):
                a = unit_index(slots, u, i)
                t = ada[:, s, :].rearrange("p (k n) -> p k n", k=KT)
                if u < 3:
                    nc.vector.wait_ge(ada_mult, i * 12 + 4 * (u + 1))
                else:
                    nc.vector.wait_ge(ada_here[s], i * 16 + 16)
                    V.mark(nc.vector.tensor_tensor(t, t, cact.unsqueeze(2).to_broadcast([P, KT, P]), ALU.mult))
                    V.after()
                nc.vector.wait_ge(ada_col, a + 1)
                nc.vector.tensor_reduce(adacc[:, s, :], t.rearrange("p k n -> p n k"), AX.X,
                                        ALU.add).then_inc(start_sum, 1)

        def ada_cols(slots, i=None, summed=None, col_bank=6):
            for u, s in enumerate(slots):
                a = unit_index(slots, u, i)
                nc.tensor.wait_ge(summed or ada_sum, a + 5)
                nc.tensor.matmul(PS[:, bass.ds(a + col_bank * 512, 1)] if i is not None
                                 else PS[:, col_bank * 512 + a:col_bank * 512 + a + 1],
                                 adacc[:, s, :], ones_f[:, 0:1], start=True, stop=True,
                                 skip_group_check=True).then_inc(ada_col, 1)

        def ada_advance(slots, turns=1):
            for s in slots:
                ada_slot[s] += turns
            state["a"] += len(slots) * turns

        ones_f = sb("ones_f", [P, 1])
        ones_ready = V.mark(nc.vector.memset(ones_f[:], 1.0))
        T.wait(ones_ready)

        def mod_add(a0, a1, col_bank=6):
            nc.vector.wait_ge(ada_col, a1 + 4)
            return V.mark(nc.vector.tensor_tensor(mod[:, a0:a1], bank(col_bank)[:, a0:a1],
                                                  par["ada_b"][:, a0:a1], ALU.add))

        def prep(q, s):
            nc.scalar.wait_ge(w_here[s], q * 8 + (16 - 8 * s))
            nc.scalar.wait_ge(w_used, q + 1)
            for h in range(2):
                c = slice(h * 1024, (h + 1) * 1024)
                nc.scalar.activation(whi[s][:, c], stage[s][:, c], ACT.Copy).then_inc(w_hi_done, 1)
                nc.vector.wait_ge(w_hi_done, q * 2 + (h + 1))
                nc.vector.tensor_tensor(wlo[s][:, c], stage[s][:, c], whi[s][:, c].bitcast(F32),
                                        ALU.subtract).then_inc(w_lo_done, 1)

        def half_ready(q, h):
            nc.tensor.wait_ge(w_lo_done, q * 2 + (h + 1))

        def up_products(q, s, o_of, token_major):
            wh = whi[s][:].rearrange("p (k n) -> p k n", k=KT)
            wl = wlo[s][:].rearrange("p (k n) -> p k n", k=KT)
            half_ready(q, 0)
            for t in range(2):
                o, c = o_of(t), slice(t * P, (t + 1) * P)
                for k in range(KT):
                    if t == 0 and k == KT // 2:
                        half_ready(q, 1)
                    for n, (w, a) in enumerate(((wh, hh), (wh, hl), (wl, hh))):
                        first, last = k == 0 and n == 0, k == KT - 1 and n == 2
                        if token_major:
                            m = nc.tensor.matmul(o, a[:, k, c], w[:, k, :], start=first, stop=last)
                        else:
                            m = nc.tensor.matmul(o, w[:, k, c], a[:, k, :], start=first, stop=last)
            m.then_inc(w_used, 1)

        def gemm_chunk(q, s, token_major):
            nc.tensor.wait_ge(out_free, q_out(q) + 1)
            up_products(q, s, lambda t: PS[:, s * 512 + t * S:s * 512 + (t + 1) * S], token_major)

        outs = {"n": 0}

        def q_out(q):
            return q - outs["n"]

        def gemm(n, evac, token_major=False, units=(), per=None):
            per = dict(per or {})
            m = 4 if units else 2
            segments.append(((n - state["ahead"]) // m, m, tuple(units)))
            state["ahead"] = 0
            q0 = state["q"]
            with Loop(n // m, gpsimd=bool(units), **{k: v * m // 2 for k, v in per.items()}) as i:
                for j in range(m):
                    s = j % 2
                    q = i * m + (q0 + j)
                    prep(q + 1, 1 - s)
                    gemm_chunk(q, s, token_major)
                    if j == 0 and units:
                        ada_units(units, i)
                    if j % 2 and units:
                        ada_cols(units[j - 1:j + 1], (i, j // 2))
                    evac(i * m + j, s, q)
            if units:
                ada_advance(units, n // m)
            state["q"] += n

        def product_ready(lane, q):
            lane.eng.wait_ge(w_used, q + 3)

        def rsqrt(o, mean):
            V.wait(A.mark(nc.scalar.activation(o, mean, ACT.Sqrt, bias=eps[:])))
            V.after()
            return V.mark(nc.vector.reciprocal(o, o))

        def norm(gain_of, shift_cols, same_x=False, split=True, squares=None):
            sq = squares if squares is not None else arena[:, 0:KT * S].rearrange("p (k t) -> p k t", k=KT)
            sums = PS[:, 7 * 512:7 * 512 + S]
            A.wait(V.last())
            A.wait(T.last())
            V.wait(A.last())
            V.after()
            if not same_x:
                for k in range(0, KT, 2):
                    two = slice(k, k + 2)
                    if k % 4:
                        T.wait(V.mark(nc.vector.tensor_tensor(sq[:, two, :], x[:, two, :], x[:, two, :], ALU.mult)))
                    else:
                        T.wait(A.mark(nc.scalar.activation(sq[:, two, :], x[:, two, :], ACT.Square)))
                    for t in (k, k + 1):
                        mm = nc.tensor.matmul(sums, ones[:], sq[:, t, :], start=t == 0, stop=t == KT - 1)
                summed = T.mark(mm)
            for k in range(KT // 2):
                A.mark(nc.scalar.activation(xa[:, k, :], x[:, k, :], ACT.Copy, scale=gain_of[:, k:k + 1]))
                V.mark(nc.vector.tensor_scalar(xa[:, k + KT // 2, :], x[:, k + KT // 2, :],
                                               gain_of[:, k + KT // 2:k + KT // 2 + 1], None, ALU.mult))
            if not same_x:
                A.wait(summed)
                rsqrt(rstd[:, 0:S], sums)
            V.wait(A.last())
            V.after()
            prods = {}
            for k in range(0, KT, 2):
                two = slice(k, k + 2)
                prods[k] = V.mark(nc.vector.tensor_tensor(
                    xa[:, two, :], xa[:, two, :], rstd[:, 0:S].unsqueeze(1).to_broadcast([P, 2, S]), ALU.mult))
            if not split:
                return
            for k in range(0, KT, 2):
                two = slice(k, k + 2)
                A.wait(prods[k])
                if shift_cols is None:
                    V.wait(A.mark(nc.scalar.activation(hh[:, two, :], xa[:, two, :], ACT.Copy)))
                    lo = V.mark(nc.vector.tensor_tensor(hl[:, two, :], xa[:, two, :], hh[:, two, :].bitcast(F32),
                                                        ALU.subtract))
                    continue
                for t in (k, k + 1):
                    sh = shift_cols[:, t:t + 1]
                    V.wait(A.mark(nc.scalar.activation(hh[:, t, :], xa[:, t, :], ACT.Identity, bias=sh)))
                    lo = V.mark(nc.vector.scalar_tensor_tensor(hl[:, t, :], xa[:, t, :], sh,
                                                               hh[:, t, :].bitcast(F32), ALU.add, ALU.subtract))
            T.wait(lo)

        def gain_mod(g, scale_cols):
            V.after()
            V.mark(nc.vector.scalar_tensor_tensor(gain[:], scale_cols, 1.0, g, ALU.add, ALU.mult))

        def split_act(src, k, waits):
            A.wait(waits)
            hi = A.mark(nc.scalar.activation(hh[:, k, :], src, ACT.Copy))
            V.wait(hi)
            return V.mark(nc.vector.tensor_tensor(hl[:, k, :], src, hh[:, k, :].bitcast(F32), ALU.subtract))

        def residual_evac(gate_cols):
            def evac(i, s, q):
                product_ready(V, q)
                for t in range(2):
                    tile = i * 2 + t
                    xt = x[:, bass.ds(tile, 1), :].rearrange("p a t -> p (a t)")
                    src = PS[:, s * 512 + t * S:s * 512 + (t + 1) * S]
                    g = gate_cols[:, bass.ds(tile, 1)] if gate_cols is not None else one[:]
                    m = nc.vector.scalar_tensor_tensor(xt, src, g, xt, ALU.mult, ALU.add)
                    V.mark(m)
                V.after()
                nc.vector.sem_inc(out_free, 1)
            return evac

        f_parts = sb("forget_parts", [112, S], F32R)
        f_sel = sb("forget_select", [112, 32], F32R)
        act_a = sb("mlp_relu", [P, 2 * S])
        act_y = act_a
        ah = sb("mlp_hi", [P, 2 * S], F32R)
        al = sb("mlp_lo", [P, 2 * S], F32R)

        def mlp(gate_of, units=(), between=None, turns_before=0):
            q0 = state["q"]
            segments.append((1, 1, ()))
            segments.append((MLP_CHUNKS // 2 - 1, 4, tuple(units)))
            segments.append((1, 2, tuple(units[:2])))
            segments.append((1, 1, tuple(units[2:])))
            T.wait(V.last())
            for b in range(4):
                for t in range(2):
                    nc.tensor.matmul(PS[:, b * 512 + t * S:b * 512 + (t + 1) * S], zr[:, 0:P], zr[:],
                                     start=t == 0, stop=False, skip_group_check=True)

            def up(q, s):
                up_products(q, s, lambda t: PS[:, 2048 + t * S:2048 + (t + 1) * S], False)

            def hidden(q, waits):
                product_ready(A, q)
                A.wait(waits)
                V.wait(A.mark(nc.scalar.activation(act_a[:], bank(4), ACT.Relu)))
                V.mark(nc.vector.tensor_tensor(act_a[:], act_a[:], act_a[:], ALU.mult))

            def split_hidden(squared, q_before):
                A.wait(squared)
                product_ready(A, q_before)
                V.wait(A.mark(nc.scalar.activation(ah[:], act_a[:], ACT.Copy)))
                return V.mark(nc.vector.tensor_tensor(al[:], act_a[:], ah[:].bitcast(F32), ALU.subtract))

            def down(q, s, lo):
                wh = whi[s][:].rearrange("p (k n) -> p k n", k=2)
                wl = wlo[s][:].rearrange("p (k n) -> p k n", k=2)
                T.wait(lo)
                for kk in range(2):
                    half_ready(q, kk)
                    a_h, a_l = ah[:, kk * S:(kk + 1) * S], al[:, kk * S:(kk + 1) * S]
                    for n in range(KT):
                        c = slice(n * P, (n + 1) * P)
                        for w, a in ((wh, a_h), (wh, a_l), (wl, a_h)):
                            m = nc.tensor.matmul(PS[:, n * S:(n + 1) * S], w[:, kk, c], a, start=False,
                                                 stop=False, skip_group_check=True)
                m.then_inc(w_used, 1)

            def turn(q, i, last_al, slots):
                relu = A.last()
                lo = split_hidden(V.last(), q - 1)
                T.wait(relu)
                up(q, 1)
                prep(q + 1, 0)
                down(q + 1, 0, lo)
                if slots:
                    ada_units(slots, i)
                hidden(q, lo)
                prep(q + 2, 1)
                if slots:
                    ada_cols(slots, i)

            prep(q0 + 1, 1)
            up(q0, 0)
            hidden(q0, None)
            both = (units[:2], units[2:])
            if between is not None:
                with Loop(turns_before, V=4, A=4) as i:
                    for n in range(2):
                        turn(i * 4 + (q0 + 1 + 2 * n), None, None, ())
                between()
            with Loop(MLP_CHUNKS // 2 - 1 - turns_before, gpsimd=bool(units), V=4, A=4) as i:
                for n in range(2):
                    turn(i * 4 + (q0 + 4 * turns_before + 1 + 2 * n), (i, n) if units else i, None, both[n])
            if units:
                ada_advance(units, MLP_CHUNKS // 2 - 1)
            q = q0 + 2 * MLP_CHUNKS - 3
            turn(q, None, None, both[0])
            if units:
                ada_advance(both[0])
            q += 2
            lo = split_hidden(V.last(), q - 1)
            if units:
                ada_units(both[1])
            if q + 1 < TOTAL:
                prep(q + 1, 0)
            down(q, 1, lo)
            if units:
                ada_cols(both[1])
                ada_advance(both[1])
            state["q"] += 2 * MLP_CHUNKS
            outs["n"] += 2 * MLP_CHUNKS
            product_ready(V, q)
            g = gate_of()
            V.after()
            for n in range(KT):
                V.mark(nc.vector.scalar_tensor_tensor(x[:, n, :], PS[:, n * S:(n + 1) * S],
                                                      g[:, n:n + 1] if g is not None else one[:],
                                                      x[:, n, :], ALU.mult, ALU.add))
            V.after()

        def copy_evac(dst, scale=1.0):
            def evac(i, s, q):
                product_ready(A, q)
                o = dst[:, bass.ds(i * 2, 2), :]
                A.mark(nc.scalar.activation(o, bank(s).rearrange("p (a t) -> p a t", a=2), ACT.Copy,
                                            scale=scale))
                A.after()
                nc.scalar.sem_inc(out_free, 1)
            return evac

        def copy_evac_tm(dst):
            def evac(i, s, q):
                product_ready(A, q)
                o = dst[:, :, bass.ds(i * CW, CW)]
                A.mark(nc.scalar.activation(o, bank(s).rearrange("p (a t) -> p a t", a=2), ACT.Copy))
                A.after()
                nc.scalar.sem_inc(out_free, 1)
            return evac

        def carve(*sizes):
            o, got = 0, []
            for n in sizes:
                got.append(arena[:, o:o + n])
                o += n
            assert o <= ARENA, o
            return got

        def hgrn(u, vt, side):
            ab, ac, acth, hq, hf, hg = (u[:, 4 * n:4 * n + 4, :] for n in range(6))
            o = 24 * S + NB * 512
            pre, suf, ql, kl, kk, sc0, sc1, y, t1 = [arena[:, o + n * 1024:o + (n + 1) * 1024] for n in range(9)]
            ql2, kl2, p_, cv = [arena[:, o + n * 1024:o + (n + 1) * 1024] for n in range(9, 13)]
            heads = lambda t: t.rearrange("p (h t) -> p h t", h=HG_HEADS)
            A.wait(V.last())
            V.wait(A.last())
            sig = A.mark(nc.scalar.activation(hf, hf, ACT.Sigmoid))
            sig_g = A.mark(nc.scalar.activation(heads(y), hg, ACT.Sigmoid))
            V.mark(nc.vector.memset(suf, 1.0))
            for t in (ql, kl, ql2, kl2):
                V.mark(nc.vector.memset(t, 0.0))
            V.mark(nc.vector.memset(sc0, 0.0))
            V.mark(nc.vector.memset(sc1[:, 0:512], 0.0))
            lg = par["lb"]
            lb, oml, tmp, ex = small[:, 16:20], small[:, 20:24], small[:, 24:28], small[:, 28:40]
            V.mark(nc.vector.tensor_tensor(tmp, lg[:, 0:4], lg[:, 4:8], ALU.max))
            V.mark(V.then().tensor_tensor(tmp, tmp, lg[:, 8:12], ALU.max))
            for r in range(3):
                V.mark(V.then().tensor_tensor(ex[:, 4 * r:4 * r + 4], lg[:, 4 * r:4 * r + 4], tmp, ALU.subtract))
            A.wait(V.last())
            V.wait(A.mark(nc.scalar.activation(ex, ex, ACT.Exp)))
            V.mark(nc.vector.tensor_tensor(tmp, ex[:, 0:4], ex[:, 4:8], ALU.add))
            V.mark(V.then().tensor_tensor(tmp, tmp, ex[:, 8:12], ALU.add))
            V.mark(V.then().reciprocal(tmp, tmp))
            V.mark(V.then().tensor_tensor(lb, ex[:, 0:4], tmp, ALU.mult))
            V.mark(V.then().tensor_scalar(oml, lb, -1.0, 1.0, ALU.mult, ALU.add))
            V.wait(sig)
            V.after()
            for h in range(HG_HEADS):
                V.mark(nc.vector.tensor_scalar(heads(pre)[:, h, :], hf[:, h, :], oml[:, h:h + 1],
                                               lb[:, h:h + 1], ALU.mult, ALU.add))
            V.mark(V.then().tensor_scalar(kk, pre, -1.0, 1.0, ALU.mult, ALU.add))
            sc0h = sc0.rearrange("p (h t) -> p h t", h=HG_HEADS)
            sc1h = sc1[:, 0:512].rearrange("p (h t) -> p h t", h=HG_HEADS)

            def block_scores(key, query, waits, pair):
                T.wait(waits)
                for b in range(NB):
                    for h in range(HG_HEADS):
                        cols = slice(h * S + b * P, h * S + (b + 1) * P)
                        m = nc.tensor.matmul(PS[:, (pair + b) * 512 + h * P:(pair + b) * 512 + (h + 1) * P],
                                             key[:, cols], query[:, cols], start=True, stop=True)
                return T.mark(m), pair

            def keep_scores(done, mask):
                V.wait(done[0])
                for b, dst in ((0, sc0h[:, :, 0:P]), (1, sc1h)):
                    V.mark(nc.vector.copy_predicated(
                        dst, mask.bitcast(I32).unsqueeze(1).to_broadcast([P, HG_HEADS, P]),
                        bank(done[1] + b).rearrange("p (h t) -> p h t", h=HG_HEADS)))

            hqf = u[:, 12:16, :].rearrange("p h t -> p (h t)")
            V.wait(masks_ready)
            done, mask = block_scores(kk, hqf, V.last(), 4), masks[7]
            c = 1
            for lev in range(8):
                if lev in side:
                    side[lev]()
                q_, k_ = ((ql, kl), (ql2, kl2))[lev % 2]
                seg = lambda t: t.rearrange("p (n a c) -> p n a c", a=2, c=c)
                n = HG_HEADS * S // (2 * c)
                V.after()
                left_total = seg(pre)[:, :, 0, c - 1:c].to_broadcast([P, n, c])
                right_total = seg(pre)[:, :, 1, c - 1:c].to_broadcast([P, n, c])
                V.mark(nc.vector.tensor_tensor(seg(q_)[:, :, 1, :], seg(hqf)[:, :, 1, :],
                                               seg(pre)[:, :, 1, :], ALU.mult))
                V.mark(nc.vector.tensor_tensor(seg(k_)[:, :, 0, :], seg(kk)[:, :, 0, :],
                                               seg(suf)[:, :, 0, :], ALU.mult))
                scaled = V.last()
                if lev < 7:
                    V.mark(V.then().tensor_tensor(seg(suf)[:, :, 0, :], seg(suf)[:, :, 0, :], right_total,
                                                  ALU.mult))
                    V.mark(V.then().tensor_tensor(seg(pre)[:, :, 1, :], seg(pre)[:, :, 1, :], left_total,
                                                  ALU.mult))
                    before = done, mask
                    done, mask = block_scores(k_, q_, scaled, 2 + 2 * (lev % 2)), masks[lev]
                    V.after()
                    keep_scores(*before)
                else:
                    V.after()
                    keep_scores(done, mask)
                    T.wait(scaled)
                    for h in range(HG_HEADS):
                        m = nc.tensor.matmul(PS[:, h * P:(h + 1) * P], k_[:, h * S:h * S + P],
                                             q_[:, h * S + P:(h + 1) * S], start=True, stop=True)
                    V.wait(T.mark(m))
                    V.mark(V.then().tensor_copy(sc0h[:, :, P:S], bank(0).rearrange("p (h t) -> p h t", h=HG_HEADS)))
                c *= 2
            T.wait(V.last())
            for h in range(HG_HEADS):
                o_h = PS[:, 2048 + h * S:2048 + (h + 1) * S]
                nc.tensor.matmul(o_h, vt[:, 0, h * P:(h + 1) * P], sc0h[:, h, :], start=True, stop=False,
                                 skip_group_check=True)
                m = nc.tensor.matmul(o_h[:, P:S], vt[:, 1, h * P:(h + 1) * P], sc1h[:, h, :], start=False,
                                     stop=True, skip_group_check=True)
            o_done = T.mark(m)
            cw = par["conv_w"]
            V.mark(nc.vector.tensor_tensor(heads(p_), ac, acth, ALU.mult))
            V.after()
            for m_ in range(4):
                V.mark(nc.vector.tensor_scalar(heads(cv)[:, m_, :], heads(p_)[:, m_, :], cw[:, 8 + m_:9 + m_],
                                               None, ALU.mult))
            for tap, sh in ((1, 1), (0, 2)):
                V.after()
                for m_ in range(4):
                    d = heads(cv)[:, m_, sh:S]
                    V.mark(nc.vector.scalar_tensor_tensor(d, heads(p_)[:, m_, 0:S - sh],
                                                          cw[:, 4 * tap + m_:4 * tap + m_ + 1], d,
                                                          ALU.mult, ALU.add))
            conv_done = V.mark(V.then().tensor_tensor(heads(cv), heads(cv), ab, ALU.mult))
            A.wait(o_done)
            sq = A.mark(nc.scalar.activation(ql, PS[:, 2048:3072], ACT.Square))
            T.wait(sq)
            for b in range(2):
                m = nc.tensor.matmul(bank(2 + b), ones_h[:], ql[:, b * 512:(b + 1) * 512], start=True, stop=True)
            A.wait(T.mark(m))
            rsqrt(kl, PS[:, 1024:2048])
            V.wait(sig_g)
            for m_ in range(4):
                split_act(heads(cv)[:, m_, :], m_, conv_done)
            V.mark(nc.vector.tensor_tensor(heads(y), heads(y), hg, ALU.mult))
            V.after()
            for h in range(HG_HEADS):
                V.mark(nc.vector.scalar_tensor_tensor(heads(t1)[:, h, :], PS[:, 2048 + h * S:2048 + (h + 1) * S],
                                                      par["hg_norm"][:, h:h + 1], heads(kl)[:, h, :],
                                                      ALU.mult, ALU.mult))
            y_done = V.mark(V.then().tensor_tensor(y, y, t1, ALU.mult))
            for h in range(HG_HEADS):
                lo = split_act(heads(y)[:, h, :], 4 + h, y_done)
            T.wait(lo)

        def attend_out(h, w_s0, w_s1, vt, waits):
            po, pr = HD * (h % 2), h // 2
            o = PS[po:po + HD, (6 + pr % 2) * 512:(6 + pr % 2) * 512 + S]
            T.wait(waits)
            nc.tensor.matmul(o, vt[:, 0, h * HD:(h + 1) * HD], w_s0, start=True, stop=False,
                             skip_group_check=True)
            return T.mark(nc.tensor.matmul(o[:, P:S], vt[:, 1, h * HD:(h + 1) * HD], w_s1, start=False,
                                           stop=True, skip_group_check=True))

        def split_pair(pr, waits):
            return split_act(PS[:, (6 + pr % 2) * 512:(6 + pr % 2) * 512 + S], pr, waits)

        def scores(h, qk, b_of, waits, stop=True):
            po, pr = HD * (h % 2), h // 2
            T.wait(*waits)
            z = bank(b_of)
            nc.tensor.matmul(z[:, 0:P], qk[po:po + HD, pr, 0:P], qk[po:po + HD, 8 + pr, 0:P], start=True,
                             stop=stop, skip_group_check=True)
            return nc.tensor.matmul(z[:, P:P + S], qk[po:po + HD, pr, P:S], qk[po:po + HD, 8 + pr, :],
                                    start=True, stop=stop, skip_group_check=True)

        def stick_breaking(qk, vt, work, side):
            A.wait(V.last())
            V.wait(A.last())
            T.wait(A.last())
            W = P + S
            bt = [work[:, n * W:(n + 1) * W] for n in (0, 1, 2)]
            om = [work[:, n * W:(n + 1) * W] for n in (3, 4)]
            o = 5 * W
            pr_ = [work[:, o + n * (W + 2):o + (n + 1) * (W + 2)] for n in (0, 1)]
            o += 2 * (W + 2)
            wt = [work[:, o + n * W:o + (n + 1) * W] for n in (0, 1)]
            o += 2 * W
            late, keep = rstd, work[:, o:o + W]
            V.mark(V.then().memset(late[:, 0:P], 0.0))
            V.mark(nc.vector.memset(late[:, P:S], 1.0))
            V.mark(nc.vector.memset(keep, 1.0))
            G.wait(V.last())
            G.mark(G.then().affine_select(out=late[:, P:S], in_=late[:, P:S], compare_op=ALU.is_ge, fill=0.0,
                                           base=0, pattern=[[1, P]], channel_multiplier=-1))
            for c in (0, S):
                G.mark(G.then().affine_select(out=keep[:, c:c + P], in_=keep[:, c:c + P], compare_op=ALU.is_ge,
                                               fill=0.0, base=-1, pattern=[[1, P]], channel_multiplier=-1))
            late_done = G.last()
            side[-1]()
            sq2 = [work[:, 0:512], work[:, 512:1024]]
            rs2 = [work[:, 1024:1536], work[:, 1536:2048]]
            used = [None, None]
            freed = [None, None]
            for n in range(8):
                src = qk[:, 2 * n:2 * n + 2, :].rearrange("p m t -> p (m t)")
                A.wait(used[n % 2])
                T.wait(A.mark(nc.scalar.activation(sq2[n % 2], src, ACT.Square)))
                m = T.mark(nc.tensor.matmul(bank(2 + n % 2), blk[:], sq2[n % 2], start=True, stop=True))
                used[n % 2] = m
                A.wait(m, freed[n % 2])
                rsqrt(rs2[n % 2], bank(2 + n % 2))
                g = par["q_norm"] if n < 4 else par["k_norm"]
                freed[n % 2] = V.mark(V.then().scalar_tensor_tensor(src, src, g, rs2[n % 2], ALU.mult, ALU.mult))
            A.wait(V.last())
            for n in (0, 1):
                V.mark(V.then().memset(pr_[n][:, P:P + 1], 1.0))
                V.mark(nc.vector.memset(pr_[n][:, W + 1:W + 2], 1.0))
            V.wait(late_done)
            T.wait(V.last())
            z_read, w_done, w_read, wt_done, pv, o_read = {}, {}, {}, {}, {}, {}

            def weights(h):
                n = h % 2
                zz = T.mark(scores(h, qk, n, (z_read.get(h - 2),)))
                A.wait(zz, w_read.get(h - 3), w_done.get(h - 2))
                A.mark(nc.scalar.activation(bt[h % 3], bank(n)[:, 0:W], ACT.Sigmoid, scale=HD ** -0.5))
                z_read[h] = A.mark(nc.scalar.activation(om[n], bank(n)[:, 0:W], ACT.Sigmoid,
                                                        scale=-HD ** -0.5))
                V.wait(z_read[h])
                q = pr_[n]
                V.mark(nc.vector.tensor_tensor_scan(q[:, 0:P][:, ::-1], om[n][:, 0:P][:, ::-1],
                                                    late[:, P:S][:, ::-1], 1.0, ALU.mult, ALU.max))
                V.mark(nc.vector.tensor_tensor_scan(q[:, P + 1:W + 1][:, ::-1], om[n][:, P:W][:, ::-1],
                                                    late[:, ::-1], 1.0, ALU.mult, ALU.max))
                V.mark(V.then().tensor_tensor(bt[h % 3][:, 0:P], bt[h % 3][:, 0:P], q[:, 1:P + 1], ALU.mult))
                w_done[h] = V.mark(nc.vector.tensor_tensor(bt[h % 3][:, P:W], bt[h % 3][:, P:W],
                                                           q[:, P + 2:W + 2], ALU.mult))

            def turned(h):
                n = h % 2
                T.wait(w_done[h], wt_done.get(h - 2))
                wb = bank(2 + n)
                for c in (0, P, S):
                    m = nc.tensor.transpose(wb[:, c:c + P], bt[h % 3][:, c:c + P], ident[:])
                w_read[h] = T.mark(m)
                V.wait(w_read[h], pv.get(h - 2))
                wt_done[h] = V.mark(nc.vector.tensor_tensor(wt[n], wb[:, 0:W], keep, ALU.mult))

            def values(h):
                n, pr = h % 2, h // 2
                if n == 0:
                    T.wait(o_read.get(pr - 2))
                pv[h] = attend_out(h, wt[n][:, 0:S], wt[n][:, S:W], vt, wt_done[h])
                if n:
                    o_read[pr] = split_pair(pr, pv[h])

            for step in range(HEADS + 3):
                if step < HEADS:
                    weights(step)
                if step in side:
                    side[step]()
                if 2 <= step <= HEADS + 1:
                    turned(step - 2)
                if step >= 3:
                    values(step - 3)
            T.wait(o_read[HEADS // 2 - 1])

        def glu_evac(sg):
            def evac(i, s, q):
                product_ready(A, q)
                A.wait(V.last())
                V.wait(A.mark(nc.scalar.activation(sg[s], PS[:, s * 512 + S:s * 512 + 2 * S], ACT.Sigmoid)))
                V.mark(nc.vector.tensor_tensor(sg[s], PS[:, s * 512:s * 512 + S], sg[s], ALU.mult))
                xt = x[:, bass.ds(i, 1), :].rearrange("p a t -> p (a t)")
                V.mark(V.then().tensor_tensor(xt, xt, sg[s], ALU.add))
                V.after()
                nc.vector.sem_inc(out_free, 1)
            return evac

        wide = lambda t: t.unsqueeze(2).to_broadcast([P, GROUPS, GC])
        gc = lambda t: t.rearrange("p (g c) -> p g c", g=GROUPS)
        gic = lambda t: t.rearrange("p (g i c) -> p g i c", g=GROUPS, i=TAPS)
        to_out, toep, to_state = [arena[:, n * 8192:(n + 1) * 8192] for n in range(3)]
        bs, bsw, cs, csw, b_bar, jb_bar = [arena[:, 10240 + n * 1024:11264 + n * 1024] for n in range(6)]
        adaf = ada[:].rearrange("p s n -> p (s n)")
        small_of = lambda n: adaf[:, n * 64:(n + 1) * 64]
        powr = [small_of(n) for n in range(13)]
        powi = [small_of(n) for n in range(13, 26)]
        ldt, are, aim = [small_of(n) for n in range(26, 29)]
        dt, er, th, rn, co, si, den, wr, wi, nr, tt, tu = [small_of(n) for n in range(29, 41)]
        prod = adaf[:, 3072:4096]
        taps = prod
        sgn, nsgn = small[:, 40:41], small[:, 41:42]
        act_squares = adaf[:, 2048:4096].rearrange("p (k t) -> p k t", k=KT)
        ssm_marks = {}

        def gtt(o, a, b, op, after=True):
            return G.mark((G.then() if after else nc.gpsimd).tensor_tensor(o, a, b, op))

        def ssm_load():
            w0 = GROUPS * 3
            A.wait(V.last())
            nc.scalar.dma_start(adaf[:, 26 * 64:29 * 64], p["ssm_in"][:, 0:w0]).then_inc(s_dma, 16)
            nc.scalar.dma_start(arena[:, 10240:14336], p["ssm_in"][:, w0:w0 + 4096]).then_inc(s_dma, 16)

        def ssm_steps():
            nc.scalar.wait_ge(s_dma, 32)
            ssm_marks["dt"] = A.mark(nc.scalar.activation(dt, ldt, ACT.Exp))

        def ssm_angles():
            nc.vector.wait_ge(s_dma, 32)
            V.wait(ssm_marks["dt"])
            V.mark(nc.vector.memset(small[0:64, 40:41], -1.0))
            V.mark(nc.vector.memset(small[64:128, 40:41], 1.0))
            V.mark(nc.vector.memset(small[0:64, 41:42], 1.0))
            V.mark(nc.vector.memset(small[64:128, 41:42], -1.0))
            V.mark(nc.vector.tensor_tensor(den, are, are, ALU.mult))
            V.mark(nc.vector.tensor_tensor(tt, aim, aim, ALU.mult))
            V.mark(nc.vector.tensor_tensor(er, are, dt, ALU.mult))
            V.mark(nc.vector.tensor_tensor(th, aim, dt, ALU.mult))
            V.mark(V.then().tensor_tensor(den, den, tt, ALU.add))
            V.mark(nc.vector.tensor_scalar(rn, th, 1.0 / TWO_PI, ROUND, ALU.mult, ALU.add))
            V.mark(V.then().tensor_scalar(rn, rn, -ROUND, None, ALU.add))
            V.mark(nc.vector.reciprocal(den, den))
            for part in (PI_A, PI_B, PI_C):
                V.mark(V.then().scalar_tensor_tensor(th, rn, -part, th, ALU.mult, ALU.add))
            ssm_marks["angle"] = V.mark(V.then().tensor_scalar(th, th, -3.1415925, 3.1415925, ALU.max, ALU.min))

        def ssm_rotations():
            A.wait(ssm_marks["angle"])
            A.mark(nc.scalar.activation(er, er, ACT.Exp))
            A.mark(nc.scalar.activation(si, th, ACT.Sin))
            A.mark(nc.scalar.activation(co, th, ACT.Abs))
            ssm_marks["rotation"] = A.mark(A.then().activation(co, co, ACT.Sin, scale=-1.0, bias=halfpi[:]))

        def ssm_inputs_to_states():
            G.wait(ssm_marks["rotation"])
            nc.gpsimd.wait_ge(s_dma, 32)
            lr, li = powr[1], powi[1]
            gtt(lr, er, co, ALU.mult)
            gtt(li, er, si, ALU.mult, False)
            G.mark(nc.gpsimd.memset(powr[0], 1.0))
            G.mark(nc.gpsimd.memset(powi[0], 0.0))

            def cmul(o_r, o_i, a_r, a_i, b_r, b_i):
                gtt(tt, a_i, b_i, ALU.mult)
                gtt(tu, a_i, b_r, ALU.mult, False)
                gtt(o_r, a_r, b_r, ALU.mult, False)
                gtt(o_i, a_r, b_i, ALU.mult, False)
                gtt(o_r, o_r, tt, ALU.subtract)
                gtt(o_i, o_i, tu, ALU.add, False)

            for k in range(2, 9):
                cmul(powr[k], powi[k], powr[k // 2], powi[k // 2], powr[k - k // 2], powi[k - k // 2])
            for k in range(9, 12):
                cmul(powr[k], powi[k], powr[k - 1], powi[k - 1], powr[k - 1], powi[k - 1])
            G.mark(G.then().tensor_scalar(nr, lr, -1.0, None, ALU.add))
            gtt(wr, nr, are, ALU.mult)
            gtt(tt, li, aim, ALU.mult, False)
            gtt(wi, li, are, ALU.mult, False)
            gtt(tu, nr, aim, ALU.mult, False)
            gtt(wr, wr, tt, ALU.add)
            gtt(wi, wi, tu, ALU.subtract, False)
            gtt(wr, wr, den, ALU.mult)
            gtt(wi, wi, den, ALU.mult, False)
            G.mark(nc.gpsimd.tensor_scalar(bsw, bsw, sgn, None, ALU.mult))
            G.mark(nc.gpsimd.tensor_scalar(cs, cs, nsgn, None, ALU.mult))
            gtt(gc(b_bar), gc(bs), wide(wr), ALU.mult)
            gtt(gc(prod), gc(bsw), wide(wi), ALU.mult, False)
            gtt(b_bar, b_bar, prod, ALU.add)
            gtt(gc(jb_bar), gc(bsw), wide(wr), ALU.mult, False)
            gtt(gc(prod), gc(bs), wide(wi), ALU.mult)
            gtt(jb_bar, jb_bar, prod, ALU.subtract)
            for i in range(TAPS):
                gtt(gc(prod), gc(jb_bar), wide(powi[7 - i]), ALU.mult)
                gtt(gic(to_state)[:, :, i, :], gc(b_bar), wide(powr[7 - i]), ALU.mult, False)
                ssm_marks["to_state"] = gtt(gic(to_state)[:, :, i, :], gic(to_state)[:, :, i, :], gc(prod), ALU.add)

        def ssm_states_to_outputs():
            G.wait(T.last(), V.last())
            for i in range(TAPS):
                gtt(gc(prod), gc(csw), wide(powi[i + 1]), ALU.mult)
                gtt(gic(to_out)[:, :, i, :], gc(cs), wide(powr[i + 1]), ALU.mult, False)
                ssm_marks["to_out"] = gtt(gic(to_out)[:, :, i, :], gic(to_out)[:, :, i, :], gc(prod), ALU.subtract)

        def ssm_taps():
            T.wait(ssm_marks["to_state"])
            for g in range(GROUPS):
                m = nc.tensor.matmul(PS[:, 2560 + g * GC:2560 + (g + 1) * GC], to_state[:, g * P:(g + 1) * P],
                                     cs[:, g * GC:(g + 1) * GC], start=True, stop=True)
            A.wait(T.mark(m), ssm_marks["to_out"])
            ssm_marks["taps"] = A.mark(nc.scalar.activation(taps, PS[:, 2560:3584], ACT.Copy))
            read = {5: ssm_marks["taps"], 6: ssm_marks["taps"], 7: None}
            for n in range(GROUPS // 4):
                b = (7, 5, 6)[n % 3]
                cols = slice(n * 512, (n + 1) * 512)
                T.wait(read[b])
                for g in range(4):
                    m = nc.tensor.transpose(PS[:, b * 512 + g * P:b * 512 + (g + 1) * P],
                                            to_state[:, (4 * n + g) * P:(4 * n + g + 1) * P], ident[:])
                m = T.mark(m)
                if n % 2:
                    V.wait(m)
                    read[b] = V.mark(nc.vector.tensor_copy(to_state[:, cols], bank(b)))
                else:
                    A.wait(m)
                    read[b] = A.mark(nc.scalar.activation(to_state[:, cols], bank(b), ACT.Copy))

        def ssm_toeplitz():
            G.wait(ssm_marks["taps"])
            G.mark(G.then().memset(toep, 0.0))
            G.mark(G.then().tensor_copy(gic(toep)[:, :, TAPS - 1, :], gc(taps)))
            xf = xa[:].rearrange("p k t -> p (k t)")
            moved = [xf[:, 0:1024], xf[:, 1024:2048], adaf[:, 2048:3072]]
            count = 0
            for blocks in ((0, 1, 2), (3, 4, 5), (6,)):
                G.after()
                for n, i in enumerate(blocks):
                    rows = (i + 1) * GC
                    nc.gpsimd.dma_start(moved[n][0:rows, :], taps[P - rows:P, :]).then_inc(s_shift, 16)
                    count += 16
                nc.gpsimd.wait_ge(s_shift, count)
                for n, i in enumerate(blocks):
                    rows = (i + 1) * GC
                    G.mark(nc.gpsimd.tensor_copy(gic(toep)[0:rows, :, i, :], gc(moved[n])[0:rows]))

        def ssm():
            uc = adaf[:, 2048:4096]
            xs = to_state[:, 0:2048]
            t_ = to_state[:, 2048:4096]
            buf = [act_a[:], adacc[:].rearrange("p s n -> p (s n)")]
            by_bank = lambda t, h, a: t.rearrange("p (h q a u j) -> p h a q u j", h=2, q=4, a=2, u=4)[:, h, a]
            quarter = lambda b: bank(b).rearrange("p (u q j) -> p q u j", u=4, q=4)
            T.wait(V.last(), G.last())
            A.wait(V.last())
            V.wait(T.last(), A.last())

            def copy(n, o, i):
                if n % 2:
                    return A.mark(nc.scalar.activation(o, i, ACT.Copy))
                return V.mark(nc.vector.tensor_copy(o, i))
            copier = [V, A]
            here = []
            for h in range(2):
                for q in range(4):
                    for i in range(TAPS):
                        src = xa[:, 4 * h + q, :].rearrange("p (j i) -> p i j", i=TAPS)[:, i, :]
                        m = nc.tensor.matmul(PS[32 * q:32 * q + NJ, h * 1024 + i * P:h * 1024 + (i + 1) * P],
                                             src, ident[:], start=True, stop=True, tile_position=(0, 32 * q))
                here.append(T.mark(m))
            turned = {}
            for h in range(2):
                v = PS[:, h * 1024:(h + 1) * 1024].rearrange("p (i g c) -> p i g c", i=TAPS, g=8)
                for a in range(2):
                    copier[h].wait(here[h], turned.get((h - 1, a)))
                    m = copy(h, buf[a].rearrange("p (g i c) -> p i g c", g=4, i=TAPS), v[:, :, 4 * a:4 * a + 4, :])
                    T.wait(m)
                    b = 4 + 2 * h + a
                    for g in range(4):
                        m = nc.tensor.transpose(PS[:, b * 512 + g * P:b * 512 + (g + 1) * P],
                                                buf[a][:, g * P:(g + 1) * P], ident[:])
                    turned[h, a] = T.mark(m)
            uc_here = []
            for h in range(2):
                for a in range(2):
                    copier[a].wait(turned[h, a])
                    uc_here.append(copy(a, by_bank(uc, h, a), quarter(4 + 2 * h + a)))
            T.wait(*uc_here[:2])
            turned, y_of = {}, {}

            def chunk_products(h, a, left, right, o, start):
                for q in range(4):
                    for u in range(4):
                        g = (4 * h + q) * 8 + 4 * a + u
                        m = nc.tensor.matmul(PS[32 * q:32 * q + NJ, o + u * P:o + (u + 1) * P],
                                             left[:, g * NJ:(g + 1) * NJ], right[:, g * P:(g + 1) * P],
                                             start=start and u == 0, stop=True, skip_group_check=True,
                                             tile_position=(0, 32 * q))
                return T.mark(m)

            def turn_added(n):
                for u in range(4):
                    m = nc.tensor.transpose(PS[:, (4 + n) * 512 + u * P:(4 + n) * 512 + (u + 1) * P],
                                            buf[n % 2][:, u * P:(u + 1) * P], ident[:])
                turned[n] = T.mark(m)

            copied = {}
            for n in range(4):
                h, a = n // 2, n % 2
                if n == 2:
                    T.wait(*uc_here[2:])
                done = chunk_products(h, a, uc, to_state, n * 512, True)
                copier[a].wait(done, turned.get(n - 2))
                copied[n] = copy(a, buf[a], bank(n))
                if n:
                    T.wait(copied[n - 1])
                    turn_added(n - 1)
            T.wait(copied[3])
            turn_added(3)
            V.wait(turned[3])
            A.wait(turned[3])
            xj = xs.rearrange("p (g j) -> p g j", g=GROUPS)
            tj = t_.rearrange("p (g j) -> p g j", g=GROUPS)
            V.mark(nc.vector.memset(xj[:, :, 0:1], 0.0))
            for n in range(4):
                copy(n, by_bank(xs, n // 2, n % 2)[:, :, :, 1:NJ], quarter(4 + n)[:, :, :, 0:NJ - 1])
            steps = [(d, 2 ** d) for d in range(4)] + [(d, 2 ** (d + 1)) for d in (3, 2, 1, 0)]
            T.wait(A.last())
            V.wait(A.last())
            for lev, (d, first) in enumerate(steps):
                n, gap = NJ // 2 ** (d + 1) - 1, 2 ** (d + 1)
                at = lambda t, o: t[:, :, o:o + gap * (n - 1) + 1:gap]
                src, dst, tmp = at(xj, first), at(xj, first + 2 ** d), tj[:, :, 0:n]
                pr_, pi_ = [w[8 + d].unsqueeze(2).to_broadcast([P, GROUPS, n]) for w in (powr, powi)]
                T.wait(V.last())
                blocks = 2 if n > 8 else 1
                gs = GROUPS // blocks
                for b in range(blocks):
                    m = nc.tensor.matmul(PS[:, b * 512:b * 512 + gs * n].rearrange("p (g j) -> p g j", j=n),
                                         jt[:], src[:, b * gs:(b + 1) * gs, :], start=True, stop=True)
                jx_here = T.mark(m)
                V.mark(V.then().tensor_tensor(tmp, src, pr_, ALU.mult))
                V.mark(V.then().tensor_tensor(dst, dst, tmp, ALU.add))
                V.wait(jx_here)
                V.after()
                jx = PS[:, 0:blocks * 512].rearrange("p (b c) -> p b c", b=blocks)[:, :, 0:gs * n]
                four = lambda t: t.rearrange("p (b g) j -> p b g j", b=blocks)
                V.mark(nc.vector.tensor_tensor(four(tmp), jx.rearrange("p b (g j) -> p b g j", j=n), four(pi_),
                                               ALU.mult))
                V.mark(V.then().tensor_tensor(dst, dst, tmp, ALU.add))
                if lev < 4:
                    chunk_products(lev // 2, lev % 2, uc, toep, 2048 + lev * 512, True)
            T.wait(V.last())
            vbuf = [to_state[:, 4096 + h * 1024:5120 + h * 1024] for h in range(2)]
            for n in range(4):
                h, a = n // 2, n % 2
                done = chunk_products(h, a, xs, to_out, 2048 + n * 512, False)
                copier[a].wait(done)
                y_of[n] = copy(a, vbuf[h].rearrange("p (i a u c) -> p a u i c", i=TAPS, a=2, u=4)[:, a],
                               bank(4 + n).rearrange("p (u i c) -> p u i c", u=4, i=TAPS))
            yt = [act_y[:, 0:S], act_y[:, S:2 * S]]
            split, turned = {}, {}
            for h in range(2):
                T.wait(y_of[2 * h], y_of[2 * h + 1])
                for i in range(TAPS):
                    m = nc.tensor.transpose(PS[:, h * 1024 + i * P:h * 1024 + (i + 1) * P],
                                            vbuf[h][:, i * P:(i + 1) * P], ident[:])
                turned[h] = T.mark(m)
            added, gelu = {}, {}
            for kt in range(KT + 1):
                if kt < KT:
                    h, q = kt // 4, kt % 4
                    V.wait(turned[h], split.get(kt - 2))
                    yk = yt[kt % 2]
                    V.after()
                    added[kt] = V.mark(nc.vector.scalar_tensor_tensor(
                        yk.rearrange("p (j i) -> p j i", i=TAPS),
                        xa[:, kt, :].rearrange("p (j i) -> p j i", i=TAPS), par["ssm_d"][:, kt:kt + 1],
                        PS[:, h * 1024:(h + 1) * 1024].rearrange("p (i q j) -> p q j i", i=TAPS, q=4)[:, q],
                        ALU.mult, ALU.add))
                    A.wait(added[kt])
                    gelu[kt] = A.mark(nc.scalar.activation(yk, yk, ACT.Gelu_apprx_tanh))
                if kt:
                    split[kt - 1] = split_act(yt[(kt - 1) % 2], kt - 1, gelu[kt - 1])
            T.wait(V.last())

        def forget_gates(fw):
            z, a, cum = fw[0:16, 0:S], fw[0:16, S:2 * S], fw[0:16, 2 * S:3 * S]
            A.wait(A.last(), V.last())
            T.wait(V.last())
            wf = fw[:, 3 * S:3 * S + KT * 16].rearrange("p (k h) -> p k h", k=KT)
            nc.scalar.dma_start(wf, p["w_f"]).then_inc(s_par, 16)
            nc.tensor.wait_ge(s_par, 32)
            f = PS[0:16, 3584:3584 + S]
            for k in range(KT):
                m = nc.tensor.matmul(f, wf[:, k, :], xa[:, k, :], start=k == 0, stop=k == KT - 1)
            A.wait(T.mark(m))
            A.mark(nc.scalar.activation(z, f, ACT.Identity, bias=par["b_f"][0:16, :]))
            A.mark(A.then().activation(a, z, ACT.Abs))
            A.mark(A.then().activation(a, a, ACT.Exp, scale=-1.0))
            V.wait(A.mark(A.then().activation(a, a, ACT.Ln, bias=one[0:16, :])))
            V.mark(nc.vector.scalar_tensor_tensor(z, z, 0.0, a, ALU.min, ALU.subtract))
            V.mark(V.then().memset(a, 1.0))
            V.mark(V.then().tensor_tensor_scan(cum, a, z, 0.0, ALU.mult, ALU.add))
            V.mark(nc.vector.memset(f_parts[:].bitcast(F32), 0.0))
            for r in (0, 64):
                V.mark(V.then().tensor_copy(f_parts[r:r + 16, :], cum))
            V.mark(V.then().tensor_tensor(a, cum, f_parts[0:16, :].bitcast(F32), ALU.subtract))
            A.wait(V.last())
            for r in (32, 96):
                A.mark(nc.scalar.activation(f_parts[r:r + 16, :], a, ACT.Copy))
            V.mark(V.then().memset(f_sel[:].bitcast(F32), 0.0))
            for r in (0, 32, 64, 96):
                V.mark(V.then().tensor_copy(f_sel[r:r + 16, 0:16], ident[0:16, 0:16]))
                V.mark(nc.vector.tensor_scalar(f_sel[r:r + 16, 16:32], ident[0:16, 0:16], -1.0, None, ALU.mult))

        def fox(qk, vt, work):
            W = P + S
            we = [work[:, n * W:(n + 1) * W] for n in range(3)]
            wt = [work[:, n * W:(n + 1) * W] for n in (3, 4)]
            o = 5 * W
            later, st = work[:, o:o + P], work[:, o + P:o + P + 32]
            A.wait(V.last())
            V.wait(A.last())
            T.wait(A.last())
            V.mark(nc.vector.memset(later, -1e30))
            G.wait(V.last())
            T.wait(G.mark(G.then().affine_select(out=later, in_=later, compare_op=ALU.is_ge, fill=0.0, base=-1,
                                                 pattern=[[1, P]], channel_multiplier=-1)))
            T.wait(V.last())
            z_read, scaled, w_read, wt_done, pv, o_read = {}, {}, {}, {}, {}, {}

            def exps(h):
                n, po, pr = h % 2, HD * (h % 2), h // 2
                T.wait(z_read.get(h - 2))
                z = bank(n)
                for c, w, b in ((0, P, 0), (P, S, 1)):
                    zb = z[:, c:c + w]
                    nc.tensor.matmul(zb, qk[po:po + HD, pr, b * P:(b + 1) * P], qk[po:po + HD, 8 + pr, 0:w],
                                     start=True, stop=False, skip_group_check=True)
                    nc.tensor.matmul(zb, f_parts[po:po + 48, b * P:(b + 1) * P],
                                     f_sel[po:po + 48, h:h + 1].to_broadcast([48, w]),
                                     start=False, stop=False, skip_group_check=True)
                    nc.tensor.matmul(zb, f_sel[po:po + 48, 16 + h:17 + h].to_broadcast([48, P]),
                                     f_parts[po:po + 48, 0:w],
                                     start=False, stop=False, skip_group_check=True)
                    m = nc.tensor.matmul(z[:, c + w - P:c + w], ident[:], later, start=False, stop=True,
                                         skip_group_check=True)
                V.wait(T.mark(m), z_read.get(h - 2))
                sv = st[:, 8 * (h % 3):8 * (h % 3) + 8]
                V.wait(scaled.get(h - 3))
                V.mark(nc.vector.tensor_reduce(sv[:, 0:1], z[:, 0:P], AX.X, ALU.max, negate=True))
                V.mark(nc.vector.tensor_reduce(sv[:, 1:2], z[:, P:W], AX.X, ALU.max, negate=True))
                A.wait(V.last(), w_read.get(h - 3))
                A.mark(nc.scalar.activation(we[h % 3][:, 0:P], z[:, 0:P], ACT.Exp, bias=sv[:, 0:1],
                                            accum_out=sv[:, 2:3]))
                z_read[h] = A.mark(nc.scalar.activation(we[h % 3][:, P:W], z[:, P:W], ACT.Exp,
                                                        bias=sv[:, 1:2], accum_out=sv[:, 3:4]))

            def scale(h):
                w, sv = we[h % 3], st[:, 8 * (h % 3):8 * (h % 3) + 8]
                V.wait(z_read[h])
                V.mark(nc.vector.reciprocal(sv[:, 2:4], sv[:, 2:4]))
                V.mark(V.then().tensor_scalar(w[:, 0:P], w[:, 0:P], sv[:, 2:3], None, ALU.mult))
                scaled[h] = V.mark(nc.vector.tensor_scalar(w[:, P:W], w[:, P:W], sv[:, 3:4], None, ALU.mult))

            def turned(h):
                n = h % 2
                T.wait(scaled[h], wt_done.get(h - 2))
                wb = bank(2 + n)
                for c in (0, P, S):
                    m = nc.tensor.transpose(wb[:, c:c + P], we[h % 3][:, c:c + P], ident[:])
                w_read[h] = T.mark(m)
                A.wait(w_read[h], pv.get(h - 2))
                wt_done[h] = A.mark(nc.scalar.activation(wt[n], wb[:, 0:W], ACT.Copy))

            def values(h):
                n, pr = h % 2, h // 2
                if n == 0:
                    T.wait(o_read.get(pr - 2))
                pv[h] = attend_out(h, wt[n][:, 0:S], wt[n][:, S:W], vt, wt_done[h])
                if n:
                    o_read[pr] = split_pair(pr, pv[h])

            for step in range(HEADS + 3):
                if step < HEADS:
                    exps(step)
                if 1 <= step <= HEADS:
                    scale(step - 1)
                if 2 <= step <= HEADS + 1:
                    turned(step - 2)
                if step >= 3:
                    values(step - 3)
            T.wait(o_read[HEADS // 2 - 1])

        def load_weights():
            sy = nc.sync
            q = a = 0
            for number, (turns, chunks, slots) in enumerate(segments):
                first = number == 0
                if number == 1:
                    sy.wait_ge(start_sum, START_UNITS + 4)
                def turn(i):
                    step_q, step_a = chunks, len(slots)
                    units = list(enumerate(slots))
                    per = max(1, -(-len(units) // max(chunks, 1)))
                    for c in range(max(chunks, 1)):
                        if chunks:
                            qq = q + c if i is None else i * step_q + (q + c)
                            s = (q + c) % 2
                            if not (i is None and q + c < 2):
                                sy.wait_ge(w_lo_done, qq * 2 - 2)
                            src = p["w"][bass.ds(qq, 1), :, :] if i is not None else p["w"][qq:qq + 1, :, :]
                            sy.dma_start(stage[s][:], src.rearrange("a p n -> (a p) n")).then_inc(w_here[s], 16)
                        for u, s in units[c * per:(c + 1) * per]:
                            aa = a + u if i is None else i * step_a + (a + u)
                            sy.wait_ge(start_sum if first else ada_sum, aa + 1)
                            src = p["ada"][bass.ds(aa, 1), :, :] if i is not None else p["ada"][aa:aa + 1, :, :]
                            sy.dma_start(ada[:, s, :], src.rearrange("a p n -> (a p) n")).then_inc(ada_here[s], 16)
                if turns > 1 and q < 2 and chunks:
                    turn(None)
                    q += chunks
                    a += len(slots)
                    turns -= 1
                if turns == 1:
                    turn(None)
                elif turns:
                    with nc.sync.Fori(0, turns) as i:
                        turn(i)
                q += chunks * turns
                a += len(slots) * turns

        def finish(g):
            norm(g, None, split=False)
            A.wait(V.last())
            nc.scalar.dma_start(out, xa[:]).then_inc(s_out, 16)
            nc.scalar.wait_ge(s_out, 16)
            load_weights()

        slots4 = (0, 1, 2, 3)
        segments.append((4, 0, slots4))
        with Loop(4, gpsimd=True, V=1) as i:
            ada_units(slots4[:3], i, sums=False)
            ada_sums(slots4, i)
            ada_cols(slots4, i, start_sum)
        ada_advance(slots4, 4)
        masks = [arena[:, ARENA - 1024 + n * P:ARENA - 1024 + (n + 1) * P] for n in range(8)]
        G.mark(G.then().memset(arena[:, ARENA - 1024:ARENA], 0.0))
        for lev in range(7):
            c = 2 ** lev
            view = masks[lev].rearrange("p (n a c) -> p n a c", a=2, c=c)
            G.mark(G.then().memset(view[:, :, 1, :], 1.0))
        for lev in range(7):
            c = 2 ** lev
            n = P // (2 * c)
            view = masks[lev].rearrange("p (n r) -> p n r", n=n)
            G.mark(G.then().affine_select(out=view, in_=view, compare_op=ALU.is_ge, fill=0.0, base=0,
                                          pattern=[[-2 * c, n], [0, 2 * c]], channel_multiplier=1))
            G.mark(G.then().affine_select(out=view, in_=view, compare_op=ALU.is_ge, fill=0.0, base=c - 1,
                                          pattern=[[2 * c, n], [0, 2 * c]], channel_multiplier=-1))
        G.mark(G.then().tensor_copy(masks[7], ident[:]))
        masks_ready = G.last()
        nc.vector.wait_ge(s_par2, 16)
        nc.scalar.wait_ge(s_par2, 16)
        nc.scalar.wait_ge(s_x, 16)
        nc.vector.wait_ge(s_x, 16)
        mod_add(0, 16)
        A.wait(consts)
        T.wait(consts)
        V.wait(consts)
        gain_mod(par["norm_mix"][:, 0:KT], mod[:, 8:16])
        prep(0, 0)
        norm(gain, mod[:, 0:8])

        u, vt = carve(24 * S, NB * 512)
        u = u.rearrange("p (m t) -> p m t", m=24)
        vt = vt.rearrange("p (b n) -> p b n", b=NB)
        gemm(12, copy_evac(u), units=slots4, per={"A": 2})
        gemm(2, copy_evac_tm(vt), token_major=True, per={"A": 2})

        def side_units(turns, col_bank=6):
            segments.append((1, 2, ()))
            state["ahead"] = 2
            segments.append((turns, 0, slots4))

            def columns():
                ada_cols(slots4, col_bank=col_bank)
                ada_advance(slots4)

            def units():
                a0, counts = state["a"], list(ada_slot)
                for _ in range(turns):
                    ada_units(slots4)
                    ada_advance(slots4)
                state["a"], ada_slot[:] = a0, counts
            return units, columns
        units, columns = side_units(3)
        units()
        hgrn(u, vt, {2: columns, 4: columns, 6: columns})
        mod_add(16, 40)
        V.after()
        gemm(4, residual_evac(mod[:, 16:24]), per={"V": 4})
        gain_mod(par["norm_mlp"][:, 0:KT], mod[:, 32:40])
        norm(gain, mod[:, 24:32])

        def gate_mlp0():
            mod_add(40, 72)
            return mod[:, 40:48]
        mlp(gate_mlp0, slots4)

        gain_mod(par["norm_mix"][:, KT:2 * KT], mod[:, UNITS + 8:UNITS + 16])
        norm(gain, mod[:, UNITS:UNITS + 8])
        u, vt, work = carve(16 * S, NB * D, ARENA - 16 * S - NB * D)
        qk = u.rearrange("p (m t) -> p m t", m=16)
        vt = vt.rearrange("p (b n) -> p b n", b=NB)
        gemm(8, copy_evac(qk), units=slots4, per={"A": 2})
        gemm(4, copy_evac_tm(vt), token_major=True, units=slots4, per={"A": 2})
        mod_add(72, 84)
        units, columns = side_units(3, col_bank=5)

        def last_columns():
            columns()
            mod_add(84, 96, col_bank=5)
            ssm_load()
        stick_breaking(qk, vt, work, {-1: units, 0: columns, 4: columns, 12: last_columns, 13: ssm_steps, 15: ssm_angles,
                                      17: ssm_rotations})
        ssm_inputs_to_states()
        gemm(4, residual_evac(mod[:, UNITS + 16:UNITS + 24]), per={"V": 4})
        gain_mod(par["norm_mlp"][:, KT:2 * KT], mod[:, UNITS + 32:UNITS + 40])
        norm(gain, mod[:, UNITS + 24:UNITS + 32])
        ssm_states_to_outputs()
        mlp(lambda: mod[:, UNITS + 40:UNITS + 48], between=ssm_taps, turns_before=4)
        ssm_toeplitz()

        A.wait(G.last())
        V.wait(G.last())
        norm(par["mix_norm_2"][:, 0:KT], None, split=False,
             squares=act_squares)
        ssm()
        gemm(8, glu_evac([act_y[:, 0:S], act_y[:, S:2 * S]]), per={"V": 4, "A": 2})
        norm(par["mlp_norm_2"][:, 0:KT], None)
        mlp(lambda: None)

        norm(par["kv_norm_2"], None)
        u, vt, fox_f, work = carve(16 * S, NB * D, 1024, ARENA - 16 * S - NB * D - 1024)
        qk = u.rearrange("p (m t) -> p m t", m=16)
        vt = vt.rearrange("p (b n) -> p b n", b=NB)
        forget_gates(fox_f)
        gemm(4, copy_evac(qk[:, 8:16, :]), per={"A": 2})
        gemm(4, copy_evac_tm(vt), token_major=True, per={"A": 2})
        norm(par["mix_norm_2"][:, KT:2 * KT], None, same_x=True)
        gemm(4, copy_evac(qk[:, 0:8, :], HD ** -0.5), per={"A": 2})
        fox(qk, vt, work)
        gemm(4, residual_evac(None), per={"V": 4})
        norm(par["mlp_norm_2"][:, KT:2 * KT], None)
        mlp(lambda: None)
        finish(par["final_norm_2"])


def tiles(w):
    k, n = w.shape
    return w.reshape(k // P, P, n // CW, CW).transpose(2, 1, 0, 3).reshape(n // CW, P, -1)


def row_tiles(w):
    return w.reshape(-1, 2, P, D).transpose(0, 2, 1, 3).reshape(-1, P, 2 * D)


def mlp_tiles(w1, w2):
    a, b = tiles(w1), row_tiles(w2)
    mixed = np.stack([a[1:], b[:-1]], axis=1).reshape(-1, P, 2 * D)
    return [a[:1], mixed, b[-1:]]


def cols(v):
    v = np.asarray(v)
    return v.reshape(-1, P).T


def layout(i):
    g = {k: np.asarray(v) for k, v in i.items()}
    w_in = g["w_in_ab"][0]
    c5 = D // 2
    order = [w_in[:, n * c5:(n + 1) * c5] for n in (0, 1, 2, 3, 4, 6, 5)]
    qkv = g["w_qkv"][0]
    glu = g["ssm_w_glu_2"][0].reshape(D, 2, KT, P).transpose(0, 2, 1, 3).reshape(D, 2 * D)
    kvf = g["w_kvf_2"]
    parts = [tiles(np.concatenate(order, axis=1)), tiles(g["w_out_ab"][0])]
    parts += mlp_tiles(g["mlp_w1"][0], g["mlp_w2"][0])
    parts += [tiles(qkv), tiles(g["w_out_c"][0])]
    parts += mlp_tiles(g["mlp_w1"][1], g["mlp_w2"][1])
    parts += [tiles(glu)]
    parts += mlp_tiles(g["mlp_w1_2"][0], g["mlp_w2_2"][0])
    parts += [tiles(kvf[:, 0:2 * D]), tiles(g["attn_wq_2"][0]), tiles(g["attn_wo_2"][0])]
    parts += mlp_tiles(g["mlp_w1_2"][1], g["mlp_w2_2"][1])
    w = np.concatenate(parts)
    ada = g["ada_w"].reshape(2, KT, P, UNITS, P).transpose(0, 3, 2, 1, 4).reshape(2 * UNITS, P, D)
    x = g["x"][0].T.reshape(KT, P, S).transpose(1, 0, 2)
    both = lambda v: np.tile(v, 2)[:, None]
    pv = {"c": cols(g["c"]), "ada_b": cols(g["ada_b"]), "norm_mix": cols(g["norm_mix"]),
          "norm_mlp": cols(g["norm_mlp"]), "lb": cols(g["lb_logits"]), "hg_norm": cols(g["hg_norm"]),
          "conv_w": cols(g["conv_w"]), "q_norm": both(g["q_norm"][0]), "k_norm": both(g["k_norm"][0]),
          "mix_norm_2": cols(g["mix_norm_2"]), "mlp_norm_2": cols(g["mlp_norm_2"]),
          "kv_norm_2": cols(g["kv_norm_2"]), "final_norm_2": cols(g["final_norm_2"]),
          "ssm_d": cols(g["ssm_d_2"]), "b_f": np.tile(g["b_f_2"], P // HEADS)[:, None]}
    params = np.concatenate([pv[n] for n, _ in PARAM_COLS], axis=1)
    twice = lambda v: np.concatenate([v.T, v.T])
    ldt = np.broadcast_to(g["ssm_log_dt_2"][0], (P, GROUPS))
    b = [g["ssm_b_%s_2" % r][0].transpose(1, 0, 2).reshape(NSTATE, -1) for r in ("re", "im")]
    c = [g["ssm_c_%s_2" % r][0].transpose(2, 0, 1).reshape(NSTATE, -1) for r in ("re", "im")]
    ssm_in = np.concatenate([ldt, twice(g["ssm_a_re_2"][0]), twice(g["ssm_a_im_2"][0]),
                             np.concatenate(b), np.concatenate(b[::-1]),
                             np.concatenate(c), np.concatenate(c[::-1])], axis=1)
    w_f = kvf[:, 2 * D:].reshape(KT, P, HEADS).transpose(1, 0, 2)
    arrays = {"w": w, "ada": ada, "x": x, "params": params, "ssm_in": ssm_in, "w_f": w_f}
    return {"in_" + k: np.ascontiguousarray(v) for k, v in arrays.items()}


def kernel(**inputs):
    import concourse.bacc as bacc
    from concourse.bass_utils import run_bass_kernel_spmd

    nc = bacc.Bacc("TRN2", target_bir_lowering=False, num_devices=1)
    arrays = layout(inputs)
    p = {k[3:]: nc.dram_tensor(k, v.shape, F32, kind="ExternalInput").ap() for k, v in arrays.items()}
    out = nc.dram_tensor("out_0", (P, KT, S), F32, kind="ExternalOutput").ap()
    build(nc, p, out)
    r = run_bass_kernel_spmd(nc, [arrays], core_ids=[0])
    y = r.results[0]["out_0"]
    return np.ascontiguousarray(y.transpose(2, 1, 0).reshape(1, S, D))
```
